# Optimizing a Trainium2 kernel written in Bass

```python
import jax, jax.numpy as jnp
from jax import lax
import numpy as np

D_MODEL = 1024
BATCH = 1
SEQ = 512
DEPTH = 2

GRID_W = 64
CTX_LEN = 256
N_MIXERS = 2
N_A = (DEPTH + N_MIXERS - 1) // N_MIXERS
N_B = DEPTH // N_MIXERS
D_INNER = 2 * D_MODEL
M_HEADS = 4
M_HEAD_DIM = D_INNER // M_HEADS
CHUNK = 64
CONV_K = 3
F_GROUPS = 4
D_FF = 4 * D_MODEL
ALPHA = float((2 * DEPTH) ** 0.25)
BETA = float((8 * DEPTH) ** -0.25)
LN_EPS = 1e-5

kernel_name = "hybrid_mlstm_fourier_prefix_dit"

def layer_norm(x):
    xf = x.astype(jnp.float32)
    mu = xf.mean(-1, keepdims=True)
    var = jnp.square(xf - mu).mean(-1, keepdims=True)
    return ((xf - mu) * lax.rsqrt(var + LN_EPS)).astype(x.dtype)

def modulate(x, shift, scale):
    return layer_norm(x) * (1 + scale) + shift

def post_norm(x, g, b):
    return layer_norm(x) * g + b

def conv_grid(x, w):
    B, T, C = x.shape
    rows = T // GRID_W
    y = lax.conv_general_dilated(
        x.reshape(B, rows, GRID_W, C), w[:, :, None, :], window_strides=(1, 1), padding="SAME",
        dimension_numbers=("NHWC", "HWIO", "NHWC"), feature_group_count=C)
    return y.reshape(B, T, C)

def conv_seq(x, w):
    C = x.shape[-1]
    return lax.conv_general_dilated(
        x, w[CONV_K // 2][:, None, :], window_strides=(1,), padding="SAME",
        dimension_numbers=("NWC", "WIO", "NWC"), feature_group_count=C)

def mlstm_chunkwise(q, k, v, log_i, log_f, state):
    B, H, T, dh = q.shape
    nc = T // CHUNK

    def to_chunks(a):
        return jnp.moveaxis(a.reshape(a.shape[:2] + (nc, CHUNK) + a.shape[3:]), 2, 0)

    tril = jnp.tril(jnp.ones((CHUNK, CHUNK), dtype=bool))

    def step(carry, inp):
        C, n, m = carry
        qc, kc, vc, li, lf = inp
        b = jnp.cumsum(lf, axis=-1)
        a_inter = b + m[..., None]
        log_w = jnp.where(tril, b[..., :, None] - b[..., None, :] + li[..., None, :], -jnp.inf)
        m_row = jnp.maximum(a_inter, log_w.max(-1))
        w_inter = jnp.exp(a_inter - m_row)
        s = jnp.einsum("bhld,bhsd->bhls", qc, kc).astype(jnp.float32) * jnp.exp(log_w - m_row[..., None])
        num = (w_inter[..., None] * jnp.einsum("bhed,bhld->bhle", C, qc)
               + jnp.einsum("bhls,bhse->bhle", s, vc))
        den = w_inter * jnp.einsum("bhd,bhld->bhl", n, qc) + s.sum(-1)
        h = num / jnp.maximum(jnp.abs(den), jnp.exp(-m_row))[..., None]
        m_new = m_row[..., -1]
        w_k = jnp.exp(b[..., -1:] - b + li - m_new[..., None])
        decay = jnp.exp(b[..., -1] + m - m_new)
        C = decay[..., None, None] * C + jnp.einsum("bhs,bhse,bhsd->bhed", w_k, vc, kc)
        n = decay[..., None] * n + jnp.einsum("bhs,bhsd->bhd", w_k, kc)
        return (C, n, m_new), h

    state, h = lax.scan(step, state, (to_chunks(q), to_chunks(k), to_chunks(v),
                                      to_chunks(log_i), to_chunks(log_f)))
    return jnp.moveaxis(h, 0, 2).reshape(B, H, T, dh), state

def mlstm_mixer(h_x, h_c, need_ctx, w_in, w_conv, b_conv, w_q, w_k, w_v, w_gate, b_gate, gn_w, skip, w_out):
    wg = w_gate.reshape(3, M_HEADS, M_HEAD_DIM, 4 * M_HEADS)

    def branch(h, conv_fn):
        B, T, _ = h.shape
        x_m, z = jnp.split(h @ w_in, 2, axis=-1)
        x_c = jax.nn.silu(conv_fn(x_m, w_conv) + b_conv)
        xh_c = x_c.reshape(B, T, M_HEADS, M_HEAD_DIM)
        q = jnp.einsum("bthd,hde->bhte", xh_c, w_q)
        k = jnp.einsum("bthd,hde->bhte", xh_c, w_k) * (M_HEAD_DIM ** -0.5)
        v = jnp.einsum("bthd,hde->bhte", x_m.reshape(B, T, M_HEADS, M_HEAD_DIM), w_v)
        pre = (jnp.einsum("bhte,hen->btn", q, wg[0]) + jnp.einsum("bhte,hen->btn", k, wg[1])
               + jnp.einsum("bhte,hen->btn", v, wg[2]) + b_gate).astype(jnp.float32)
        pre = jnp.transpose(pre.reshape(B, T, 2, 2, M_HEADS), (2, 3, 0, 4, 1))
        return x_c, z, q, k, v, pre[:, 0], jax.nn.log_sigmoid(pre[:, 1])

    def readout(h, x_c, z):
        mu = h.mean(-1, keepdims=True)
        var = jnp.square(h - mu).mean(-1, keepdims=True)
        hn = (h - mu) * lax.rsqrt(var + LN_EPS)
        B, H, T, dh = h.shape
        hn = jnp.transpose(hn, (0, 2, 1, 3)).reshape(B, T, H * dh).astype(x_c.dtype) * gn_w
        return ((hn + skip * x_c) * jax.nn.silu(z)) @ w_out

    cb = branch(h_c, conv_seq)
    xb = branch(h_x, conv_grid)
    B = h_c.shape[0]
    outs_c, outs_x = [], []
    for d in range(2):
        if d == 0:
            flip = lambda a: a
        else:
            flip = lambda a: jnp.flip(a, axis=2)
        state0 = (jnp.zeros((B, M_HEADS, M_HEAD_DIM, M_HEAD_DIM), jnp.float32),
                  jnp.zeros((B, M_HEADS, M_HEAD_DIM), jnp.float32),
                  jnp.zeros((B, M_HEADS), jnp.float32))
        hc, st = mlstm_chunkwise(flip(cb[2]), flip(cb[3]), flip(cb[4]), flip(cb[5][d]), flip(cb[6][d]), state0)
        hx, _ = mlstm_chunkwise(flip(xb[2]), flip(xb[3]), flip(xb[4]), flip(xb[5][d]), flip(xb[6][d]), st)
        outs_c.append(flip(hc))
        outs_x.append(flip(hx))
    y_x = readout(outs_x[0] + outs_x[1], xb[0], xb[1])
    y_c = readout(outs_c[0] + outs_c[1], cb[0], cb[1]) if need_ctx else None
    return y_x, y_c

def fourier_mixer(h, w_out):
    B, T, D = h.shape
    hg = h.astype(jnp.float32).reshape(B, T, F_GROUPS, D // F_GROUPS)
    mixed = jnp.fft.fft2(hg, axes=(1, 3), norm="ortho").real
    return mixed.reshape(B, T, D).astype(h.dtype) @ w_out

def sq_relu_mlp(h, w1, w2):
    return jnp.square(jax.nn.relu(h @ w1)) @ w2

def setup_inputs(seed: int = 0) -> dict:
    key = jax.random.key(seed)
    ks = jax.random.split(key, 24)
    nrm = lambda k, shape, s: jax.random.normal(k, shape, jnp.float32) * s
    b_gate = nrm(ks[14], (N_A, 2, 2, M_HEADS), 0.1)
    b_gate = b_gate.at[:, :, 1, :].add(jnp.linspace(3.0, 6.0, M_HEADS, dtype=jnp.float32))
    return {
        "x": nrm(ks[0], (BATCH, SEQ, D_MODEL), 1.0),
        "c": nrm(ks[1], (BATCH, D_MODEL), 1.0),
        "ctx": nrm(ks[2], (BATCH, CTX_LEN, D_MODEL), 1.0),
        "c_ctx": nrm(ks[3], (D_MODEL,), 1.0),
        "ada_w": nrm(ks[4], (DEPTH, D_MODEL, 6 * D_MODEL), D_MODEL ** -0.5),
        "ada_b": nrm(ks[5], (DEPTH, 6 * D_MODEL), 0.02),
        "post_g": 1.0 + nrm(ks[6], (DEPTH, 2, D_MODEL), 0.02),
        "post_b": nrm(ks[7], (DEPTH, 2, D_MODEL), 0.02),
        "m_w_in": nrm(ks[8], (N_A, D_MODEL, 2 * D_INNER), D_MODEL ** -0.5),
        "m_w_conv": nrm(ks[9], (N_A, CONV_K, CONV_K, D_INNER), 1.0 / CONV_K),
        "m_b_conv": nrm(ks[10], (N_A, D_INNER), 0.02),
        "m_w_q": nrm(ks[11], (N_A, M_HEADS, M_HEAD_DIM, M_HEAD_DIM), M_HEAD_DIM ** -0.5),
        "m_w_k": nrm(ks[12], (N_A, M_HEADS, M_HEAD_DIM, M_HEAD_DIM), M_HEAD_DIM ** -0.5),
        "m_w_v": nrm(ks[13], (N_A, M_HEADS, M_HEAD_DIM, M_HEAD_DIM), M_HEAD_DIM ** -0.5),
        "m_w_gate": nrm(ks[15], (N_A, 3, D_INNER, 4 * M_HEADS), (3 * D_INNER) ** -0.5),
        "m_b_gate": b_gate.reshape(N_A, 4 * M_HEADS),
        "m_gn_w": 1.0 + nrm(ks[16], (N_A, D_INNER), 0.02),
        "m_skip": 1.0 + nrm(ks[17], (N_A, D_INNER), 0.02),
        "m_w_out": nrm(ks[18], (N_A, D_INNER, D_MODEL), BETA * D_INNER ** -0.5),
        "f_w_out": nrm(ks[19], (N_B, D_MODEL, D_MODEL), BETA * D_MODEL ** -0.5),
        "mlp_w1": nrm(ks[20], (DEPTH, D_MODEL, D_FF), D_MODEL ** -0.5),
        "mlp_w2": nrm(ks[21], (DEPTH, D_FF, D_MODEL), BETA * D_FF ** -0.5),
    }

def reference(x, c, ctx, c_ctx, ada_w, ada_b, post_g, post_b, m_w_in, m_w_conv, m_b_conv, m_w_q, m_w_k,
              m_w_v, m_w_gate, m_b_gate, m_gn_w, m_skip, m_w_out, f_w_out, mlp_w1, mlp_w2):
    s_lat = jax.nn.silu(c)
    s_ctx = jax.nn.silu(c_ctx)
    for i in range(DEPTH):
        is_mlstm = i % N_MIXERS == 0
        j = i // N_MIXERS
        need_ctx = i < DEPTH - 1
        use_ctx = need_ctx or is_mlstm
        sh1, sc1, g1, sh2, sc2, g2 = jnp.split((s_lat @ ada_w[i] + ada_b[i])[:, None, :], 6, axis=-1)
        h_x = modulate(x, sh1, sc1)
        h_c = None
        if use_ctx:
            csh1, csc1, cg1, csh2, csc2, cg2 = jnp.split(s_ctx @ ada_w[i] + ada_b[i], 6, axis=-1)
            h_c = modulate(ctx, csh1, csc1)
        if is_mlstm:
            y_x, y_c = mlstm_mixer(h_x, h_c, need_ctx, m_w_in[j], m_w_conv[j], m_b_conv[j], m_w_q[j], m_w_k[j],
                                   m_w_v[j], m_w_gate[j], m_b_gate[j], m_gn_w[j], m_skip[j], m_w_out[j])
        else:
            y_x = fourier_mixer(h_x, f_w_out[j])
            y_c = fourier_mixer(h_c, f_w_out[j]) if need_ctx else None
        x = post_norm(ALPHA * x + g1 * y_x, post_g[i, 0], post_b[i, 0])
        x = post_norm(ALPHA * x + g2 * sq_relu_mlp(modulate(x, sh2, sc2), mlp_w1[i], mlp_w2[i]),
                      post_g[i, 1], post_b[i, 1])
        if need_ctx:
            ctx = post_norm(ALPHA * ctx + cg1 * y_c, post_g[i, 0], post_b[i, 0])
            ctx = post_norm(ALPHA * ctx + cg2 * sq_relu_mlp(modulate(ctx, csh2, csc2), mlp_w1[i], mlp_w2[i]),
                            post_g[i, 1], post_b[i, 1])
    return x


_drawn_inputs = setup_inputs


def setup_inputs(seed=0):
    import zlib

    import numpy as np

    out = dict(_drawn_inputs(seed))
    spreads = {}
    factors = {'m_b_conv': 5.435, 'm_gn_w': 8.0, 'm_skip': 8.0}
    for name, (base, spread) in spreads.items():
        noise = np.random.default_rng([zlib.crc32(name.encode()), seed]).standard_normal(out[name].shape)
        drawn = base * np.exp(spread * noise) if base else spread * noise
        out[name] = __import__('jax').numpy.asarray(drawn.astype(out[name].dtype))
    for name, factor in factors.items():
        out[name] = (out[name] * factor).astype(out[name].dtype)
    return out
```

```python
from contextlib import ExitStack

import numpy as np

import concourse.bass as bass
from concourse import mybir

F32 = mybir.dt.float32
F32R = mybir.dt.float32r
ALU = mybir.AluOpType
ACT = mybir.ActivationFunctionType

P = 128
D = 1024
NL, NC = 512, 256
NT = NL + NC
KD = D // P
DI = 2048
H, DH = 4, 512
JH = DH // P
ST = NT // P
TT = NL // P
DFF = 4096
GRID = 64
ROWS = NL // GRID
NG = 16
GROUPS = 4
FT = DFF // P // GROUPS
FG = 256
ALPHA = float(4 ** 0.25)
EPS = 1e-5
K_SCALE = float(DH ** -0.5)
UNIT = 2048
KB = 1024

ADA0 = [3, 4, 2, 5]
ADA1_LOOP = [0, 1, 2, 3]
ADA1_TAIL = [4, 5]
SH2_0, SC2_0, SH1_1, SC1_1, SH2_1, SC2_1 = range(6)
MODS = [(SH2_0, SC2_0), (SH1_1, SC1_1), (SH2_1, SC2_1)]

HEAD = ([("xm", j) for j in range(4)] + [("vT", 0), ("vT", 1), ("vN", 0), ("vT", 2), ("vN", 1),
        ("vT", 3), ("vN", 2), ("z", 0), ("vN", 3), ("z", 1), ("z", 2), ("z", 3)]
        + [("q", j) for j in range(4)] + [("k", j) for j in range(4)] + [("S", j) for j in range(6)])
SLOTS = 3
USES = len(HEAD) // SLOTS
USE = {what: n for n, what in enumerate(HEAD)}
READERS = {"xm": (), "vT": ("turn",), "vN": ("dve",), "z": ("dma",), "S": ("dma",),
           "q": ("pe", "dve"), "k": ("pe", "dve")}


def reads_before(reader, n):
    return sum(reader in READERS[HEAD[m][0]] for m in range(n % SLOTS, n + 1, SLOTS))


def reads_per_head(reader, slot):
    return reads_before(reader, len(HEAD) - SLOTS + slot)


RAW_P1, RAW_P2 = 7 * H, 6 * H
RAW0_P2 = RAW_P1
RAW0_MLP0 = RAW0_P2 + RAW_P2
RAW0_F = RAW0_MLP0 + 12 * GROUPS
RAW0_MLP1 = RAW0_F + 3 + 8 + 4
SPLIT0_P2 = 7 * H
SPLIT0_MLP0 = SPLIT0_P2 + 2 * H
SPLIT0_F = SPLIT0_MLP0 + 8 * GROUPS
SPLIT0_MLP1 = SPLIT0_F + 7
CHUNK0_MLP0 = 2 * H
CHUNK0_F = CHUNK0_MLP0 + 2 * GROUPS


def hybrid_block(nc, x, c, ctx, c_ctx, ada_w, ada_b, post_g, post_b, m_w_in, m_w_conv, m_b_conv, m_w_q,
                 m_w_k, m_w_v, m_w_gate, m_b_gate, m_gn_w, m_skip, m_w_out, f_w_out, mlp_w1, mlp_w2,
                 dft, out):
    es = ExitStack()
    with es:
        base = 16512
        region = base + 54 * KB

        def at(name, shape, off_kb, dt=F32):
            return nc.alloc_sbuf_tensor_at(name, shape, dt, offset=int(region + off_kb * KB))

        def fixed(name, shape, off, dt=F32):
            return nc.alloc_sbuf_tensor_at(name, shape, dt, offset=base + off)

        def sem(name):
            return es.enter_context(nc.semaphore(name))

        def sems(name, n):
            return [sem(f"{name}{i}") for i in range(n)]

        raw = fixed("raw", [P, 2, UNIT], 0)
        w_hi = fixed("w_hi", [P, 2, UNIT], 16 * KB, F32R)
        w_lo = fixed("w_lo", [P, 2, UNIT], 32 * KB, F32R)
        o = [48 * KB]

        def const(name, shape):
            n = 4 * int(np.prod(shape[1:]))
            o[0] += (n + 31) // 32 * 32
            assert o[0] <= 54 * KB
            return fixed(name, shape, o[0] - (n + 31) // 32 * 32)

        ident = const("ident", [P, P])
        ones = const("ones", [P, P])
        sel = const("sel", [P, H, P])
        mask = const("mask", [P, 2, P])
        cols = const("cols", [P, 208])
        cvec = const("cvec", [P, 2, KD])
        svec = const("svec", [P, 2, KD])
        mod0 = const("mod0", [P, 2 * KD, 2])
        adac = const("adac", [P, 8, KD])
        stat = const("stat", [P, 6, 2, 6])
        mv = const("mv", [P, 6, 2])
        std = const("std", [P, 6])
        rstd = const("rstd", [P, 6])
        nmr = const("nmr", [P, 6])
        gcol = const("gcol", [P, 2, ST, H])

        x_in = at("x_in", [P, TT, D], 48)
        c_in = at("c_in", [P, 2, D], 64)
        ada_in = at("ada_in", [P, 4, KD, 512], 72)
        modrow = at("modrow", [2, 2 * D], 24)
        colrow = at("colrow", [P, 2, P], 32)
        ht_hi = at("ht_hi", [P, KD, NT], 0, F32R)
        ht_lo = at("ht_lo", [P, KD, NT], 24, F32R)
        xx_hi = at("xx_hi", [P, JH, NT], 48, F32R)
        xx_lo = at("xx_lo", [P, JH, NT], 60, F32R)
        xm = at("xm", [P, JH, NT], 72)
        q_hi = at("q_hi", [P, JH, NL], 84, F32R)
        q_lo = at("q_lo", [P, JH, NL], 92, F32R)
        k_hi = at("k_hi", [P, JH, NT], 100, F32R)
        k_lo = at("k_lo", [P, JH, NT], 112, F32R)
        tile = at("tile", [P, SLOTS, NT], 124)
        v_st_hi = at("v_st_hi", [P, ST, P], 133, F32R)
        v_st_lo = at("v_st_lo", [P, ST, P], 136, F32R)
        xc = at("xc", [P, 2, NT], 139)
        sx_st = at("sx_st", [P, 2, NL], 145)
        wg = at("wg", [P, 2, 3, JH, NG], 149)
        bg = at("bg", [1, NG], 151)
        pre = at("pre", [NG, NT], 48)
        g_i = at("g_i", [H, 2, NT], 52)
        g_f = at("g_f", [H, 2, NT], 58)
        g_t = at("g_t", [H, 2, NT], 64)
        g_F = at("g_F", [H, 2, NT], 70)
        g_g = at("g_g", [H, 2, NT], 76)
        g_M = at("g_M", [H, 2, NT], 82)
        g_z = at("g_z", [H, NT], 88)
        g_a = at("g_a", [H, 2, NT], 92)
        m_rows = at("m_rows", [P, NL], 144)
        mb = at("mb", [P, 2, NL], 146)
        junk = at("junk", [P, P], 152)
        y_acc = at("y_acc", [P, TT, D], 0)
        u_hi = at("u_hi", [P, JH, NL], 16, F32R)
        u_lo = at("u_lo", [P, JH, NL], 24, F32R)
        g1_row = at("g1_row", [P, D], 32)
        g2_row = at("g2_row", [P, D], 36)
        acc = at("acc", [P, 2, 512], 40)
        v_hi = at("v_hi", [P, ST, DH], 44, F32R)
        v_lo = at("v_lo", [P, ST, DH], 56, F32R)
        pf = at("pf", [P, ST, NL], 68)
        pb = at("pb", [P, ST, NL], 80)
        p_hi = at("p_hi", [P, ST, NL], 92, F32R)
        p_lo = at("p_lo", [P, ST, NL], 104, F32R)
        ef = at("ef", [P, 2, NL], 116)
        dg = at("dg", [P, 2, TT, P], 120)
        rr = at("rr", [P, 2, NL], 124)
        zt = at("zt", [P, 2, NL], 128)
        sxt = at("sxt", [P, 2, NL], 132)
        hn = at("hn", [P, TT, DH], 136)
        x_nat = at("x_nat", [P, TT, D], 16)
        x_res = at("x_res", [P, TT, D], 80)
        hh_hi = at("hh_hi", [P, KD, NL], 44, F32R)
        hh_lo = at("hh_lo", [P, KD, NL], 60, F32R)
        ff_hi = at("ff_hi", [P, FT, NL], 76, F32R)
        ff_lo = at("ff_lo", [P, FT, NL], 92, F32R)
        relu = at("relu", [P, 2, NL], 108)
        sq = at("sq", [P, 2, NL], 112)
        btile = at("btile", [P, 2, NL], 116)
        pg = at("pg", [P, D], 120)
        pbb = at("pbb", [P, D], 124)
        rows = at("rows", [P, 4, D], 136)
        a_hi = at("a_hi", [P, TT, 4, 512], 76, F32R)
        a_lo = at("a_lo", [P, TT, 4, 512], 108, F32R)
        ftile = [at("ftile0", [P, NL], 148), at("ftile1", [P, NL], 150)]

        psum = es.enter_context(nc.psum_tensor("psum", [P, 8, 512], F32))

        v_hi_d = nc.dram_tensor("v_hi_d", [H, P, ST, DH], F32, kind="Internal").ap()
        v_lo_d = nc.dram_tensor("v_lo_d", [H, P, ST, DH], F32, kind="Internal").ap()
        s_d = nc.dram_tensor("s_d", [H, ST, P, NL], F32, kind="Internal").ap()
        z_d = nc.dram_tensor("z_d", [DI // P, P, NL], F32, kind="Internal").ap()
        sx_d = nc.dram_tensor("sx_d", [DI // P, P, NL], F32, kind="Internal").ap()

        raw_landed = sems("raw_landed", 2)
        prepared = sem("prepared")
        w_ready = sem("w_ready")
        w_begun = sem("w_begun")
        pool_step = sem("pool_step")
        acc_zero = sem("acc_zero")
        bias_landed = sems("bias_landed", 2)
        ada_ready = sem("ada_ready")
        consts = sem("consts")
        in_landed = sems("in_landed", 4)
        ada0_landed = sems("ada0_landed", 4)
        silu_c = sem("silu_c")
        mod_sum = sem("mod_sum")
        modrow_done = sem("modrow_done")
        mod_T = sem("mod_T")
        col_T = sem("col_T")
        cols_done = sem("cols_done")
        mod_done = sem("mod_done")
        var_done = sem("var_done")
        std_done = sem("std_done")
        xhat_done = sem("xhat_done")
        x0_full = sems("x0_full", 3)
        x0_tile = sems("x0_tile", 3)
        x0_split = sems("x0_split", 3)
        ht_ready = sem("ht_ready")
        full = sems("full", SLOTS)
        evac = sems("evac", SLOTS)
        aux = sems("aux", SLOTS)
        taken = sems("taken", SLOTS)
        spilled = sems("spilled", SLOTS)
        x_split = sem("x_split")
        qk_split = sem("qk_split")
        conv_done = sem("conv_done")
        xc_done = sem("xc_done")
        sx_done = sem("sx_done")
        sx_spilled = sems("sx_spilled", 2)
        v_split = sem("v_split")
        v_spilled = sem("v_spilled")
        wg_landed = sems("wg_landed", 2)
        wg_used = sem("wg_used")
        bg_landed = sem("bg_landed")
        gates_full = sem("gates_full")
        scans = sem("scans")
        m_landed = sem("m_landed")
        pre_done = sem("pre_done")
        gate_rows = sem("gate_rows")
        abs_f = sem("abs_f")
        soft = sem("soft")
        g_done = sem("g_done")
        gT_full = sem("gT_full")
        m_done = sem("m_done")
        s_landed = sem("s_landed")
        v_landed = sem("v_landed")
        z_landed = sems("z_landed", 2)
        bc_full = sem("bc_full")
        bc_free = sem("bc_free")
        gg_ready = sem("gg_ready")
        mb_read = sem("mb_read")
        dgx = sem("dgx")
        dge = sem("dge")
        eb_done = sem("eb_done")
        ef_done = sem("ef_done")
        ef_read = sem("ef_read")
        p_done = sem("p_done")
        sums = sem("sums")
        pool_sum = sem("pool_sum")
        r_done = sem("r_done")
        norm_done = sem("norm_done")
        p_split = sem("p_split")
        pv_full = sems("pv_full", 2)
        pv_free = sems("pv_free", 2)
        h_var = sem("h_var")
        h_std = sem("h_std")
        h_norm = sem("h_norm")
        tr_full = sem("tr_full")
        tr_free = sem("tr_free")
        u_done = sem("u_done")
        zu_done = sem("zu_done")
        y_full = sems("y_full", TT)
        y_free = sems("y_free", TT)
        res_landed = sem("res_landed")
        pgb_landed = sem("pgb_landed")
        b_var = sem("b_var")
        b_std = sem("b_std")
        b_stat = sem("b_stat")
        b_norm_in = sem("b_norm_in")
        b_turned = sem("b_turned")
        b_cols = sem("b_cols")
        b_norm = sem("b_norm")
        b_x = sem("b_x")
        b_xhat = sem("b_xhat")
        b_full = sems("b_full", 2)
        b_tile = sems("b_tile", 2)
        b_split = sems("b_split", 2)
        y_zero = sem("y_zero")
        a_full = sems("a_full", 2)
        a_relu = sems("a_relu", 2)
        a_sq = sems("a_sq", 2)
        a_split = sems("a_split", 2)
        c_full = sem("c_full")
        c_row = sem("c_row")
        f_full = sems("f_full", 2)
        f_tile = sems("f_tile", 2)
        f_split = sems("f_split", 2)
        stored = sem("stored")

        def mul3(pe, dst, lh, ll, rh, rl, first, last, begun=None):
            mm = pe.matmul(dst, lh, rh, start=first, stop=False)
            if begun is not None:
                mm.then_inc(begun, 1)
            pe.matmul(dst, lh, rl, start=False, stop=False)
            return pe.matmul(dst, ll, rh, start=False, stop=last)

        def tblk(i, n=P):
            return slice(i * n, (i + 1) * n)

        block = es.enter_context(nc.Block())

        @block.sync
        def _(sp):
            sp.dma_start(cvec[:, 0], c.rearrange("a (p k) -> p (a k)", k=KD)).then_inc(in_landed[0], 16)
            sp.dma_start(cvec[:, 1], c_ctx.rearrange("(p k) -> p k", k=KD)).then_inc(in_landed[0], 16)
            for n in range(4):
                sp.dma_start(ada_in[:, n], ada_w[0].rearrange("(p k) n -> p k n", k=KD)[:, :, tblk(n, 512)]
                             ).then_inc(ada0_landed[n], 16)
            sp.dma_start(colrow[:, 0], m_w_conv.rearrange("a k l (j p) -> (a k l j) p", p=P)[0:128]
                         ).then_inc(in_landed[3], 16)
            sp.dma_start(colrow[0:16, 1], m_w_conv.rearrange("a k l (j p) -> (a k l j) p", p=P)[128:144]
                         ).then_inc(in_landed[3], 16)
            for n, v in enumerate((m_b_conv, m_gn_w, m_skip)):
                sp.dma_start(colrow[16 + 16 * n:32 + 16 * n, 1], v.rearrange("a (j p) -> (a j) p", p=P)
                             ).then_inc(in_landed[3], 16)
            sp.dma_start(colrow[64:80, 1], ada_b[0:1, 0:2 * D].rearrange("a (j p) -> (a j) p", p=P)
                         ).then_inc(in_landed[3], 16)
            sp.dma_start(bg[:, :], m_b_gate).then_inc(bg_landed, 16)

            def raw_unit(n, slot, src, free=True):
                if free:
                    sp.wait_ge(prepared, n - 1)
                sp.dma_start(raw[:, slot], src).then_inc(raw_landed[slot], 16)

            w_in_v = m_w_in[0].rearrange("(k p) n -> p k n", p=P)

            def head_units(h, hh, n, lead=False):
                def cols_of(start):
                    return w_in_v[:, :, bass.ds(start, 256)]

                def square(w):
                    return w[0][bass.ds(h, 1)].rearrange("a (k p) n -> p (a k) n", p=P)

                sp.wait_ge(wg_used, h + 1)
                for m in range(3):
                    sp.dma_start(wg[:, hh, m], m_w_gate[0, m].rearrange("(j p) n -> p j n", p=P)
                                 [:, bass.ds(h * JH, JH)]).then_inc(wg_landed[hh], 16)
                src = [cols_of(h * DH), cols_of(h * DH + 256), square(m_w_v), cols_of(h * DH + DI),
                       cols_of(h * DH + DI + 256), square(m_w_q), square(m_w_k)]
                for u in range(7):
                    raw_unit(n + u, (7 * hh + u) % 2, src[u])

            with sp.Fori(0, H // 2) as it:
                for hh in range(2):
                    head_units(it * 2 + hh, hh, it * 14 + 7 * hh + 2)

            def ada_src(layer, col, half):
                return ada_w[layer].rearrange("(p k) n -> p k n", k=KD)[:, tblk(half, 4), bass.ds(col, 512)]

            def chunk(layer, col, ch, n, slot0, par):
                sp.wait_ge(acc_zero, ch + 1)
                sp.dma_start(acc[0:1, par], ada_b[layer:layer + 1, bass.ds(col, 512)]
                             ).then_inc(bias_landed[par], 16)
                for half in range(2):
                    raw_unit(n + half, (slot0 + half) % 2, ada_src(layer, col, half))

            w_out_v = m_w_out[0].rearrange("(k p) n -> p k n", p=P)
            n = RAW0_P2 + 2
            for h in range(H):
                for i in range(2):
                    chunk(0, ADA0[h] * D + i * 512, 2 * h + i, n, 0, i)
                    n += 2
                for half in range(2):
                    raw_unit(n, half, w_out_v[:, tblk(h, JH), tblk(half, 512)])
                    n += 1

            def mlp_units(layer, n0, chunk0):
                w1 = mlp_w1[layer].rearrange("(k p) n -> p k n", p=P)
                w2 = mlp_w2[layer].rearrange("(k p) n -> p k n", p=P)
                step = 12 if chunk0 is not None else 8
                with sp.Fori(0, GROUPS) as g:
                    n = g * step + n0 + 2
                    for u in range(4):
                        raw_unit(n + u, (n0 + u) % 2, w1[:, :, bass.ds(g * 1024 + u * 256, 256)])
                    n = n + 4
                    if chunk0 is not None:
                        for i in range(2):
                            chunk(1, g * D + i * 512, g * 2 + chunk0 + i, n + 2 * i, n0 % 2, i)
                        n = n + 4
                    for u in range(4):
                        raw_unit(n + u, (n0 + u) % 2,
                                 w2[:, bass.ds(g * FT + (u % 2) * 4, 4), tblk(u // 2, 512)])

            assert RAW0_MLP0 % 2 == 0 and SPLIT0_MLP0 % 2 == 0
            mlp_units(0, RAW0_MLP0, CHUNK0_MLP0)

            n = RAW0_F
            for u in range(3):
                raw_unit(n + 2, n % 2, dft[u])
                n += 1
            f_v = f_w_out[0].rearrange("(k p) n -> p k n", p=P)
            for i in range(4):
                chunk(1, ADA1_TAIL[i // 2] * D + (i % 2) * 512, CHUNK0_F + i, n + 2, n % 2, i % 2)
                n += 2
            for u in range(4):
                raw_unit(n + 2, n % 2, f_v[:, tblk(u % 2, 4), tblk(u // 2, 512)])
                n += 1
            mlp_units(1, RAW0_MLP1, None)

            out_v = out.rearrange("a (i p) d -> p (a i) d", p=P)
            for i in range(TT):
                sp.wait_ge(b_x, 3 * TT + i + 1)
                sp.dma_start(out_v[:, i], x_nat[:, i]).then_inc(stored, 16)
            sp.wait_ge(stored, 16 * TT)

        @block.gpsimd
        def _(pool):
            g = nc.gpsimd
            g.memset(ident[:], 0.0)
            g.memset(ones[:], 1.0)
            g.memset(sel[:], 0.0)
            g.memset(mask[:], 1.0)
            pool.drain()
            g.affine_select(out=ident[:], in_=ident[:], compare_op=ALU.not_equal, fill=1.0, base=0,
                            pattern=[[-1, P]], channel_multiplier=1)
            for q in range(4):
                pool.drain()
                g.affine_select(out=sel[32 * q:32 * q + 32], in_=sel[32 * q:32 * q + 32],
                                compare_op=ALU.not_equal, fill=1.0, base=0,
                                pattern=[[-1, H], [0, P]], channel_multiplier=1)
            pool.drain()
            g.affine_select(out=mask[:, 0], in_=mask[:, 0], compare_op=ALU.is_ge, fill=0.0, base=0,
                            pattern=[[1, P]], channel_multiplier=-1)
            g.affine_select(out=mask[:, 1], in_=mask[:, 1], compare_op=ALU.is_ge, fill=0.0, base=0,
                            pattern=[[-1, P]], channel_multiplier=1)
            pool.drain().then_inc(consts, 1)
            pool.wait_ge(consts, 1)
            pool.sem_inc(prepared, 2)
            pool.sem_inc(wg_used, 2)

            def split_unit(n, slot, m, wslot):
                pool.wait_ge(raw_landed[slot], n)
                pool.wait_ge(w_begun, m)
                pool.sem_inc(pool_step, 1)
                g.tensor_scalar(w_hi[:, wslot], raw[:, slot], 1.0, 0.0, ALU.mult, ALU.add)
                pool.drain()
                g.tensor_tensor(w_lo[:, wslot], raw[:, slot], w_hi[:, wslot].bitcast(F32), ALU.subtract)
                pool.drain().then_inc(w_ready, 1)
                pool.sem_inc(prepared, 1)

            def chunk(landed, slots, bias, par):
                g.memset(acc[:, par], 0.0)
                pool.drain().then_inc(acc_zero, 1)
                for half in range(2):
                    if half == 0:
                        pool.wait_ge(bias_landed[par], bias)
                    pool.wait_ge(raw_landed[slots[half]], landed[half])
                    pool.sem_inc(pool_step, 1)
                    part = raw[:, slots[half]].rearrange("p (k n) -> p k n", k=4)
                    g.tensor_tensor(part, part, svec[:, 0, 4 * half:4 * half + 4].unsqueeze(2).to_broadcast([P, 4, 512]), ALU.mult)
                    pool.drain()
                    g.tensor_tensor(part[:, 0:2], part[:, 0:2], part[:, 2:4], ALU.add)
                    pool.drain()
                    g.tensor_tensor(part[:, 0], part[:, 0], part[:, 1], ALU.add)
                    pool.drain()
                    g.tensor_tensor(acc[:, par], acc[:, par], part[:, 0], ALU.add)
                    pool.drain().then_inc(prepared, 1)
                pool.sem_inc(ada_ready, 1)

            with pool.Fori(0, H // 2) as it:
                for u in range(14):
                    split_unit(it * (7 * 16) + 16 * (u // 2 + 1), u % 2, it * 14 + u, u % 2)

            pool.wait_ge(silu_c, 1)
            n, m = RAW0_P2, SPLIT0_P2
            pool.wait_ge(m_done, 1)
            for h in range(H):
                for i in range(2):
                    if h:
                        pool.wait_ge(bc_full, 8 * (h - 1) + 7 + i)
                    chunk([16 * (n // 2 + 1), 16 * ((n + 1) // 2 + 1)], [n % 2, (n + 1) % 2], 16 * (h + 1), i)
                    n += 2
                for i in range(2):
                    split_unit(16 * (n // 2 + 1), n % 2, m, m % 2)
                    n += 1
                    m += 1

            def mlp(n0, m0, chunk0):
                step = 12 if chunk0 is not None else 8
                with pool.Fori(0, GROUPS) as gr:
                    def landed(u):
                        return gr * (8 * step) + 16 * ((n0 + u) // 2 + 1)

                    for u in range(4):
                        split_unit(landed(u), (n0 + u) % 2, gr * 8 + m0 + u, (m0 + u) % 2)
                    u = 4
                    if chunk0 is not None:
                        for i in range(2):
                            pool.wait_ge(c_full, gr * 2)
                            pool.sem_inc(pool_step, 1)
                            chunk([landed(u), landed(u + 1)], [(n0 + u) % 2, (n0 + u + 1) % 2],
                                  gr * 16 + 16 * (chunk0 // 2 + 1), i)
                            u += 2
                    for w in range(4):
                        split_unit(landed(u + w), (n0 + u + w) % 2, gr * 8 + m0 + 4 + w, (m0 + w) % 2)

            pool.wait_ge(bc_full, 32)
            mlp(RAW0_MLP0, SPLIT0_MLP0, CHUNK0_MLP0)
            n, m = RAW0_F, SPLIT0_F
            for u in range(3):
                split_unit(16 * (n // 2 + 1), n % 2, m, m % 2)
                n += 1
                m += 1
            for i in range(4):
                pool.wait_ge(c_full, 2 * GROUPS - 1 + i)
                chunk([16 * (n // 2 + 1), 16 * ((n + 1) // 2 + 1)], [n % 2, (n + 1) % 2],
                      16 * ((CHUNK0_F + i) // 2 + 1), i % 2)
                n += 2
            for u in range(4):
                split_unit(16 * (n // 2 + 1), n % 2, m, m % 2)
                n += 1
                m += 1
            mlp(RAW0_MLP1, SPLIT0_MLP1, None)

        @block.tensor
        def _(pe):
            pe.wait_ge(consts, 1)
            pe.wait_ge(in_landed[3], 96)
            pe.transpose(psum[:, 7, 0:128], colrow[:, 0], ident[:])
            pe.transpose(psum[:, 7, 128:208], colrow[0:80, 1], ident[0:80, 0:80]).then_inc(col_T, 1)
            pe.wait_ge(silu_c, 1)
            for n in range(4):
                pe.wait_ge(ada0_landed[n], 16)
                for k in range(KD):
                    mm = pe.matmul(psum[0:2, n, :], svec[:, :, k], ada_in[:, n, k], start=(k == 0),
                                   stop=(k == KD - 1))
                mm.then_inc(mod_sum, 1)
            pe.wait_ge(modrow_done, 4)
            for j in range(2 * KD):
                mm = pe.transpose(psum[:, 6, 2 * j:2 * j + 2], modrow[0:2, tblk(j)], ident[0:2, 0:2])
            mm.then_inc(mod_T, 1)
            pe.wait_ge(xhat_done, 1)
            for k in range(KD):
                r = k % 3
                if k >= 3:
                    pe.wait_ge(x0_tile[r], k // 3)
                for i in range(TT):
                    pe.transpose(psum[:, 2 * r, tblk(i)], x_in[:, i, tblk(k)], ident[:])
                for i in range(2):
                    mm = pe.transpose(psum[:, 2 * r + 1, tblk(i)], c_in[:, i, tblk(k)], ident[:])
                mm.then_inc(x0_full[r], 1)

            pe.wait_ge(bg_landed, 16)
            pe.wait_ge(cols_done, 1)
            pe.wait_ge(mod_done, 1)
            pe.wait_ge(x0_tile[1], 3)
            pe.matmul(psum[0:NG, 6, 0:128], bg[0:1, :], ones[0:1, :], start=True, stop=False,
                      skip_group_check=True)
            for i in range(1, 4):
                pe.matmul(psum[0:NG, 6, tblk(i)], bg[0:1, :], ones[0:1, :], start=False, stop=False,
                          skip_group_check=True)
            pe.matmul(psum[0:NG, 7, 0:128], bg[0:1, :], ones[0:1, :], start=True, stop=False,
                      skip_group_check=True)
            pe.matmul(psum[0:NG, 7, 128:256], bg[0:1, :], ones[0:1, :], start=False, stop=False,
                      skip_group_check=True)
            pe.wait_ge(ht_ready, KD)

            def slot_of(what, h):
                n = USE[what]
                pe.wait_ge(evac[n % SLOTS], h * USES + n // SLOTS)
                return n % SLOTS

            def expand(what, h, slot, col, rh, rl, kt, ctx_too, begun=None):
                r = slot_of(what, h)
                wh = w_hi[:, slot].rearrange("p (k n) -> p k n", k=kt)
                wl = w_lo[:, slot].rearrange("p (k n) -> p k n", k=kt)
                for k in range(kt):
                    mm = mul3(pe, psum[:, 2 * r, :], wh[:, k, tblk(col)], wl[:, k, tblk(col)],
                              rh[:, k, NC:NT], rl[:, k, NC:NT], k == 0, k == kt - 1,
                              begun if k == 0 else None)
                if ctx_too:
                    for k in range(kt):
                        mm = mul3(pe, psum[:, 2 * r + 1, 0:NC], wh[:, k, tblk(col)], wl[:, k, tblk(col)],
                                  rh[:, k, 0:NC], rl[:, k, 0:NC], k == 0, k == kt - 1)
                mm.then_inc(full[r], 1)
                return mm

            def unit_ready(m):
                pe.wait_ge(w_ready, m + 1)

            def gate(kind, j, h, hh):
                what = ("vT" if kind == 2 else "qk"[kind], j)
                n = USE[what]
                r = n % SLOTS
                pe.wait_ge(evac[r], h * USES + n // SLOTS + 1)
                pe.matmul(psum[0:NG, 6, :], wg[:, hh, kind, j], tile[:, r, NC:NT], start=False, stop=False,
                          skip_group_check=True)
                mm = pe.matmul(psum[0:NG, 7, 0:NC], wg[:, hh, kind, j], tile[:, r, 0:NC], start=False,
                               stop=False, skip_group_check=True)
                if kind < 2:
                    mm.then_inc(aux[r], 1)

            def turn_v(j, h):
                r = slot_of(("vN", j), h)
                src = USE[("vT", j)] % SLOTS
                for s in range(ST):
                    bank, at_ = (2 * r, s - 2) if s >= 2 else (2 * r + 1, s)
                    mm = pe.transpose(psum[:, bank, tblk(at_)], tile[:, src, tblk(s)], ident[:])
                mm.then_inc(full[r], 1)

            with pe.Fori(0, H // 2) as it:
                for hh in range(2):
                    h = it * 2 + hh
                    m0 = it * 14 + 7 * hh
                    sl = [(7 * hh + u) % 2 for u in range(7)]
                    for u in range(2):
                        unit_ready(m0 + u)
                        for c2 in range(2):
                            expand(("xm", 2 * u + c2), h, sl[u], c2, ht_hi, ht_lo, KD, True,
                                   w_begun if c2 == 0 else None)
                    unit_ready(m0 + 2)
                    pe.wait_ge(x_split, h * 8 + 4)
                    pe.wait_ge(wg_landed[hh], it * 48 + 48)
                    for j in range(JH):
                        expand(("vT", j), h, sl[2], j, xx_hi, xx_lo, JH, True, w_begun if j == 0 else None)
                        if j >= 1:
                            gate(2, j - 1, h, hh)
                            turn_v(j - 1, h)
                    for u in range(2):
                        unit_ready(m0 + 3 + u)
                        for c2 in range(2):
                            expand(("z", 2 * u + c2), h, sl[3 + u], c2, ht_hi, ht_lo, KD, False,
                                   w_begun if c2 == 0 else None)
                            if u == 0 and c2 == 0:
                                gate(2, 3, h, hh)
                                turn_v(3, h)
                    unit_ready(m0 + 5)
                    pe.wait_ge(x_split, h * 8 + 8)
                    for j in range(JH):
                        expand(("q", j), h, sl[5], j, xx_hi, xx_lo, JH, True, w_begun if j == 0 else None)
                        if j >= 1:
                            gate(0, j - 1, h, hh)
                    unit_ready(m0 + 6)
                    for j in range(JH):
                        expand(("k", j), h, sl[6], j, xx_hi, xx_lo, JH, True, w_begun if j == 0 else None)
                        gate(1, j - 1, h, hh) if j >= 1 else gate(0, 3, h, hh)
                    pe.wait_ge(qk_split, h * 8 + 8)
                    for s in range(ST):
                        r = slot_of(("S", s), h)
                        for k in range(JH):
                            mm = mul3(pe, psum[:, 2 * r, :], k_hi[:, k, tblk(s)], k_lo[:, k, tblk(s)],
                                      q_hi[:, k], q_lo[:, k], k == 0, k == JH - 1,
                                      wg_used if s == 1 and k == 0 else None)
                        mm.then_inc(full[r], 1)
                        if s == 0:
                            gate(1, 3, h, hh)
            pe.drain().then_inc(gates_full, 1)

            pe.wait_ge(g_done, 1)
            for d in range(2):
                for s in range(ST):
                    mm = pe.transpose(psum[:, 0, (d * ST + s) * H:(d * ST + s + 1) * H],
                                      g_g[0:H, d, tblk(s)], ident[0:H, 0:H])
            mm.then_inc(gT_full, 1)
            pe.wait_ge(m_done, 1)
            pe.wait_ge(m_landed, 64)
            uses = [0]

            def bc_bank():
                if uses[0]:
                    pe.wait_ge(bc_free, uses[0])
                uses[0] += 1

            def broadcasts(h):
                for kind in range(2):
                    for d in range(2):
                        bc_bank()
                        q = 32 * (2 * kind + d)
                        pe.matmul(psum[:, 3, :], sel[q:q + H, h], m_rows[q:q + H, :], start=True,
                                  stop=True).then_inc(bc_full, 1)

            def denominators(h):
                for d in range(2):
                    bc_bank()
                    pe.wait_ge(sums, 2 * h + d + 1)
                    pe.matmul(psum[:, 3, :], ones[:], dg[:, d].rearrange("p j t -> p (j t)"), start=True,
                              stop=True).then_inc(bc_full, 1)

            def chunks(ch):
                for i in range(2):
                    bc_bank()
                    pe.wait_ge(ada_ready, ch + i + 1)
                    pe.matmul(psum[:, 3, :], ones[:], acc[:, i], start=True, stop=True).then_inc(bc_full, 1)

            yuse = [0]

            def contract(lh, ll, k0, slot, wait_free=None):
                wh = w_hi[:, slot].rearrange("p (k n) -> p k n", k=4)
                wl = w_lo[:, slot].rearrange("p (k n) -> p k n", k=4)
                for i in range(TT):
                    if wait_free is not None:
                        pe.wait_ge(y_free[i], wait_free)
                    elif yuse[0]:
                        pe.wait_ge(y_free[i], yuse[0])
                    for k in range(4):
                        mm = mul3(pe, psum[:, 4 + i, :], lh[:, k0 + k, tblk(i)], ll[:, k0 + k, tblk(i)],
                                  wh[:, k], wl[:, k], k == 0, k == 3,
                                  w_begun if i == 0 and k == 0 else None)
                    mm.then_inc(y_full[i], 1)
                if wait_free is None:
                    yuse[0] += 1

            broadcasts(0)
            denominators(0)
            for h in range(H):
                pe.wait_ge(p_split, h + 1)
                pe.wait_ge(v_landed, 32 * (h + 1))
                for i in range(TT):
                    b = i % 2
                    if h * 2 + i // 2:
                        pe.wait_ge(pv_free[b], h * 2 + i // 2)
                    for s in range(ST):
                        mm = mul3(pe, psum[:, b, :], p_hi[:, s, tblk(i)], p_lo[:, s, tblk(i)],
                                  v_hi[:, s], v_lo[:, s], s == 0, s == ST - 1)
                    mm.then_inc(pv_full[b], 1)
                chunks(2 * h)
                if h + 1 < H:
                    broadcasts(h + 1)
                pe.wait_ge(h_norm, h + 1)
                for e in range(JH):
                    if h * JH + e:
                        pe.wait_ge(tr_free, h * JH + e)
                    for i in range(TT):
                        mm = pe.transpose(psum[:, 2, tblk(i)], hn[:, i, tblk(e)], ident[:])
                    mm.then_inc(tr_full, 1)
                pe.wait_ge(u_done, h + 1)
                for half in range(2):
                    unit_ready(SPLIT0_P2 + 2 * h + half)
                    contract(u_hi, u_lo, 0, (SPLIT0_P2 + 2 * h + half) % 2)
                if h + 1 < H:
                    denominators(h + 1)

            def boundary(b):
                pe.wait_ge(b_xhat, b + 1)
                for k in range(KD):
                    r = k % 2
                    if b * 4 + k // 2:
                        pe.wait_ge(b_tile[r], b * 4 + k // 2)
                    for i in range(TT):
                        mm = pe.transpose(psum[:, r, tblk(i)], y_acc[:, i, tblk(k)], ident[:])
                    mm.then_inc(b_full[r], 1)
                pe.drain().then_inc(b_turned, 1)

            def mlp(layer, m0, y0, chunk0):
                pe.wait_ge(b_split[0], (2 * layer + 1) * 4)
                pe.wait_ge(b_split[1], (2 * layer + 1) * 4)
                with pe.Fori(0, GROUPS) as gr:
                    for u in range(4):
                        slot = (m0 + u) % 2
                        wh = w_hi[:, slot].rearrange("p (k n) -> p k n", k=KD)
                        wl = w_lo[:, slot].rearrange("p (k n) -> p k n", k=KD)
                        unit_ready(gr * 8 + m0 + u)
                        for c2 in range(2):
                            pe.wait_ge(a_relu[c2], gr * 4 + layer * 16 + u)
                            for k in range(KD):
                                mm = mul3(pe, psum[:, c2, :], wh[:, k, tblk(c2)], wl[:, k, tblk(c2)],
                                          hh_hi[:, k], hh_lo[:, k], k == 0, k == KD - 1,
                                          w_begun if c2 == 0 and k == 0 else None)
                            mm.then_inc(a_full[c2], 1)
                    if chunk0 is not None:
                        for i in range(2):
                            pe.wait_ge(ada_ready, gr * 2 + chunk0 + i + 1)
                            pe.wait_ge(c_row, gr * 2 + i)
                            pe.matmul(psum[:, 2, :], ones[:], acc[:, i], start=True, stop=True
                                      ).then_inc(c_full, 1)
                    for u in range(4):
                        unit_ready(gr * 8 + m0 + 4 + u)
                        if u == 0:
                            pe.wait_ge(a_split[0], gr * 4 + layer * 16 + 2)
                            pe.wait_ge(a_split[1], gr * 4 + layer * 16 + 2)
                        if u == 1:
                            pe.wait_ge(a_split[0], gr * 4 + layer * 16 + 4)
                            pe.wait_ge(a_split[1], gr * 4 + layer * 16 + 4)
                        contract(ff_hi, ff_lo, (u % 2) * 4, (m0 + u) % 2, gr * 4 + y0 + u)

            boundary(0)
            mlp(0, SPLIT0_MLP0, 8, CHUNK0_MLP0)
            boundary(1)

            pe.wait_ge(b_split[0], 8)
            pe.wait_ge(b_split[1], 8)
            m = SPLIT0_F
            unit_ready(m)
            s0 = m % 2
            n = 0
            for gr in range(4):
                for i in range(TT):
                    if n >= 2:
                        pe.wait_ge(f_tile[n % 2], n // 2)
                    for k in range(2):
                        mm = mul3(pe, psum[:, n % 2, :], hh_hi[:, 2 * gr + k, tblk(i)],
                                  hh_lo[:, 2 * gr + k, tblk(i)], w_hi[:, s0, tblk(k, 512)],
                                  w_lo[:, s0, tblk(k, 512)], k == 0, k == 1,
                                  w_begun if n == 0 and k == 0 else None)
                    mm.then_inc(f_full[n % 2], 1)
                    n += 1
            unit_ready(m + 1)
            pe.wait_ge(f_split[0], 8)
            pe.wait_ge(f_split[1], 8)
            for gr in range(4):
                for part in range(2):
                    sl = (m + 1 + part) % 2
                    if gr == 0 and part == 1:
                        unit_ready(m + 2)
                    for half in range(2):
                        n = 16 + 2 * gr + half
                        if part == 0:
                            pe.wait_ge(f_tile[n % 2], n // 2)
                        begins = half == 0 and (gr, part) in ((0, 0), (3, 1))
                        for i in range(TT):
                            cs = slice(part * 256 + half * P, part * 256 + half * P + P)
                            mm = mul3(pe, psum[:, n % 2, :], a_hi[:, i, gr, cs], a_lo[:, i, gr, cs],
                                      w_hi[:, sl, tblk(i, 512)], w_lo[:, sl, tblk(i, 512)],
                                      part == 0 and i == 0, part == 1 and i == TT - 1,
                                      w_begun if begins and i == 0 else None)
                        if part == 1:
                            mm.then_inc(f_full[n % 2], 1)
            for i in range(4):
                pe.wait_ge(ada_ready, CHUNK0_F + i + 1)
                pe.wait_ge(c_row, 2 * GROUPS + i)
                pe.matmul(psum[:, 2, :], ones[:], acc[:, i % 2], start=True, stop=True).then_inc(c_full, 1)
            pe.wait_ge(f_split[0], 12)
            pe.wait_ge(f_split[1], 12)
            for u in range(4):
                unit_ready(m + 3 + u)
                contract(hh_hi, hh_lo, (u % 2) * 4, (m + 3 + u) % 2, 24 + u)
            boundary(2)
            mlp(1, SPLIT0_MLP1, 28, None)

        @block.scalar
        def _(act):
            a = nc.scalar
            act.dma_start(x_in[:], x.rearrange("a (i p) d -> p (a i) d", p=P)).then_inc(in_landed[1], 16)
            act.dma_start(c_in[:], ctx.rearrange("a (i p) d -> p (a i) d", p=P)).then_inc(in_landed[2], 16)
            act.wait_ge(in_landed[0], 32)
            a.activation(svec[:], cvec[:], ACT.Silu).then_inc(silu_c, 1)
            for n in range(4):
                act.wait_ge(mod_sum, n + 1)
                a.copy(modrow[0:2, tblk(n, 512)], psum[0:2, n, :]).then_inc(modrow_done, 1)
            act.wait_ge(var_done, 1)
            a.activation(std[:], std[:], ACT.Sqrt).then_inc(std_done, 1)
            act.wait_ge(mod_done, 1)
            for k in range(KD):
                r = k % 3
                act.wait_ge(x0_full[r], k // 3 + 1)
                if k >= 3:
                    act.wait_ge(x0_split[r], k // 3)
                a.activation(tile[:, r, NC:NT], psum[:, 2 * r, :], ACT.Identity,
                             scale=mod0[:, KD + k, 0:1], bias=mod0[:, k, 0:1])
                a.activation(tile[:, r, 0:NC], psum[:, 2 * r + 1, 0:NC], ACT.Identity,
                             scale=mod0[:, KD + k, 1:2], bias=mod0[:, k, 1:2]).then_inc(x0_tile[r], 1)

            act.wait_ge(ht_ready, KD)

            def stage_tile(what, h):
                n = USE[what]
                r = n % SLOTS
                act.wait_ge(full[r], h * USES + n // SLOTS + 1)
                if what[0] == "xm":
                    act.wait_ge(conv_done, h * JH)
                else:
                    prev = n - SLOTS
                    while prev >= 0 and HEAD[prev][0] == "xm":
                        prev -= SLOTS
                    for reader, s, w in (("pe", aux, 1), ("dve", taken, 1), ("dma", spilled, 16)):
                        if reader in READERS[HEAD[prev][0]]:
                            act.wait_ge(s[r], h * (w * reads_per_head(reader, r))
                                        + w * reads_before(reader, prev))
                    if HEAD[prev][0] == "vT":
                        t = USE[("vN", HEAD[prev][1])]
                        act.wait_ge(full[t % SLOTS], h * USES + t // SLOTS + 1)
                dst = xm[:, what[1]] if what[0] == "xm" else tile[:, r]
                lat_only = what[0] in ("z", "S")
                if what[0] == "z":
                    op = a.activation(dst[:, NC:NT], psum[:, 2 * r, :], ACT.Silu)
                elif lat_only:
                    op = a.copy(dst[:, NC:NT], psum[:, 2 * r, :])
                else:
                    scale = K_SCALE if what[0] == "k" else 1.0
                    a.activation(dst[:, NC:NT], psum[:, 2 * r, :], ACT.Copy, scale=scale)
                    op = a.activation(dst[:, 0:NC], psum[:, 2 * r + 1, 0:NC], ACT.Copy, scale=scale)
                op.then_inc(evac[r], 1)
                return n, r

            def spill(n, r, h, dst):
                act.wait_ge(evac[r], h * USES + n // SLOTS + 1)
                act.dma_start(dst, tile[:, r, NC:NT]).then_inc(spilled[r], 16)

            def spill_v(j, h):
                act.wait_ge(v_split, h * JH + j + 1)
                for st_, d_ in ((v_st_hi, v_hi_d), (v_st_lo, v_lo_d)):
                    act.dma_start(d_[bass.ds(h, 1)].rearrange("a p s e -> p (a s) e")[:, :, tblk(j)],
                                  st_[:].bitcast(F32)).then_inc(v_spilled, 16)

            def gate_x(j, h):
                act.wait_ge(conv_done, h * JH + j + 1)
                a.activation(xc[:, j % 2], xc[:, j % 2], ACT.Silu).then_inc(xc_done, 1)
                act.wait_ge(xc_done, h * JH + j + 1)
                act.wait_ge(sx_spilled[j % 2], h * 32 + 16 * (j // 2))
                a.activation(sx_st[:, j % 2], xc[:, j % 2, NC:NT], ACT.Copy,
                             scale=cols[:, bass.ds(h * JH + 176 + j, 1)]).then_inc(sx_done, 1)
                act.wait_ge(sx_done, h * JH + j + 1)
                act.dma_start(sx_d[bass.ds(h * JH + j, 1)].rearrange("a p t -> p (a t)"), sx_st[:, j % 2]
                              ).then_inc(sx_spilled[j % 2], 16)

            def z_out(j, h):
                n, r = stage_tile(("z", j), h)
                spill(n, r, h, z_d[bass.ds(h * JH + j, 1)].rearrange("a p t -> p (a t)"))

            with act.Fori(0, H // 2) as it:
                for hh in range(2):
                    h = it * 2 + hh
                    for what in HEAD[0:9]:
                        stage_tile(what, h)
                    spill_v(0, h)
                    stage_tile(("vT", 3), h)
                    gate_x(0, h)
                    stage_tile(("vN", 2), h)
                    spill_v(1, h)
                    z_out(0, h)
                    gate_x(1, h)
                    spill_v(2, h)
                    stage_tile(("vN", 3), h)
                    z_out(1, h)
                    gate_x(2, h)
                    z_out(2, h)
                    spill_v(3, h)
                    z_out(3, h)
                    gate_x(3, h)
                    for j in range(JH):
                        stage_tile(("q", j), h)
                    for j in range(JH):
                        stage_tile(("k", j), h)
                    for s in range(ST):
                        n, r = stage_tile(("S", s), h)
                        spill(n, r, h, s_d[bass.ds(h, 1), s].rearrange("a p t -> p (a t)"))

            act.wait_ge(gates_full, 1)
            a.copy(pre[:, NC:NT], psum[0:NG, 6, :])
            a.copy(pre[:, 0:NC], psum[0:NG, 7, 0:NC]).then_inc(pre_done, 1)
            act.wait_ge(pre_done, 1)
            for d in range(2):
                act.dma_start(g_i[:, d], pre[8 * d:8 * d + 4, :]).then_inc(gate_rows, 16)
                act.dma_start(g_f[:, d], pre[8 * d + 4:8 * d + 8, :]).then_inc(gate_rows, 16)
            act.wait_ge(abs_f, 1)
            a.activation(g_t[:], g_a[:], ACT.Exp, scale=-1.0).then_inc(soft, 1)
            act.wait_ge(soft, 1)
            a.activation(g_t[:], g_t[:], ACT.Ln, bias=1.0).then_inc(soft, 1)

            def load_head(h):
                if h:
                    act.wait_ge(p_split, h)
                act.dma_start(pf[:], s_d[h].rearrange("s p t -> p s t")).then_inc(s_landed, 16)
                if h:
                    act.wait_ge(pv_full[1], 2 * h)
                act.dma_start(v_hi[:].bitcast(F32), v_hi_d[h]).then_inc(v_landed, 16)
                act.dma_start(v_lo[:].bitcast(F32), v_lo_d[h]).then_inc(v_landed, 16)

            def load_z(h, e):
                n = h * JH + e
                if n >= 2:
                    act.wait_ge(zu_done, n - 1)
                act.dma_start(zt[:, n % 2], z_d[n]).then_inc(z_landed[n % 2], 16)
                act.dma_start(sxt[:, n % 2], sx_d[n]).then_inc(z_landed[n % 2], 16)

            for r in range(SLOTS):
                act.wait_ge(spilled[r], 16 * H * reads_per_head("dma", r))
            for r in range(2):
                act.wait_ge(sx_spilled[r], 32 * H)
            act.wait_ge(v_spilled, 32 * JH * H)
            act.wait_ge(scans, 1)
            for kind, src in ((0, g_M), (1, g_F)):
                for d in range(2):
                    q = 32 * (2 * kind + d)
                    act.dma_start(m_rows[q:q + H, :], src[:, d, NC:NT]).then_inc(m_landed, 16)
            act.wait_ge(m_done, 1)
            act.wait_ge(m_landed, 64)
            load_head(0)
            load_z(0, 0)
            load_z(0, 1)

            def rows_in(h):
                for kind in range(2):
                    for d in range(2):
                        act.wait_ge(bc_full, 8 * h + 2 * kind + d + 1)
                        if kind == 0:
                            a.copy(mb[:, d], psum[:, 3, :]).then_inc(bc_free, 1)
                        else:
                            a.activation(rr[:, d], psum[:, 3, :], ACT.Exp, scale=-1.0).then_inc(bc_free, 1)
                act.drain().then_inc(gg_ready, 1)

            def weights(h):
                act.wait_ge(dgx, h + 1)
                a.activation(dg[:], dg[:], ACT.Exp, scale=-1.0).then_inc(dge, 1)
                for s in range(ST):
                    n = NL if s < 2 else (s - 2) * P
                    if n:
                        a.activation(pb[:, s, 0:n], mb[:, 1, 0:n], ACT.Exp, scale=-1.0,
                                     bias=gcol[:, 1, s, h:h + 1])
                act.drain().then_inc(eb_done, 1)
                for s in range(ST - 1):
                    t0 = 0 if s < 2 else (s - 1) * P
                    n = 5 * h + s
                    if n >= 2:
                        act.wait_ge(ef_read, n - 1)
                    a.activation(ef[:, n % 2, t0:NL], mb[:, 0, t0:NL], ACT.Exp, scale=-1.0,
                                 bias=gcol[:, 0, s, h:h + 1]).then_inc(ef_done, 1)

            rows_in(0)
            weights(0)
            for h in range(H):
                for i in range(TT):
                    act.wait_ge(pv_full[i % 2], 2 * h + i // 2 + 1)
                    if h and i == 0:
                        act.wait_ge(tr_full, JH * h)
                    a.copy(hn[:, i], psum[:, i % 2, :]).then_inc(pv_free[i % 2], 1)
                if h + 1 < H:
                    load_head(h + 1)
                if ADA0[h] in (2, 5):
                    dst = g1_row if ADA0[h] == 2 else g2_row
                    for i in range(2):
                        act.wait_ge(bc_full, 8 * h + 7 + i)
                        a.copy(dst[:, tblk(i, 512)], psum[:, 3, :]).then_inc(bc_free, 1)
                act.wait_ge(h_var, h + 1)
                a.activation(std[:, 0:TT], std[:, 0:TT], ACT.Sqrt).then_inc(h_std, 1)
                if h + 1 < H:
                    rows_in(h + 1)
                for e in range(JH):
                    if h * JH + e + 2 < H * JH:
                        load_z((h * JH + e + 2) // JH, (h * JH + e + 2) % JH)
                if h + 1 < H:
                    weights(h + 1)

            def boundary_loads(b):
                act.dma_start(pg[:], post_g[b // 2, b % 2:b % 2 + 1, :].to_broadcast([P, D])
                              ).then_inc(pgb_landed, 16)
                act.dma_start(pbb[:], post_b[b // 2, b % 2:b % 2 + 1, :].to_broadcast([P, D])
                              ).then_inc(pgb_landed, 16)

            def boundary(b):
                act.wait_ge(b_var, 2 * b + 1)
                a.activation(std[:, 0:TT], std[:, 0:TT], ACT.Sqrt).then_inc(b_std, 1)
                for i in range(TT):
                    act.wait_ge(b_norm_in, 2 * b + 1)
                    a.activation(y_acc[:, i], y_acc[:, i], ACT.Identity, scale=rstd[:, i:i + 1],
                                 bias=nmr[:, i:i + 1]).then_inc(b_norm, 1)
                if b == 3:
                    return
                act.wait_ge(b_var, 2 * b + 2)
                a.activation(std[:, 0:TT], std[:, 0:TT], ACT.Sqrt).then_inc(b_std, 1)
                for i in range(TT):
                    act.wait_ge(b_norm_in, 2 * b + 2)
                    a.activation(y_acc[:, i], x_nat[:, i], ACT.Identity, scale=rstd[:, i:i + 1],
                                 bias=nmr[:, i:i + 1])
                act.drain().then_inc(b_xhat, 1)
                sh, sc = MODS[b]
                act.wait_ge(b_cols, b + 1)
                for k in range(KD):
                    r = k % 2
                    act.wait_ge(b_full[r], 4 * b + k // 2 + 1)
                    if b * 4 + k // 2:
                        act.wait_ge(b_split[r], 4 * b + k // 2)
                    a.activation(btile[:, r], psum[:, r, :], ACT.Identity, scale=adac[:, sc, k:k + 1],
                                 bias=adac[:, sh, k:k + 1]).then_inc(b_tile[r], 1)

            act.wait_ge(y_full[0], 7)
            act.dma_start(x_res[:], x.rearrange("a (i p) d -> p (a i) d", p=P)).then_inc(res_landed, 16)
            boundary_loads(0)
            boundary(0)

            def mlp(layer, chunk0):
                act.wait_ge(b_x, (2 * layer + 1) * TT)
                boundary_loads(2 * layer + 1)
                with act.Fori(0, GROUPS) as gr:
                    for u in range(4):
                        for c2 in range(2):
                            n = gr * 4 + layer * 16 + u
                            act.wait_ge(a_full[c2], n + 1)
                            act.wait_ge(a_sq[c2], n)
                            a.activation(relu[:, c2], psum[:, c2, :], ACT.Relu).then_inc(a_relu[c2], 1)
                            act.wait_ge(a_split[c2], n)
                            act.wait_ge(a_relu[c2], n + 1)
                            a.activation(sq[:, c2], relu[:, c2], ACT.Square).then_inc(a_sq[c2], 1)
                    if chunk0 is not None:
                        for i in range(2):
                            act.wait_ge(c_full, gr * 2 + i + 1)
                            a.copy(rows[:, bass.ds(gr, 1), tblk(i, 512)].rearrange("p a n -> p (a n)"),
                                   psum[:, 2, :]).then_inc(c_row, 1)

            mlp(0, CHUNK0_MLP0)
            boundary(1)
            for n in range(24):
                act.wait_ge(f_full[n % 2], n // 2 + 1)
                if n >= 2:
                    act.wait_ge(f_split[n % 2], n // 2)
                a.copy(ftile[n % 2][:], psum[:, n % 2, :]).then_inc(f_tile[n % 2], 1)
            for i in range(4):
                if i >= 2:
                    act.wait_ge(c_full, 2 * GROUPS + i + 1)
                    a.copy(g2_row[:, tblk(i % 2, 512)], psum[:, 2, :]).then_inc(c_row, 1)
            boundary_loads(2)
            boundary(2)
            mlp(1, None)
            boundary(3)

        @block.vector
        def _(dve):
            v = nc.vector

            def split(dst_hi, dst_lo, src):
                v.tensor_copy(dst_hi, src)
                dve.drain()
                return v.tensor_tensor(dst_lo, src, dst_hi.bitcast(F32), ALU.subtract)

            def finish_stats(n):
                dve.drain()
                for i in range(n):
                    v.bn_aggr(mv[:, i], stat[:, i].rearrange("p a b -> p (a b)"))
                dve.drain()
                return v.tensor_scalar(std[:, 0:n], mv[:, 0:n, 1], EPS, None, ALU.add)

            def rstd_nmr(n):
                v.reciprocal(rstd[:, 0:n], std[:, 0:n])
                dve.drain()
                return v.scalar_tensor_tensor(out=nmr[:, 0:n], in0=mv[:, 0:n, 0], scalar=-1.0,
                                              in1=rstd[:, 0:n], op0=ALU.mult, op1=ALU.mult)

            dve.wait_ge(in_landed[1], 16)
            for i in range(TT):
                for half in range(2):
                    v.bn_stats(stat[:, i, half], x_in[:, i, tblk(half, 512)])
            dve.wait_ge(in_landed[2], 16)
            for i in range(2):
                for half in range(2):
                    v.bn_stats(stat[:, TT + i, half], c_in[:, i, tblk(half, 512)])
            finish_stats(6).then_inc(var_done, 1)
            dve.wait_ge(std_done, 1)
            rstd_nmr(6)
            dve.drain()
            for i in range(TT):
                v.tensor_scalar(x_in[:, i], x_in[:, i], rstd[:, i:i + 1], nmr[:, i:i + 1], ALU.mult, ALU.add)
            for i in range(2):
                v.tensor_scalar(c_in[:, i], c_in[:, i], rstd[:, TT + i:TT + i + 1],
                                nmr[:, TT + i:TT + i + 1], ALU.mult, ALU.add)
            dve.drain().then_inc(xhat_done, 1)
            dve.wait_ge(col_T, 1)
            v.tensor_copy(cols[:], psum[:, 7, 0:208]).then_inc(cols_done, 1)
            dve.wait_ge(cols_done, 1)
            dve.wait_ge(mod_T, 1)
            for row in range(2):
                v.tensor_tensor(mod0[:, :, row], psum[:, 6, row:32:2], cols[:, 192:208], ALU.add)
            dve.drain()
            v.tensor_scalar(mod0[:, KD:2 * KD], mod0[:, KD:2 * KD], 1.0, None, ALU.add).then_inc(mod_done, 1)
            for k in range(KD):
                r = k % 3
                dve.wait_ge(x0_tile[r], k // 3 + 1)
                split(ht_hi[:, k], ht_lo[:, k], tile[:, r]).then_inc(x0_split[r], 1)
                dve.drain().then_inc(ht_ready, 1)

            def staged(what, h):
                n = USE[what]
                dve.wait_ge(evac[n % SLOTS], h * USES + n // SLOTS + 1)
                return n % SLOTS

            def conv(j, h):
                def tap(kl):
                    return cols[:, bass.ds(h * JH + kl * 16 + j, 1)]

                dve.drain()
                dve.wait_ge(sx_done, h * JH + (j - 1 if j >= 2 else 0))
                acc_ = xc[:, j % 2]
                src = xm[:, j]
                v.tensor_scalar(acc_, src, tap(4), cols[:, bass.ds(h * JH + 144 + j, 1)], ALU.mult, ALU.add)
                dve.drain()
                a_c, s_c = acc_[:, 0:NC], src[:, 0:NC]
                a_l = acc_[:, NC:NT].rearrange("p (r c) -> p r c", c=GRID)
                s_l = src[:, NC:NT].rearrange("p (r c) -> p r c", c=GRID)

                def add(dst, source, kl):
                    return v.scalar_tensor_tensor(out=dst, in0=source, scalar=tap(kl), in1=dst,
                                                  op0=ALU.mult, op1=ALU.add)

                add(a_c[:, 1:NC], s_c[:, 0:NC - 1], 3)
                for k in range(3):
                    for l in range(3):
                        if (k, l) == (1, 1):
                            continue
                        dr, dc = k - 1, l - 1
                        r0, r1 = max(0, -dr), ROWS - max(0, dr)
                        c0, c1 = max(0, -dc), GRID - max(0, dc)
                        add(a_l[:, r0:r1, c0:c1], s_l[:, r0 + dr:r1 + dr, c0 + dc:c1 + dc], 3 * k + l)
                        dve.drain()
                        if (k, l) == (0, 1):
                            add(a_c[:, 0:NC - 1], s_c[:, 1:NC], 5)
                dve.drain().then_inc(conv_done, 1)

            def split_v(j, h):
                r = staged(("vN", j), h)
                dve.wait_ge(v_spilled, (h * JH + j) * 32)
                split(v_st_hi[:].rearrange("p s e -> p (s e)"), v_st_lo[:].rearrange("p s e -> p (s e)"),
                      tile[:, r]).then_inc(taken[r], 1)
                dve.drain().then_inc(v_split, 1)

            def split_x(j, h):
                dve.wait_ge(xc_done, h * JH + j + 1)
                n = USE[("vT", 3)]
                dve.wait_ge(full[n % SLOTS], h * USES + n // SLOTS + 1)
                split(xx_hi[:, j], xx_lo[:, j], xc[:, j % 2]).then_inc(x_split, 1)

            with dve.Fori(0, H // 2) as it:
                for hh in range(2):
                    h = it * 2 + hh
                    for j in range(JH):
                        staged(("xm", j), h)
                        split(xx_hi[:, j], xx_lo[:, j], xm[:, j]).then_inc(x_split, 1)
                    conv(0, h)
                    split_v(0, h)
                    conv(1, h)
                    split_v(1, h)
                    split_x(0, h)
                    conv(2, h)
                    split_v(2, h)
                    split_x(1, h)
                    conv(3, h)
                    split_v(3, h)
                    split_x(2, h)
                    split_x(3, h)
                    for j in range(JH):
                        r = staged(("q", j), h)
                        split(q_hi[:, j], q_lo[:, j], tile[:, r, NC:NT]).then_inc(taken[r], 1)
                        dve.drain().then_inc(qk_split, 1)
                    for j in range(JH):
                        r = staged(("k", j), h)
                        split(k_hi[:, j], k_lo[:, j], tile[:, r]).then_inc(taken[r], 1)
                        dve.drain().then_inc(qk_split, 1)

            dve.wait_ge(gate_rows, 64)
            v.scalar_tensor_tensor(out=g_a[:], in0=g_f[:], scalar=-1.0, in1=g_f[:], op0=ALU.mult,
                                   op1=ALU.max).then_inc(abs_f, 1)
            v.memset(g_z[:], 0.0)
            dve.wait_ge(soft, 2)
            v.scalar_tensor_tensor(out=g_f[:], in0=g_f[:], scalar=0.0, in1=g_t[:], op0=ALU.min,
                                   op1=ALU.subtract)
            dve.drain()

            def scan(dst, src, other, op1):
                v.tensor_tensor_scan(dst[:, 0], src[:, 0], other(0, slice(0, NT)), 0.0, op1, op1)
                back_c, back_l = slice(NC - 1, None, -1), slice(NT - 1, NC - 1, -1)
                v.tensor_tensor_scan(dst[:, 1, back_c], src[:, 1, back_c], other(1, back_c), 0.0,
                                     op1, op1)
                dve.drain()
                v.tensor_tensor_scan(dst[:, 1, back_l], src[:, 1, back_l], other(1, back_l), dst[:, 1, 0:1],
                                     op1, op1)
                dve.drain()

            scan(g_F, g_f, lambda d, s: g_z[:, s], ALU.add)
            v.tensor_tensor(g_g[:], g_i[:], g_F[:], ALU.subtract)
            dve.drain().then_inc(g_done, 1)
            scan(g_M, g_g, lambda d, s: g_g[:, d, s], ALU.max)
            v.tensor_tensor(g_F[:], g_F[:], g_M[:], ALU.add).then_inc(scans, 1)
            dve.wait_ge(gT_full, 1)
            v.tensor_copy(gcol[:].rearrange("p d s h -> p (d s h)"), psum[:, 0, 0:2 * ST * H]
                          ).then_inc(m_done, 1)

            def exponents(h):
                dve.wait_ge(gg_ready, h + 1)
                for d in range(2):
                    for j in range(TT):
                        v.tensor_scalar(dg[:, d, j], mb[:, d, tblk(j)], gcol[:, d, 2 + j, h:h + 1], 0.0,
                                        ALU.subtract, ALU.max)
                dve.drain().then_inc(dgx, 1)

            def diagonals(h):
                dve.wait_ge(dge, h + 1)
                for j in range(TT):
                    v.tensor_tensor(pb[:, 2 + j, tblk(j)], dg[:, 1, j], mask[:, 1], ALU.mult)
                    v.tensor_tensor(dg[:, 0, j], dg[:, 0, j], mask[:, 0], ALU.mult)
                dve.wait_ge(eb_done, h + 1)
                dve.wait_ge(s_landed, 16 * (h + 1))
                dve.drain()

            def products(h, s):
                n = NL if s < 2 else (s - 1) * P
                v.tensor_tensor(pb[:, s, 0:n], pb[:, s, 0:n], pf[:, s, 0:n], ALU.mult)
                dve.drain()
                t0 = 0 if s < 2 else (s - 1) * P
                if s >= 2:
                    v.tensor_tensor(pf[:, s, tblk(s - 2)], pf[:, s, tblk(s - 2)], dg[:, 0, s - 2], ALU.mult)
                if t0 < NL:
                    e = 5 * h + s
                    dve.wait_ge(ef_done, e + 1)
                    v.tensor_tensor(pf[:, s, t0:NL], pf[:, s, t0:NL], ef[:, e % 2, t0:NL], ALU.mult
                                    ).then_inc(ef_read, 1)

            def key_sums(h):
                dve.drain()
                for d, p_ in ((0, pf), (1, pb)):
                    tot = dg[:, d].rearrange("p j t -> p (j t)")
                    v.tensor_tensor(tot, p_[:, 0], p_[:, 1], ALU.add)
                dve.drain()
                for s in range(2, ST):
                    for d, p_ in ((0, pf), (1, pb)):
                        tot = dg[:, d].rearrange("p j t -> p (j t)")
                        sl = slice((s - 2) * P, NL) if d == 0 else slice(0, (s - 1) * P)
                        v.tensor_tensor(tot[:, sl], tot[:, sl], p_[:, s, sl], ALU.add)
                    dve.drain()
                dve.drain().then_inc(sums, 2)

            def normalise(h):
                for d in range(2):
                    dve.wait_ge(bc_full, 8 * h + 5 + d)
                    v.scalar_tensor_tensor(out=rr[:, d], in0=psum[:, 3, :], scalar=-1.0, in1=rr[:, d],
                                           op0=ALU.mult, op1=ALU.max)
                    dve.drain()
                    v.tensor_tensor(rr[:, d], psum[:, 3, :], rr[:, d], ALU.max).then_inc(bc_free, 1)
                dve.drain()
                v.reciprocal(rr[:], rr[:])
                dve.drain()
                for s in range(ST):
                    nb = NL if s < 2 else (s - 1) * P
                    t0 = 0 if s < 2 else (s - 2) * P
                    v.tensor_tensor(pb[:, s, 0:nb], pb[:, s, 0:nb], rr[:, 1, 0:nb], ALU.mult)
                    v.tensor_tensor(pf[:, s, t0:NL], pf[:, s, t0:NL], rr[:, 0, t0:NL], ALU.mult)
                dve.drain()
                v.tensor_tensor(pf[:, 0:2], pf[:, 0:2], pb[:, 0:2], ALU.add)
                for j in range(TT):
                    v.tensor_tensor(pf[:, 2 + j, tblk(j)], pf[:, 2 + j, tblk(j)], pb[:, 2 + j, tblk(j)],
                                    ALU.add)
                dve.drain()
                if h:
                    dve.wait_ge(pv_full[1], 2 * h)
                for lo_part in range(2):
                    for s in range(ST):
                        for src, sl in ((pb, slice(0, max(s - 2, 0) * P)), (pf, slice(max(s - 2, 0) * P, NL))):
                            if sl.start == sl.stop:
                                continue
                            if lo_part:
                                v.tensor_tensor(p_lo[:, s, sl], src[:, s, sl], p_hi[:, s, sl].bitcast(F32),
                                                ALU.subtract)
                            else:
                                v.tensor_copy(p_hi[:, s, sl], src[:, s, sl])
                    dve.drain()
                dve.drain().then_inc(p_split, 1)

            def columns(dst, src):
                for k in range(src.shape[-1] // P):
                    v.tensor_tensor_reduce(out=junk[:], in0=src[:, tblk(k)], in1=ident[:], scale=1.0,
                                           scalar=0.0, op0=ALU.mult, op1=ALU.add,
                                           accum_out=dst[:, k:k + 1])
                    dve.drain()

            def add_y(i, half, first):
                src = psum[:, 4 + i, :]
                dst = y_acc[:, i, tblk(half, 512)]
                if first:
                    v.tensor_copy(dst, src).then_inc(y_free[i], 1)
                else:
                    v.tensor_tensor(dst, dst, src, ALU.add).then_inc(y_free[i], 1)

            exponents(0)
            diagonals(0)
            for s in range(ST):
                products(0, s)
            key_sums(0)
            normalise(0)
            for h in range(H):
                for i in range(TT):
                    dve.wait_ge(pv_free[i % 2], 2 * h + i // 2 + 1)
                    v.bn_stats(stat[:, i, 0], hn[:, i])
                dve.drain()
                for i in range(TT):
                    v.bn_aggr(mv[:, i], stat[:, i, 0])
                dve.drain()
                v.tensor_scalar(std[:, 0:TT], mv[:, 0:TT, 1], EPS, None, ALU.add).then_inc(h_var, 1)
                if ADA0[h] in (3, 4):
                    for i in range(2):
                        dve.wait_ge(bc_full, 8 * h + 7 + i)
                        columns(adac[:, SH2_0 if ADA0[h] == 3 else SC2_0, 4 * i:4 * i + 4], psum[:, 3, :])
                        dve.drain().then_inc(bc_free, 1)
                dve.wait_ge(h_std, h + 1)
                rstd_nmr(TT)
                dve.drain()
                for i in range(TT):
                    v.tensor_scalar(hn[:, i], hn[:, i], rstd[:, i:i + 1], nmr[:, i:i + 1], ALU.mult, ALU.add)
                dve.drain().then_inc(h_norm, 1)
                for e in range(JH):
                    n = h * JH + e
                    dve.wait_ge(tr_full, n + 1)
                    dve.wait_ge(z_landed[n % 2], 32 * (n // 2 + 1))
                    v.scalar_tensor_tensor(out=sxt[:, n % 2], in0=psum[:, 2, :], scalar=cols[:, 160 + n:161 + n],
                                           in1=sxt[:, n % 2], op0=ALU.mult, op1=ALU.add).then_inc(tr_free, 1)
                    dve.drain()
                    v.tensor_tensor(zt[:, n % 2], zt[:, n % 2], sxt[:, n % 2], ALU.mult)
                    dve.drain()
                    split(u_hi[:, e], u_lo[:, e], zt[:, n % 2]).then_inc(zu_done, 1)
                dve.drain().then_inc(u_done, 1)
                if h + 1 < H:
                    exponents(h + 1)
                    diagonals(h + 1)
                for n in range(2 * TT):
                    half, i = n // TT, n % TT
                    dve.wait_ge(y_full[i], 2 * h + half + 1)
                    add_y(i, half, h == 0)
                    if h + 1 < H and n < ST:
                        products(h + 1, n)
                if h + 1 < H:
                    key_sums(h + 1)
                    normalise(h + 1)

            def boundary(b):
                g_row = [g1_row[:], g2_row[:], rows[:, 2], g2_row[:]][b]
                old = x_res if b == 0 else x_nat
                dve.drain()
                for i in range(TT):
                    v.tensor_tensor(y_acc[:, i], y_acc[:, i], g_row, ALU.mult)
                if b == 0:
                    dve.wait_ge(res_landed, 16)
                dve.drain()
                for i in range(TT):
                    v.scalar_tensor_tensor(out=y_acc[:, i], in0=old[:, i], scalar=ALPHA, in1=y_acc[:, i],
                                           op0=ALU.mult, op1=ALU.add)
                dve.drain()
                for i in range(TT):
                    for half in range(2):
                        v.bn_stats(stat[:, i, half], y_acc[:, i, tblk(half, 512)])
                finish_stats(TT).then_inc(b_var, 1)
                dve.wait_ge(b_std, 1 if b == 0 else 2 * b + 1)
                rstd_nmr(TT)
                dve.drain().then_inc(b_norm_in, 1)
                dve.wait_ge(pgb_landed, 32 * (b + 1))
                for i in range(TT):
                    dve.wait_ge(b_norm, b * TT + i + 1)
                    v.tensor_tensor(y_acc[:, i], y_acc[:, i], pg[:], ALU.mult)
                    dve.drain()
                    v.tensor_tensor(x_nat[:, i], y_acc[:, i], pbb[:], ALU.add).then_inc(b_x, 1)
                if b == 3:
                    return
                dve.drain()
                for i in range(TT):
                    for half in range(2):
                        v.bn_stats(stat[:, i, half], x_nat[:, i, tblk(half, 512)])
                finish_stats(TT).then_inc(b_var, 1)
                if b == 1:
                    for dst, r in ((SH1_1, 0), (SC1_1, 1), (SH2_1, 3)):
                        columns(adac[:, dst], rows[:, r])
                sc = MODS[b][1]
                v.tensor_scalar(adac[:, sc], adac[:, sc], 1.0, None, ALU.add).then_inc(b_cols, 1)
                dve.wait_ge(b_std, 2 * b + 2)
                rstd_nmr(TT)
                dve.drain().then_inc(b_norm_in, 1)
                for k in range(KD):
                    r = k % 2
                    dve.wait_ge(b_tile[r], 4 * b + k // 2 + 1)
                    split(hh_hi[:, k], hh_lo[:, k], btile[:, r]).then_inc(b_split[r], 1)
                dve.wait_ge(b_turned, b + 1)
                v.memset(y_acc[:], 0.0)
                dve.drain()

            def mlp(layer, y0):
                with dve.Fori(0, GROUPS) as gr:
                    for u in range(4):
                        for c2 in range(2):
                            dve.wait_ge(a_sq[c2], gr * 4 + layer * 16 + u + 1)
                            split(ff_hi[:, 2 * u + c2], ff_lo[:, 2 * u + c2], sq[:, c2]
                                  ).then_inc(a_split[c2], 1)
                    for u in range(4):
                        for i in range(TT):
                            dve.wait_ge(y_full[i], gr * 4 + y0 + u + 1)
                            add_y(i, u // 2, False)

            boundary(0)
            mlp(0, 8)
            boundary(1)
            for n in range(16):
                dve.wait_ge(f_tile[n % 2], n // 2 + 1)
                split(a_hi[:, n % 4, n // 4], a_lo[:, n % 4, n // 4], ftile[n % 2][:]).then_inc(f_split[n % 2], 1)
            for n in range(16, 24):
                dve.wait_ge(f_tile[n % 2], n // 2 + 1)
                split(hh_hi[:, n - 16], hh_lo[:, n - 16], ftile[n % 2][:]).then_inc(f_split[n % 2], 1)
            for i in range(2):
                dve.wait_ge(c_full, 2 * GROUPS + i + 1)
                columns(adac[:, SC2_1, 4 * i:4 * i + 4], psum[:, 2, :])
                dve.drain().then_inc(c_row, 1)
            for u in range(4):
                for i in range(TT):
                    dve.wait_ge(y_full[i], 24 + u + 1)
                    add_y(i, u // 2, False)
            boundary(2)
            mlp(1, 28)
            boundary(3)


def dft_tables():
    ch = np.outer(np.arange(FG), np.arange(FG)) % FG * (2 * np.pi / FG)
    chan = np.concatenate([np.cos(ch), np.sin(ch)], axis=1)
    sq = np.outer(np.arange(NL), np.arange(NL)) % NL * (2 * np.pi / NL)
    scale = 1.0 / np.sqrt(NL * FG)
    units = np.zeros((3, P, UNIT))
    units[0, :, 0:1024] = chan.reshape(2, P, 512).transpose(1, 0, 2).reshape(P, 1024)
    for n, t in ((1, np.cos(sq) * scale), (2, -np.sin(sq) * scale)):
        units[n] = t.reshape(4, P, 512).transpose(1, 0, 2).reshape(P, UNIT)
    return units.astype(np.float32)


_INS = ["x", "c", "ctx", "c_ctx", "ada_w", "ada_b", "post_g", "post_b", "m_w_in", "m_w_conv", "m_b_conv",
        "m_w_q", "m_w_k", "m_w_v", "m_w_gate", "m_b_gate", "m_gn_w", "m_skip", "m_w_out", "f_w_out",
        "mlp_w1", "mlp_w2"]


def kernel(**inputs):
    import concourse.bacc as bacc
    from concourse.bass_utils import run_bass_kernel_spmd

    nc = bacc.Bacc("TRN2", target_bir_lowering=False, num_devices=1)
    arrays = {f"in_{name}": np.ascontiguousarray(inputs[name]) for name in _INS}
    arrays["dft"] = dft_tables()
    args = [nc.dram_tensor(name, a.shape, mybir.dt.from_np(a.dtype), kind="ExternalInput").ap()
            for name, a in arrays.items()]
    out = nc.dram_tensor("out", (1, NL, D), F32, kind="ExternalOutput").ap()
    hybrid_block(nc, *args, out)
    r = run_bass_kernel_spmd(nc, [arrays], core_ids=[0])
    return r.results[0]["out"]
```

```python
from contextlib import ExitStack

import numpy as np

import concourse.bass as bass
from concourse import mybir

F32 = mybir.dt.float32
F32R = mybir.dt.float32r
ALU = mybir.AluOpType
ACT = mybir.ActivationFunctionType

P = 128
D = 1024
NL, NC = 512, 256
NT = NL + NC
KD = D // P
DI = 2048
H, DH = 4, 512
JH = DH // P
ST = NT // P
TT = NL // P
DFF = 4096
GRID = 64
ROWS = NL // GRID
NG = 16
GROUPS = 4
FT = DFF // P // GROUPS
FG = 256
ALPHA = float(4 ** 0.25)
EPS = 1e-5
K_SCALE = float(DH ** -0.5)
UNIT = 2048
KB = 1024

SH1, SC1, G1, SH2, SC2, G2 = range(6)


def vec(layer, v):
    return (layer * 6 + v) * KD


ADA0 = [SH2, SC2, G1, G2]
MODS = [(vec(0, SH2), vec(0, SC2)), (vec(1, SH1), vec(1, SC1)), (vec(1, SH2), vec(1, SC2))]
GATE = [vec(0, G1), vec(0, G2), vec(1, G1), vec(1, G2)]

HEAD = ([("xm", j) for j in range(4)] + [("ada", 0), ("vT", 0), ("vT", 1), ("vN", 0), ("vT", 2), ("vN", 1),
        ("vT", 3), ("vN", 2), ("z", 0), ("vN", 3), ("z", 1), ("z", 2), ("z", 3), ("ada", 1)]
        + [("q", j) for j in range(4)] + [("k", j) for j in range(4)]
        + [("S", 0), ("ada", 2)] + [("S", j) for j in range(1, 6)])
STREAM = [0, None, 1, None, 2, None, 3, 4, None, 5, None, 6, None]
ADA_UNITS = STREAM.count(None)
SLOTS = 3
USES = len(HEAD) // SLOTS
USE = {what: n for n, what in enumerate(HEAD)}
READERS = {"xm": (), "ada": (), "vT": ("turn",), "vN": ("dve",), "z": ("dma",), "S": ("dma",),
           "q": ("pe", "dve"), "k": ("pe", "dve")}


def reads_before(reader, n):
    return sum(reader in READERS[HEAD[m][0]] for m in range(n % SLOTS, n + 1, SLOTS))


def reads_per_head(reader, slot):
    return reads_before(reader, len(HEAD) - SLOTS + slot)


STREAM_P2 = [("w_out", 0, 0), ("w_out", 0, 1), ("ada", 0, 0), ("ada", 0, 1)]
for _h in range(H):
    STREAM_P2 += [("ada", _h, 2), ("ada", _h, 3)]
    if _h + 1 < H:
        STREAM_P2 += [("ada", _h + 1, 0), ("ada", _h + 1, 1)]
    if _h:
        STREAM_P2 += [("w_out", _h, 0), ("w_out", _h, 1)]
RAW_P1, RAW_P2 = len(STREAM) * H, 6 * H
RAW0_P2 = RAW_P1
RAW0_MLP0 = RAW0_P2 + RAW_P2
RAW0_F = RAW0_MLP0 + 8 * GROUPS
RAW0_MLP1 = RAW0_F + 3 + 4
SPLIT0_P2 = 7 * H
SPLIT0_MLP0 = SPLIT0_P2 + 2 * H
SPLIT0_F = SPLIT0_MLP0 + 8 * GROUPS
SPLIT0_MLP1 = SPLIT0_F + 7
ADA0_P2 = ADA_UNITS * H


BLOCKS = [8, 8, 5, 5, 5, 5]
START = [sum(BLOCKS[:s]) for s in range(ST)]
BACK, FORTH = 0, 1
NOT_SEEN = 200.0


def pblock(d, s, i):
    return i + d * (4 if s < 2 else 1)


def key_tiles(d, i):
    return [0, 1] + (list(range(2 + i, ST)) if d == BACK else list(range(2, 3 + i)))


def bc_use(what, h, i=0):
    if what == "M" and h == 0:
        return 1 + i
    if what == "M":
        return 2 + 5 * (h - 1) + 3 + i
    last = 2 if h == H - 1 else 0
    return 2 + 5 * h + {"ada": 1 + i * (4 - last), "den": 2}[what]


def hybrid_block(nc, x, c, ctx, c_ctx, ada_w, ada_b, post_g, post_b, m_w_in, m_w_conv, m_b_conv, m_w_q,
                 m_w_k, m_w_v, m_w_gate, m_b_gate, m_gn_w, m_skip, m_w_out, f_w_out, mlp_w1, mlp_w2,
                 dft, out):
    es = ExitStack()
    with es:
        base = 16512
        region = base + 54 * KB

        def at(name, shape, off_kb, dt=F32):
            return nc.alloc_sbuf_tensor_at(name, shape, dt, offset=int(region + off_kb * KB))

        def fixed(name, shape, off, dt=F32):
            return nc.alloc_sbuf_tensor_at(name, shape, dt, offset=base + off)

        def sem(name):
            return es.enter_context(nc.semaphore(name))

        def sems(name, n):
            return [sem(f"{name}{i}") for i in range(n)]

        raw = fixed("raw", [P, 2, UNIT], 0)
        w_hi = fixed("w_hi", [P, 2, UNIT], 16 * KB, F32R)
        w_lo = fixed("w_lo", [P, 2, UNIT], 32 * KB, F32R)
        o = [48 * KB]

        def const(name, shape):
            n = 4 * int(np.prod(shape[1:]))
            o[0] += (n + 31) // 32 * 32
            assert o[0] <= 54 * KB
            return fixed(name, shape, o[0] - (n + 31) // 32 * 32)

        ident = const("ident", [P, P])
        ones = const("ones", [P, P])
        o[0] += 32
        ones_r = fixed("ones_r", [P, 2], o[0] - 32, F32R)
        exp_m = const("exp_m", [P, 2, TT, H])
        den = const("den", [P, 2, TT])
        dena = const("dena", [P, 2, TT])
        asum = const("asum", [P, 2, 256])

        cols = const("cols", [P, 288])
        cvec = const("cvec", [P, 2, KD])
        svec = const("svec", [P, 2, KD])
        mod0 = const("mod0", [P, 2 * KD, 2])
        adac = const("adac", [P, 12 * KD])
        stat = const("stat", [P, 6, 2, 6])
        mv = const("mv", [P, 6, 2])
        std = const("std", [P, 6])
        rstd = const("rstd", [P, 6])
        nmr = const("nmr", [P, 6])
        gcol = const("gcol", [P, 2, ST, H])

        x_in = at("x_in", [P, TT, D], 48)
        c_in = at("c_in", [P, 2, D], 64)
        ada_in = at("ada_in", [P, 4, KD, 512], 72)
        modrow = at("modrow", [2, 2 * D], 24)
        colrow = at("colrow", [P, 3, P], 32)
        ht_hi = at("ht_hi", [P, KD, NT], 0, F32R)
        ht_lo = at("ht_lo", [P, KD, NT], 24, F32R)
        xx_hi = at("xx_hi", [P, JH, NT], 48, F32R)
        xx_lo = at("xx_lo", [P, JH, NT], 60, F32R)
        xm = at("xm", [P, JH, NT], 72)
        q_hi = at("q_hi", [P, JH, NL], 84, F32R)
        q_lo = at("q_lo", [P, JH, NL], 92, F32R)
        k_hi = at("k_hi", [P, JH, NT], 100, F32R)
        k_lo = at("k_lo", [P, JH, NT], 112, F32R)
        tile = at("tile", [P, SLOTS, NT], 124)
        v_st_hi = at("v_st_hi", [P, ST, P], 133, F32R)
        v_st_lo = at("v_st_lo", [P, ST, P], 136, F32R)
        xc = at("xc", [P, 2, NT], 139)
        sx_st = at("sx_st", [P, 2, NL], 145)
        wg = at("wg", [P, 2, 3, JH, NG], 149)
        bg = at("bg", [1, NG], 151)
        pre = at("pre", [NG, NT], 48)
        g_i = at("g_i", [H, 2, NT], 52)
        g_f = at("g_f", [H, 2, NT], 58)
        g_t = at("g_t", [H, 2, NT], 64)
        g_F = at("g_F", [H, 2, NT], 70)
        g_g = at("g_g", [H, 2, NT], 76)
        g_M = at("g_M", [H, 2, NT], 82)
        g_z = at("g_z", [H, NT], 88)
        g_a = at("g_a", [H, 2, NT], 92)
        m_rows = at("m_rows", [P, NL], 144)
        mb = at("mb", [P, 2, NL], 146)
        sel = at("sel", [P, H, P], 150)
        mask = at("mask", [P, 2, P], 152)
        y_acc = at("y_acc", [P, TT, D], 0)
        u_hi = at("u_hi", [P, JH, NL], 16, F32R)
        u_lo = at("u_lo", [P, JH, NL], 24, F32R)
        gate_diag = at("gate_diag", [P, KD, P], 32)
        v_hi = at("v_hi", [P, ST, DH], 44, F32R)
        v_lo = at("v_lo", [P, ST, DH], 56, F32R)
        s_in = at("s_in", [P, ST, NL], 68)
        p_hi = at("p_hi", [P, sum(BLOCKS), P], 80, F32R)
        p_lo = at("p_lo", [P, sum(BLOCKS), P], 98, F32R)
        wt = [at(f"wt{n}", [P, 8, P], 32 + 4 * n) for n in range(3)]
        hn = at("hn", [P, 2, TT, DH], 116)
        u3_hi = at("u3_hi", [P, JH, NL], 108, F32R)
        u3_lo = at("u3_lo", [P, JH, NL], 98, F32R)
        zt = at("zt", [P, 3, NL], 132)
        sxt = at("sxt", [P, 3, NL], 138)
        x_nat = at("x_nat", [P, TT, D], 16)
        x_res = at("x_res", [P, TT, D], 80)
        hh_hi = at("hh_hi", [P, KD, NL], 44, F32R)
        hh_lo = at("hh_lo", [P, KD, NL], 60, F32R)
        ff_hi = at("ff_hi", [P, FT, NL], 76, F32R)
        ff_lo = at("ff_lo", [P, FT, NL], 92, F32R)
        relu = at("relu", [P, 2, NL], 108)
        sq = at("sq", [P, 2, NL], 112)
        btile = at("btile", [P, 2, NL], 116)
        pg = at("pg", [P, D], 120)
        pbb = at("pbb", [P, D], 124)

        a_hi = at("a_hi", [P, TT, 4, 512], 76, F32R)
        a_lo = at("a_lo", [P, TT, 4, 512], 108, F32R)
        ftile = [at("ftile0", [P, NL], 148), at("ftile1", [P, NL], 150)]

        psum = es.enter_context(nc.psum_tensor("psum", [P, 8, 512], F32))

        v_hi_d = nc.dram_tensor("v_hi_d", [H, P, ST, DH], F32, kind="Internal").ap()
        v_lo_d = nc.dram_tensor("v_lo_d", [H, P, ST, DH], F32, kind="Internal").ap()
        s_d = nc.dram_tensor("s_d", [H, ST, P, NL], F32, kind="Internal").ap()
        z_d = nc.dram_tensor("z_d", [DI // P, P, NL], F32, kind="Internal").ap()
        sx_d = nc.dram_tensor("sx_d", [DI // P, P, NL], F32, kind="Internal").ap()

        raw_landed = sems("raw_landed", 2)
        prepared = sem("prepared")
        w_ready = sem("w_ready")
        w_begun = sem("w_begun")
        pool_step = sem("pool_step")
        ada_ready = sem("ada_ready")
        ada_used = sem("ada_used")
        sel_ready = sem("sel_ready")
        consts = sem("consts")
        in_landed = sems("in_landed", 4)
        ada0_landed = sems("ada0_landed", 4)
        silu_c = sem("silu_c")
        mod_sum = sem("mod_sum")
        modrow_done = sem("modrow_done")
        mod_T = sem("mod_T")
        col_T = sem("col_T")
        cols_done = sem("cols_done")
        mod_done = sem("mod_done")
        var_done = sem("var_done")
        std_done = sem("std_done")
        xhat_done = sem("xhat_done")
        x0_full = sems("x0_full", 3)
        x0_tile = sems("x0_tile", 3)
        x0_split = sems("x0_split", 3)
        ht_ready = sem("ht_ready")
        full = sems("full", SLOTS)
        evac = sems("evac", SLOTS)
        aux = sems("aux", SLOTS)
        taken = sems("taken", SLOTS)
        spilled = sems("spilled", SLOTS)
        x_split = sem("x_split")
        qk_split = sem("qk_split")
        conv_done = sem("conv_done")
        xc_done = sem("xc_done")
        sx_done = sem("sx_done")
        sx_spilled = sems("sx_spilled", 2)
        v_split = sem("v_split")
        v_spilled = sem("v_spilled")
        wg_landed = sems("wg_landed", 2)
        wg_used = sem("wg_used")
        bg_landed = sem("bg_landed")
        gates_full = sem("gates_full")
        scans = sem("scans")
        m_landed = sem("m_landed")
        pre_done = sem("pre_done")
        gate_rows = sem("gate_rows")
        abs_f = sem("abs_f")
        soft = sem("soft")
        g_done = sem("g_done")
        gT_full = sem("gT_full")
        m_done = sem("m_done")
        s_landed = sem("s_landed")
        v_landed = sem("v_landed")
        z_landed = sems("z_landed", 3)
        bc_full = sem("bc_full")
        bc_free = sem("bc_free")
        mT_full = sem("mT_full")
        exp_m_done = sem("exp_m_done")
        mb_done = sem("mb_done")
        diag_in = sem("diag_in")
        w_exp = sem("w_exp")
        p_hi_done = sem("p_hi_done")
        p_ready = sem("p_ready")
        den_done = sem("den_done")
        forth_done = sem("forth_done")
        h_rs = sem("h_rs")
        pv_full = sems("pv_full", 2)
        back_done = sem("back_done")
        h_var = sem("h_var")
        h_std = sem("h_std")
        h_norm = sem("h_norm")
        tr_full = sem("tr_full")
        tr_free = sem("tr_free")
        u_done = sem("u_done")
        zu_done = sem("zu_done")
        y_full = sems("y_full", TT)
        y_free = sems("y_free", TT)
        res_landed = sem("res_landed")
        pgb_landed = sem("pgb_landed")
        b_var = sem("b_var")
        b_std = sem("b_std")
        b_stat = sem("b_stat")
        b_norm_in = sem("b_norm_in")
        b_turned = sem("b_turned")
        b_cols = sem("b_cols")
        gate_in = sem("gate_in")
        gate_full = sem("gate_full")
        b_norm = sem("b_norm")
        b_x = sem("b_x")
        b_xhat = sem("b_xhat")
        b_full = sems("b_full", 2)
        b_tile = sems("b_tile", 2)
        b_split = sems("b_split", 2)
        y_zero = sem("y_zero")
        a_full = sems("a_full", 2)
        a_relu = sems("a_relu", 2)
        a_sq = sems("a_sq", 2)
        a_split = sems("a_split", 2)

        f_full = sems("f_full", 2)
        f_tile = sems("f_tile", 2)
        f_split = sems("f_split", 2)
        stored = sem("stored")

        def mul3(pe, dst, lh, ll, rh, rl, first, last, begun=None):
            mm = pe.matmul(dst, lh, rh, start=first, stop=False)
            if begun is not None:
                mm.then_inc(begun, 1)
            pe.matmul(dst, lh, rl, start=False, stop=False)
            return pe.matmul(dst, ll, rh, start=False, stop=last)

        def tblk(i, n=P):
            return slice(i * n, (i + 1) * n)

        def u_of(h):
            return (u_hi, u_lo) if h < H - 1 else (u3_hi, u3_lo)

        block = es.enter_context(nc.Block())

        @block.sync
        def _(sp):
            sp.dma_start(cvec[:, 0], c.rearrange("a (p k) -> p (a k)", k=KD)).then_inc(in_landed[0], 16)
            sp.dma_start(cvec[:, 1], c_ctx.rearrange("(p k) -> p k", k=KD)).then_inc(in_landed[0], 16)
            for n in range(4):
                sp.dma_start(ada_in[:, n], ada_w[0].rearrange("(p k) n -> p k n", k=KD)[:, :, tblk(n, 512)]
                             ).then_inc(ada0_landed[n], 16)
            sp.dma_start(colrow[:, 0], m_w_conv.rearrange("a k l (j p) -> (a k l j) p", p=P)[0:128]
                         ).then_inc(in_landed[3], 16)
            sp.dma_start(colrow[0:16, 1], m_w_conv.rearrange("a k l (j p) -> (a k l j) p", p=P)[128:144]
                         ).then_inc(in_landed[3], 16)
            for n, v in enumerate((m_b_conv, m_gn_w, m_skip)):
                sp.dma_start(colrow[16 + 16 * n:32 + 16 * n, 1], v.rearrange("a (j p) -> (a j) p", p=P)
                             ).then_inc(in_landed[3], 16)
            sp.dma_start(colrow[0:96, 2], ada_b.rearrange("a (j p) -> (a j) p", p=P)
                         ).then_inc(in_landed[3], 16)
            sp.dma_start(bg[:, :], m_b_gate).then_inc(bg_landed, 16)

            def raw_unit(n, slot, src, free=True):
                if free:
                    sp.wait_ge(prepared, n - 1)
                sp.dma_start(raw[:, slot], src).then_inc(raw_landed[slot], 16)

            def ada_unit(layer, col):
                return ada_w[layer].rearrange("(p k) n -> p k n", k=KD)[:, :, bass.ds(col, 256)]

            w_in_v = m_w_in[0].rearrange("(k p) n -> p k n", p=P)

            def head_units(h, hh, n, lead=False):
                def cols_of(start):
                    return w_in_v[:, :, bass.ds(start, 256)]

                def square(w):
                    return w[0][bass.ds(h, 1)].rearrange("a (k p) n -> p (a k) n", p=P)

                sp.wait_ge(wg_used, h + 1)
                for m in range(3):
                    sp.dma_start(wg[:, hh, m], m_w_gate[0, m].rearrange("(j p) n -> p j n", p=P)
                                 [:, bass.ds(h * JH, JH)]).then_inc(wg_landed[hh], 16)
                src = [cols_of(h * DH), cols_of(h * DH + 256), square(m_w_v), cols_of(h * DH + DI),
                       cols_of(h * DH + DI + 256), square(m_w_q), square(m_w_k)]
                for u, what in enumerate(STREAM):
                    a_ = STREAM[:u].count(None)
                    raw_unit(n + u, (len(STREAM) * hh + u) % 2,
                             ada_unit(1, h * (ADA_UNITS * 256) + 256 * a_) if what is None else src[what])

            with sp.Fori(0, H // 2) as it:
                for hh in range(2):
                    head_units(it * 2 + hh, hh, it * (2 * len(STREAM)) + len(STREAM) * hh + 2)

            w_out_v = m_w_out[0].rearrange("(k p) n -> p k n", p=P)
            for u, (what, h, i) in enumerate(STREAM_P2):
                n = RAW0_P2 + u
                raw_unit(n + 2, n % 2, ada_unit(0, ADA0[h] * D + i * 256) if what == "ada"
                         else w_out_v[:, tblk(h, JH), tblk(i, 512)])

            def mlp_units(layer, n0):
                w1 = mlp_w1[layer].rearrange("(k p) n -> p k n", p=P)
                w2 = mlp_w2[layer].rearrange("(k p) n -> p k n", p=P)
                with sp.Fori(0, GROUPS) as g:
                    n = g * 8 + n0 + 2
                    for u in range(4):
                        raw_unit(n + u, (n0 + u) % 2, w1[:, :, bass.ds(g * 1024 + u * 256, 256)])
                    n = n + 4
                    for u in range(4):
                        raw_unit(n + u, (n0 + u) % 2,
                                 w2[:, bass.ds(g * FT + (u % 2) * 4, 4), tblk(u // 2, 512)])

            mlp_units(0, RAW0_MLP0)

            n = RAW0_F
            for u in range(3):
                raw_unit(n + 2, n % 2, dft[u])
                n += 1
            f_v = f_w_out[0].rearrange("(k p) n -> p k n", p=P)
            for u in range(4):
                raw_unit(n + 2, n % 2, f_v[:, tblk(u % 2, 4), tblk(u // 2, 512)])
                n += 1
            mlp_units(1, RAW0_MLP1)

            out_v = out.rearrange("a (i p) d -> p (a i) d", p=P)
            for i in range(TT):
                sp.wait_ge(b_x, 3 * TT + i + 1)
                sp.dma_start(out_v[:, i], x_nat[:, i]).then_inc(stored, 16)
            sp.wait_ge(stored, 16 * TT)

        @block.gpsimd
        def _(pool):
            g = nc.gpsimd
            g.memset(ident[:], 0.0)
            g.memset(ones[:], 1.0)
            pool.drain()
            g.tensor_scalar(ones_r[:], ones[:, 0:2], 1.0, 0.0, ALU.mult, ALU.add)
            pool.drain()
            g.affine_select(out=ident[:], in_=ident[:], compare_op=ALU.not_equal, fill=1.0, base=0,
                            pattern=[[-1, P]], channel_multiplier=1)

            pool.drain().then_inc(consts, 1)
            pool.wait_ge(consts, 1)
            pool.sem_inc(prepared, 2)
            pool.sem_inc(wg_used, 2)
            pool.sem_inc(ada_used, 2)
            pool.wait_ge(silu_c, 1)

            def split_unit(n, slot, m, wslot, begun=True):
                pool.wait_ge(raw_landed[slot], n)
                if begun:
                    pool.wait_ge(w_begun, m)
                pool.sem_inc(pool_step, 1)
                g.tensor_scalar(w_hi[:, wslot], raw[:, slot], 1.0, 0.0, ALU.mult, ALU.add)
                pool.drain()
                g.tensor_tensor(w_lo[:, wslot], raw[:, slot], w_hi[:, wslot].bitcast(F32), ALU.subtract)
                pool.drain().then_inc(w_ready, 1)
                pool.sem_inc(prepared, 1)

            def ada_unit(landed, slot, par, used):
                pool.wait_ge(raw_landed[slot], landed)
                pool.wait_ge(ada_used, used)
                pool.sem_inc(pool_step, 1)
                part = raw[:, slot].rearrange("p (k n) -> p k n", k=KD)
                g.tensor_tensor(part, part, svec[:, 0].unsqueeze(2).to_broadcast([P, KD, 256]), ALU.mult)
                pool.drain()
                g.tensor_tensor(part[:, 0:4], part[:, 0:4], part[:, 4:8], ALU.add)
                pool.drain()
                g.tensor_tensor(part[:, 0:2], part[:, 0:2], part[:, 2:4], ALU.add)
                pool.drain()
                g.tensor_tensor(asum[:, par], part[:, 0], part[:, 1], ALU.add)
                pool.drain().then_inc(ada_ready, 1)
                pool.sem_inc(prepared, 1)

            with pool.Fori(0, H // 2) as it:
                for u in range(2 * len(STREAM)):
                    what = STREAM[u % len(STREAM)]
                    landed = it * (len(STREAM) * 16) + 16 * (u // 2 + 1)
                    a_ = u // len(STREAM) * ADA_UNITS + STREAM[:u % len(STREAM)].count(None)
                    if what is None:
                        ada_unit(landed, u % 2, a_ % 2, it * (2 * ADA_UNITS) + a_ + 1)
                    else:
                        m = u // len(STREAM) * 7 + what
                        split_unit(landed, u % 2, it * 14 + m, m % 2)

            pool.wait_ge(gates_full, 1)
            g.memset(sel[:], 0.0)
            g.memset(mask[:], 0.0)
            pool.drain()
            g.affine_select(out=mask[:, BACK], in_=mask[:, BACK], compare_op=ALU.is_ge, fill=NOT_SEEN,
                            base=0, pattern=[[-1, P]], channel_multiplier=1)
            g.affine_select(out=mask[:, FORTH], in_=mask[:, FORTH], compare_op=ALU.is_ge, fill=NOT_SEEN,
                            base=0, pattern=[[1, P]], channel_multiplier=-1)
            for q in range(2):
                pool.drain()
                g.affine_select(out=sel[32 * q:32 * q + 32], in_=sel[32 * q:32 * q + 32],
                                compare_op=ALU.not_equal, fill=1.0, base=0,
                                pattern=[[-1, H], [0, P]], channel_multiplier=1)
            pool.drain().then_inc(sel_ready, 1)

            def head_ada(h, i):
                for u in range(2 * i, 2 * i + 2):
                    n = RAW0_P2 + STREAM_P2.index(("ada", h, u))
                    ada_unit(16 * (n // 2 + 1), n % 2, u % 2, ADA0_P2 + 4 * h + u + 1)

            def head_w_out(h):
                for half in range(2):
                    n = RAW0_P2 + STREAM_P2.index(("w_out", h, half))
                    m = SPLIT0_P2 + 2 * h + half
                    if h:
                        pool.wait_ge(y_full[TT - 1], 2 * (h - 1) + half + 1)
                    split_unit(16 * (n // 2 + 1), n % 2, m, m % 2, False)

            def products_lo(h):
                for s in range(ST):
                    n = ST * h + s
                    part = slice(START[s], START[s] + BLOCKS[s])
                    pool.wait_ge(p_hi_done, n + 1)
                    g.tensor_tensor(p_lo[:, part], wt[n % 3][:, 0:BLOCKS[s]], p_hi[:, part].bitcast(F32),
                                    ALU.subtract)
                    pool.drain().then_inc(p_ready, 1)

            head_w_out(0)
            head_ada(0, 0)
            products_lo(0)
            for h in range(H):
                head_ada(h, 1)
                if h + 1 < H:
                    products_lo(h + 1)
                    head_ada(h + 1, 0)
                if h:
                    head_w_out(h)

            def mlp(n0, m0):
                with pool.Fori(0, GROUPS) as gr:
                    for u in range(8):
                        split_unit(gr * 64 + 16 * ((n0 + u) // 2 + 1), (n0 + u) % 2, gr * 8 + m0 + u,
                                   (m0 + u) % 2)

            mlp(RAW0_MLP0, SPLIT0_MLP0)
            n, m = RAW0_F, SPLIT0_F
            for u in range(3):
                split_unit(16 * (n // 2 + 1), n % 2, m, m % 2)
                n += 1
                m += 1
            for u in range(4):
                split_unit(16 * (n // 2 + 1), n % 2, m, m % 2)
                n += 1
                m += 1
            mlp(RAW0_MLP1, SPLIT0_MLP1)

        @block.tensor
        def _(pe):
            pe.wait_ge(consts, 1)
            pe.wait_ge(in_landed[3], 96)
            pe.transpose(psum[:, 7, 0:128], colrow[:, 0], ident[:])
            pe.transpose(psum[:, 7, 128:192], colrow[0:64, 1], ident[0:64, 0:64])
            pe.transpose(psum[:, 7, 192:288], colrow[0:96, 2], ident[0:96, 0:96]).then_inc(col_T, 1)
            pe.wait_ge(silu_c, 1)
            for n in range(4):
                pe.wait_ge(ada0_landed[n], 16)
                for k in range(KD):
                    mm = pe.matmul(psum[0:2, n, :], svec[:, :, k], ada_in[:, n, k], start=(k == 0),
                                   stop=(k == KD - 1))
                mm.then_inc(mod_sum, 1)
            pe.wait_ge(modrow_done, 4)
            for j in range(2 * KD):
                mm = pe.transpose(psum[:, 6, 2 * j:2 * j + 2], modrow[0:2, tblk(j)], ident[0:2, 0:2])
            mm.then_inc(mod_T, 1)
            pe.wait_ge(xhat_done, 1)
            for k in range(KD):
                r = k % 3
                if k >= 3:
                    pe.wait_ge(x0_tile[r], k // 3)
                for i in range(TT):
                    pe.transpose(psum[:, 2 * r, tblk(i)], x_in[:, i, tblk(k)], ident[:])
                for i in range(2):
                    mm = pe.transpose(psum[:, 2 * r + 1, tblk(i)], c_in[:, i, tblk(k)], ident[:])
                mm.then_inc(x0_full[r], 1)

            pe.wait_ge(bg_landed, 16)
            pe.wait_ge(cols_done, 1)
            pe.wait_ge(mod_done, 1)
            pe.wait_ge(x0_tile[1], 3)
            pe.matmul(psum[0:NG, 6, 0:128], bg[0:1, :], ones[0:1, :], start=True, stop=False,
                      skip_group_check=True)
            for i in range(1, 4):
                pe.matmul(psum[0:NG, 6, tblk(i)], bg[0:1, :], ones[0:1, :], start=False, stop=False,
                          skip_group_check=True)
            pe.matmul(psum[0:NG, 7, 0:128], bg[0:1, :], ones[0:1, :], start=True, stop=False,
                      skip_group_check=True)
            pe.matmul(psum[0:NG, 7, 128:256], bg[0:1, :], ones[0:1, :], start=False, stop=False,
                      skip_group_check=True)
            pe.wait_ge(ht_ready, KD)

            def slot_of(what, h):
                n = USE[what]
                pe.wait_ge(evac[n % SLOTS], h * USES + n // SLOTS)
                return n % SLOTS

            def expand(what, h, slot, col, rh, rl, kt, ctx_too, begun=None):
                r = slot_of(what, h)
                wh = w_hi[:, slot].rearrange("p (k n) -> p k n", k=kt)
                wl = w_lo[:, slot].rearrange("p (k n) -> p k n", k=kt)
                for k in range(kt):
                    mm = mul3(pe, psum[:, 2 * r, :], wh[:, k, tblk(col)], wl[:, k, tblk(col)],
                              rh[:, k, NC:NT], rl[:, k, NC:NT], k == 0, k == kt - 1,
                              begun if k == 0 else None)
                if ctx_too:
                    for k in range(kt):
                        mm = mul3(pe, psum[:, 2 * r + 1, 0:NC], wh[:, k, tblk(col)], wl[:, k, tblk(col)],
                                  rh[:, k, 0:NC], rl[:, k, 0:NC], k == 0, k == kt - 1)
                mm.then_inc(full[r], 1)
                return mm

            def unit_ready(m):
                pe.wait_ge(w_ready, m + 1)

            def gate(kind, j, h, hh):
                what = ("vT" if kind == 2 else "qk"[kind], j)
                n = USE[what]
                r = n % SLOTS
                pe.wait_ge(evac[r], h * USES + n // SLOTS + 1)
                pe.matmul(psum[0:NG, 6, :], wg[:, hh, kind, j], tile[:, r, NC:NT], start=False, stop=False,
                          skip_group_check=True)
                mm = pe.matmul(psum[0:NG, 7, 0:NC], wg[:, hh, kind, j], tile[:, r, 0:NC], start=False,
                               stop=False, skip_group_check=True)
                if kind < 2:
                    mm.then_inc(aux[r], 1)

            def turn_v(j, h):
                r = slot_of(("vN", j), h)
                src = USE[("vT", j)] % SLOTS
                for s in range(ST):
                    bank, at_ = (2 * r, s - 2) if s >= 2 else (2 * r + 1, s)
                    mm = pe.transpose(psum[:, bank, tblk(at_)], tile[:, src, tblk(s)], ident[:])
                mm.then_inc(full[r], 1)

            def ada_columns(i, h):
                r = slot_of(("ada", i), h)
                for u in range(2):
                    pe.wait_ge(ada_ready, h * ADA_UNITS + 2 * i + u + 1)
                    for b_ in range(2):
                        mm = pe.matmul(psum[:, 2 * r, 2 * u + b_:2 * u + b_ + 1], asum[:, u, tblk(b_)],
                                       ones[:, 0:1], start=True, stop=True)
                    mm.then_inc(ada_used, 1)
                pe.drain().then_inc(full[r], 1)

            with pe.Fori(0, H // 2) as it:
                for hh in range(2):
                    h = it * 2 + hh
                    m0 = it * 14 + 7 * hh
                    sl = [(7 * hh + u) % 2 for u in range(7)]
                    for u in range(2):
                        unit_ready(m0 + u)
                        for c2 in range(2):
                            expand(("xm", 2 * u + c2), h, sl[u], c2, ht_hi, ht_lo, KD, True,
                                   w_begun if c2 == 0 else None)
                    ada_columns(0, h)
                    unit_ready(m0 + 2)
                    pe.wait_ge(x_split, h * 8 + 4)
                    pe.wait_ge(wg_landed[hh], it * 48 + 48)
                    for j in range(JH):
                        expand(("vT", j), h, sl[2], j, xx_hi, xx_lo, JH, True, w_begun if j == 0 else None)
                        if j >= 1:
                            gate(2, j - 1, h, hh)
                            turn_v(j - 1, h)
                    for u in range(2):
                        unit_ready(m0 + 3 + u)
                        for c2 in range(2):
                            expand(("z", 2 * u + c2), h, sl[3 + u], c2, ht_hi, ht_lo, KD, False,
                                   w_begun if c2 == 0 else None)
                            if u == 0 and c2 == 0:
                                gate(2, 3, h, hh)
                                turn_v(3, h)
                    ada_columns(1, h)
                    unit_ready(m0 + 5)
                    pe.wait_ge(x_split, h * 8 + 8)
                    for j in range(JH):
                        expand(("q", j), h, sl[5], j, xx_hi, xx_lo, JH, True, w_begun if j == 0 else None)
                        if j >= 1:
                            gate(0, j - 1, h, hh)
                    unit_ready(m0 + 6)
                    for j in range(JH):
                        expand(("k", j), h, sl[6], j, xx_hi, xx_lo, JH, True, w_begun if j == 0 else None)
                        gate(1, j - 1, h, hh) if j >= 1 else gate(0, 3, h, hh)
                    pe.wait_ge(qk_split, h * 8 + 8)
                    for s in range(ST):
                        r = slot_of(("S", s), h)
                        for k in range(JH):
                            mm = mul3(pe, psum[:, 2 * r, :], k_hi[:, k, tblk(s)], k_lo[:, k, tblk(s)],
                                      q_hi[:, k], q_lo[:, k], k == 0, k == JH - 1,
                                      wg_used if s == 1 and k == 0 else None)
                        mm.then_inc(full[r], 1)
                        if s == 0:
                            gate(1, 3, h, hh)
                            ada_columns(2, h)
            pe.drain().then_inc(gates_full, 1)

            pe.wait_ge(g_done, 1)
            for d in range(2):
                for s in range(ST):
                    mm = pe.transpose(psum[:, 0, (d * ST + s) * H:(d * ST + s + 1) * H],
                                      g_g[0:H, 1 - d, tblk(s)], ident[0:H, 0:H])
            mm.then_inc(gT_full, 1)
            pe.wait_ge(scans, 1)
            for d in range(2):
                for i in range(TT):
                    c0 = (d * TT + i) * H
                    mm = pe.transpose(psum[:, 1, c0:c0 + H], g_F[0:H, 1 - d, NC + i * P:NC + i * P + P],
                                      ident[0:H, 0:H])
            mm.then_inc(mT_full, 1)
            pe.wait_ge(m_landed, 32)
            pe.wait_ge(sel_ready, 1)

            def bc_bank(use):
                if use > 1:
                    pe.wait_ge(bc_free, use - 1)

            def spread_m(h, d):
                bc_bank(bc_use("M", h, d))
                pe.matmul(psum[:, 3, :], sel[32 * d:32 * d + H, h], m_rows[32 * d:32 * d + H, :], start=True,
                          stop=True).then_inc(bc_full, 1)

            def denominators(h):
                bc_bank(bc_use("den", h))
                pe.wait_ge(p_ready, ST * (h + 1))
                for d in range(2):
                    for i in range(TT):
                        keys = key_tiles(d, i)
                        c0 = 2 * (d * TT + i)
                        for s in keys:
                            at_ = START[s] + pblock(d, s, i)
                            pe.matmul(psum[:, 3, c0:c0 + 2], p_hi[:, at_], ones_r[:], start=(s == keys[0]),
                                      stop=False)
                            mm = pe.matmul(psum[:, 3, c0:c0 + 2], p_lo[:, at_], ones_r[:], start=False,
                                           stop=(s == keys[-1]))
                mm.then_inc(bc_full, 1)

            def ada_columns(h, i):
                bc_bank(bc_use("ada", h, i))
                for u in range(2):
                    pe.wait_ge(ada_ready, ADA0_P2 + 4 * h + 2 * i + u + 1)
                    for b_ in range(2):
                        mm = pe.matmul(psum[:, 3, 2 * u + b_:2 * u + b_ + 1], asum[:, u, tblk(b_)],
                                       ones[:, 0:1], start=True, stop=True)
                    mm.then_inc(ada_used, 1)
                pe.drain().then_inc(bc_full, 1)

            yuse = [0]

            def contract(lh, ll, k0, slot, wait_free=None):
                wh = w_hi[:, slot].rearrange("p (k n) -> p k n", k=4)
                wl = w_lo[:, slot].rearrange("p (k n) -> p k n", k=4)
                for i in range(TT):
                    if wait_free is not None:
                        pe.wait_ge(y_free[i], wait_free)
                    elif yuse[0]:
                        pe.wait_ge(y_free[i], yuse[0])
                    for k in range(4):
                        mm = mul3(pe, psum[:, 4 + i, :], lh[:, k0 + k, tblk(i)], ll[:, k0 + k, tblk(i)],
                                  wh[:, k], wl[:, k], k == 0, k == 3,
                                  w_begun if i == 0 and k == 0 else None)
                    mm.then_inc(y_full[i], 1)
                if wait_free is None:
                    yuse[0] += 1

            def turn_h(h, e):
                pe.wait_ge(h_norm, h + 1)
                bank = 2
                if h == H - 1:
                    bank = (2, 0, 1, 3)[e]
                    pe.wait_ge(back_done, TT * H)
                    pe.wait_ge(forth_done, TT * H)
                    pe.wait_ge(bc_free, bc_use("ada", h, 1))
                if bank == 2 and h:
                    pe.wait_ge(tr_free, min(h * JH + e, (H - 1) * JH))
                elif bank == 2 and e:
                    pe.wait_ge(tr_free, e)
                for i in range(TT):
                    mm = pe.transpose(psum[:, bank, tblk(i)], hn[:, h % 2, i, tblk(e)], ident[:])
                mm.then_inc(tr_full, 1)

            def attend(h, i):
                for d in (FORTH, BACK):
                    if h or i:
                        pe.wait_ge(back_done if d == BACK else forth_done, TT * h + i)
                    keys = key_tiles(d, i)
                    for s in keys:
                        at_ = START[s] + pblock(d, s, i)
                        mm = mul3(pe, psum[:, d, :], p_hi[:, at_], p_lo[:, at_], v_hi[:, s], v_lo[:, s],
                                  s == keys[0], s == keys[-1])
                    mm.then_inc(pv_full[d], 1)

            def project(h, half):
                pe.wait_ge(u_done, h + 1)
                unit_ready(SPLIT0_P2 + 2 * h + half)
                contract(*u_of(h), 0, (SPLIT0_P2 + 2 * h + half) % 2)

            spread_m(0, 0)
            spread_m(0, 1)
            for h in range(H):
                ada_columns(h, 0)
                denominators(h)
                pe.wait_ge(v_landed, 32 * (h + 1))
                for i in range(TT):
                    if h:
                        turn_h(h - 1, i)
                    attend(h, i)
                    if h + 1 < H and i < 2:
                        spread_m(h + 1, i)
                ada_columns(h, 1)
                if h:
                    project(h - 1, 0)
                    if h == H - 1:
                        for e in range(JH):
                            turn_h(h, e)
                    project(h - 1, 1)
            project(H - 1, 0)
            project(H - 1, 1)

            def gate_row(b):
                pe.wait_ge(gate_in, b + 1)
                for half in range(2):
                    mm = pe.matmul(psum[:, half, :], ones[:], gate_diag[:, tblk(half, 4)].rearrange("p k n -> p (k n)"),
                                   start=True, stop=True)
                mm.then_inc(gate_full, 1)

            def boundary(b):
                gate_row(b)
                pe.wait_ge(b_xhat, b + 1)
                for k in range(KD):
                    r = k % 2
                    if b * 4 + k // 2:
                        pe.wait_ge(b_tile[r], b * 4 + k // 2)
                    for i in range(TT):
                        mm = pe.transpose(psum[:, r, tblk(i)], y_acc[:, i, tblk(k)], ident[:])
                    mm.then_inc(b_full[r], 1)
                pe.drain().then_inc(b_turned, 1)

            def mlp(layer, m0, y0):
                pe.wait_ge(b_split[0], (2 * layer + 1) * 4)
                pe.wait_ge(b_split[1], (2 * layer + 1) * 4)
                with pe.Fori(0, GROUPS) as gr:
                    for u in range(4):
                        slot = (m0 + u) % 2
                        wh = w_hi[:, slot].rearrange("p (k n) -> p k n", k=KD)
                        wl = w_lo[:, slot].rearrange("p (k n) -> p k n", k=KD)
                        unit_ready(gr * 8 + m0 + u)
                        for c2 in range(2):
                            pe.wait_ge(a_relu[c2], gr * 4 + layer * 16 + u)
                            for k in range(KD):
                                mm = mul3(pe, psum[:, c2, :], wh[:, k, tblk(c2)], wl[:, k, tblk(c2)],
                                          hh_hi[:, k], hh_lo[:, k], k == 0, k == KD - 1,
                                          w_begun if c2 == 0 and k == 0 else None)
                            mm.then_inc(a_full[c2], 1)

                    for u in range(4):
                        unit_ready(gr * 8 + m0 + 4 + u)
                        if u == 0:
                            pe.wait_ge(a_split[0], gr * 4 + layer * 16 + 2)
                            pe.wait_ge(a_split[1], gr * 4 + layer * 16 + 2)
                        if u == 1:
                            pe.wait_ge(a_split[0], gr * 4 + layer * 16 + 4)
                            pe.wait_ge(a_split[1], gr * 4 + layer * 16 + 4)
                        contract(ff_hi, ff_lo, (u % 2) * 4, (m0 + u) % 2, gr * 4 + y0 + u)

            boundary(0)
            mlp(0, SPLIT0_MLP0, 8)
            boundary(1)

            pe.wait_ge(b_split[0], 8)
            pe.wait_ge(b_split[1], 8)
            m = SPLIT0_F
            unit_ready(m)
            s0 = m % 2
            n = 0
            for gr in range(4):
                for i in range(TT):
                    if n >= 2:
                        pe.wait_ge(f_tile[n % 2], n // 2)
                    for k in range(2):
                        mm = mul3(pe, psum[:, n % 2, :], hh_hi[:, 2 * gr + k, tblk(i)],
                                  hh_lo[:, 2 * gr + k, tblk(i)], w_hi[:, s0, tblk(k, 512)],
                                  w_lo[:, s0, tblk(k, 512)], k == 0, k == 1,
                                  w_begun if n == 0 and k == 0 else None)
                    mm.then_inc(f_full[n % 2], 1)
                    n += 1
            unit_ready(m + 1)
            pe.wait_ge(f_split[0], 8)
            pe.wait_ge(f_split[1], 8)
            for gr in range(4):
                for part in range(2):
                    sl = (m + 1 + part) % 2
                    if gr == 0 and part == 1:
                        unit_ready(m + 2)
                    for half in range(2):
                        n = 16 + 2 * gr + half
                        if part == 0:
                            pe.wait_ge(f_tile[n % 2], n // 2)
                        begins = half == 0 and (gr, part) in ((0, 0), (3, 1))
                        for i in range(TT):
                            cs = slice(part * 256 + half * P, part * 256 + half * P + P)
                            mm = mul3(pe, psum[:, n % 2, :], a_hi[:, i, gr, cs], a_lo[:, i, gr, cs],
                                      w_hi[:, sl, tblk(i, 512)], w_lo[:, sl, tblk(i, 512)],
                                      part == 0 and i == 0, part == 1 and i == TT - 1,
                                      w_begun if begins and i == 0 else None)
                        if part == 1:
                            mm.then_inc(f_full[n % 2], 1)
            pe.wait_ge(f_split[0], 12)
            pe.wait_ge(f_split[1], 12)
            for u in range(4):
                unit_ready(m + 3 + u)
                contract(hh_hi, hh_lo, (u % 2) * 4, (m + 3 + u) % 2, 24 + u)
            boundary(2)
            mlp(1, SPLIT0_MLP1, 28)
            gate_row(3)

        @block.scalar
        def _(act):
            a = nc.scalar
            act.dma_start(x_in[:], x.rearrange("a (i p) d -> p (a i) d", p=P)).then_inc(in_landed[1], 16)
            act.dma_start(c_in[:], ctx.rearrange("a (i p) d -> p (a i) d", p=P)).then_inc(in_landed[2], 16)
            act.wait_ge(in_landed[0], 32)
            a.activation(svec[:], cvec[:], ACT.Silu).then_inc(silu_c, 1)
            for n in range(4):
                act.wait_ge(mod_sum, n + 1)
                a.copy(modrow[0:2, tblk(n, 512)], psum[0:2, n, :]).then_inc(modrow_done, 1)
            act.wait_ge(var_done, 1)
            a.activation(std[:], std[:], ACT.Sqrt).then_inc(std_done, 1)
            act.wait_ge(mod_done, 1)
            for k in range(KD):
                r = k % 3
                act.wait_ge(x0_full[r], k // 3 + 1)
                if k >= 3:
                    act.wait_ge(x0_split[r], k // 3)
                a.activation(tile[:, r, NC:NT], psum[:, 2 * r, :], ACT.Identity,
                             scale=mod0[:, KD + k, 0:1], bias=mod0[:, k, 0:1])
                a.activation(tile[:, r, 0:NC], psum[:, 2 * r + 1, 0:NC], ACT.Identity,
                             scale=mod0[:, KD + k, 1:2], bias=mod0[:, k, 1:2]).then_inc(x0_tile[r], 1)

            act.wait_ge(ht_ready, KD)

            def stage_tile(what, h):
                n = USE[what]
                r = n % SLOTS
                act.wait_ge(full[r], h * USES + n // SLOTS + 1)
                if what[0] == "ada":
                    a.copy(adac[:, bass.ds(h * (2 * ADA_UNITS) + vec(1, 0) + 4 * what[1], 4)],
                           psum[:, 2 * r, 0:4]).then_inc(evac[r], 1)
                    return n, r
                if what[0] == "xm":
                    act.wait_ge(conv_done, h * JH)
                else:
                    prev = n - SLOTS
                    while prev >= 0 and HEAD[prev][0] in ("xm", "ada"):
                        prev -= SLOTS
                    for reader, s, w in (("pe", aux, 1), ("dve", taken, 1), ("dma", spilled, 16)):
                        if reader in READERS[HEAD[prev][0]]:
                            act.wait_ge(s[r], h * (w * reads_per_head(reader, r))
                                        + w * reads_before(reader, prev))
                    if HEAD[prev][0] == "vT":
                        t = USE[("vN", HEAD[prev][1])]
                        act.wait_ge(full[t % SLOTS], h * USES + t // SLOTS + 1)
                dst = xm[:, what[1]] if what[0] == "xm" else tile[:, r]
                lat_only = what[0] in ("z", "S")
                if what[0] == "z":
                    op = a.activation(dst[:, NC:NT], psum[:, 2 * r, :], ACT.Silu)
                elif lat_only:
                    op = a.copy(dst[:, NC:NT], psum[:, 2 * r, :])
                else:
                    scale = K_SCALE if what[0] == "k" else 1.0
                    a.activation(dst[:, NC:NT], psum[:, 2 * r, :], ACT.Copy, scale=scale)
                    op = a.activation(dst[:, 0:NC], psum[:, 2 * r + 1, 0:NC], ACT.Copy, scale=scale)
                op.then_inc(evac[r], 1)
                return n, r

            def spill(n, r, h, dst):
                act.wait_ge(evac[r], h * USES + n // SLOTS + 1)
                act.dma_start(dst, tile[:, r, NC:NT]).then_inc(spilled[r], 16)

            def spill_v(j, h):
                act.wait_ge(v_split, h * JH + j + 1)
                for st_, d_ in ((v_st_hi, v_hi_d), (v_st_lo, v_lo_d)):
                    act.dma_start(d_[bass.ds(h, 1)].rearrange("a p s e -> p (a s) e")[:, :, tblk(j)],
                                  st_[:].bitcast(F32)).then_inc(v_spilled, 16)

            def gate_x(j, h):
                act.wait_ge(conv_done, h * JH + j + 1)
                a.activation(xc[:, j % 2], xc[:, j % 2], ACT.Silu).then_inc(xc_done, 1)
                act.wait_ge(xc_done, h * JH + j + 1)
                act.wait_ge(sx_spilled[j % 2], h * 32 + 16 * (j // 2))
                a.activation(sx_st[:, j % 2], xc[:, j % 2, NC:NT], ACT.Copy,
                             scale=cols[:, bass.ds(h * JH + 176 + j, 1)]).then_inc(sx_done, 1)
                act.wait_ge(sx_done, h * JH + j + 1)
                act.dma_start(sx_d[bass.ds(h * JH + j, 1)].rearrange("a p t -> p (a t)"), sx_st[:, j % 2]
                              ).then_inc(sx_spilled[j % 2], 16)

            def z_out(j, h):
                n, r = stage_tile(("z", j), h)
                spill(n, r, h, z_d[bass.ds(h * JH + j, 1)].rearrange("a p t -> p (a t)"))

            with act.Fori(0, H // 2) as it:
                for hh in range(2):
                    h = it * 2 + hh
                    for what in HEAD[0:10]:
                        stage_tile(what, h)
                    spill_v(0, h)
                    stage_tile(("vT", 3), h)
                    gate_x(0, h)
                    stage_tile(("vN", 2), h)
                    spill_v(1, h)
                    z_out(0, h)
                    gate_x(1, h)
                    spill_v(2, h)
                    stage_tile(("vN", 3), h)
                    z_out(1, h)
                    gate_x(2, h)
                    z_out(2, h)
                    spill_v(3, h)
                    z_out(3, h)
                    gate_x(3, h)
                    stage_tile(("ada", 1), h)
                    for j in range(JH):
                        stage_tile(("q", j), h)
                    for j in range(JH):
                        stage_tile(("k", j), h)
                    for s in range(ST):
                        n, r = stage_tile(("S", s), h)
                        spill(n, r, h, s_d[bass.ds(h, 1), s].rearrange("a p t -> p (a t)"))
                        if s == 0:
                            stage_tile(("ada", 2), h)

            act.wait_ge(gates_full, 1)
            a.copy(pre[:, NC:NT], psum[0:NG, 6, :])
            a.copy(pre[:, 0:NC], psum[0:NG, 7, 0:NC]).then_inc(pre_done, 1)
            act.wait_ge(pre_done, 1)
            for d in range(2):
                act.dma_start(g_i[:, d], pre[8 * d:8 * d + 4, :]).then_inc(gate_rows, 16)
                act.dma_start(g_f[:, d], pre[8 * d + 4:8 * d + 8, :]).then_inc(gate_rows, 16)
            act.wait_ge(abs_f, 1)
            a.activation(g_t[:], g_a[:], ACT.Exp, scale=-1.0).then_inc(soft, 1)
            act.wait_ge(soft, 1)
            a.activation(g_t[:], g_t[:], ACT.Ln, bias=1.0).then_inc(soft, 1)

            def load_s(h):
                if h:
                    act.wait_ge(p_hi_done, ST * h)
                act.dma_start(s_in[:], s_d[h].rearrange("s p t -> p s t")).then_inc(s_landed, 16)

            def load_v(h):
                if h:
                    act.wait_ge(pv_full[BACK], TT * h)
                act.dma_start(v_hi[:].bitcast(F32), v_hi_d[h]).then_inc(v_landed, 16)
                act.dma_start(v_lo[:].bitcast(F32), v_lo_d[h]).then_inc(v_landed, 16)

            def load_z(n):
                if n >= 3:
                    act.wait_ge(zu_done, n - 2)
                act.dma_start(zt[:, n % 3], z_d[n]).then_inc(z_landed[n % 3], 16)
                act.dma_start(sxt[:, n % 3], sx_d[n]).then_inc(z_landed[n % 3], 16)

            for r in range(SLOTS):
                act.wait_ge(spilled[r], 16 * H * reads_per_head("dma", r))
            for r in range(2):
                act.wait_ge(sx_spilled[r], 32 * H)
            act.wait_ge(v_spilled, 32 * JH * H)
            act.wait_ge(scans, 1)
            for d, scan_d in ((BACK, 1), (FORTH, 0)):
                act.dma_start(m_rows[32 * d:32 * d + H, :], g_M[:, scan_d, NC:NT]).then_inc(m_landed, 16)
            act.wait_ge(mT_full, 1)
            a.activation(exp_m[:].rearrange("p d i h -> p (d i h)"), psum[:, 1, 0:2 * TT * H], ACT.Exp,
                         scale=-1.0).then_inc(exp_m_done, 1)
            act.wait_ge(m_done, 1)
            act.wait_ge(m_landed, 32)
            load_s(0)
            load_v(0)
            load_z(0)
            load_z(1)

            def take_m(h, d):
                act.wait_ge(bc_full, bc_use("M", h, d))
                a.copy(mb[:, d], psum[:, 3, :]).then_inc(bc_free, 1)
                act.drain().then_inc(mb_done, 1)

            def weights(h, s):
                n = ST * h + s
                if n >= 3:
                    act.wait_ge(p_ready, n - 2)
                w = wt[n % 3][:].rearrange("p b t -> p (b t)")
                jj = s - 2
                if s >= 2:
                    act.wait_ge(diag_in, 4 * h + jj + 1)
                    a.activation(w[:, jj * P:(jj + 2) * P], w[:, jj * P:(jj + 2) * P], ACT.Exp, scale=-1.0)
                for d, t0, t1 in (((BACK, 0, NL), (FORTH, 0, NL)) if s < 2
                                  else ((BACK, 0, jj * P), (FORTH, (jj + 1) * P, NL))):
                    if t0 < t1:
                        w0 = P * pblock(d, s, 0)
                        a.activation(w[:, w0 + t0:w0 + t1], mb[:, d, t0:t1], ACT.Exp, scale=-1.0,
                                     bias=gcol[:, d, s, h:h + 1])
                act.drain().then_inc(w_exp, 1)

            def take_ada(h, i):
                act.wait_ge(bc_full, bc_use("ada", h, i))
                c0 = vec(0, ADA0[h]) + 4 * i
                a.copy(adac[:, c0:c0 + 4], psum[:, 3, 0:4]).then_inc(bc_free, 1)

            take_m(0, 0)
            take_m(0, 1)
            for s in range(ST):
                weights(0, s)
            for h in range(H):
                take_ada(h, 0)
                act.wait_ge(den_done, h + 1)
                if h + 1 < H:
                    load_s(h + 1)
                for i in range(TT):
                    act.wait_ge(pv_full[FORTH], TT * h + i + 1)
                    a.activation(hn[:, h % 2, i], psum[:, FORTH, :], ACT.Copy, scale=den[:, FORTH, i:i + 1]
                                 ).then_inc(forth_done, 1)
                    if h:
                        load_z(4 * (h - 1) + i + 2)
                    if h + 1 < H:
                        if i < 2:
                            take_m(h + 1, i)
                        else:
                            weights(h + 1, i - 2)
                if h + 1 < H:
                    load_v(h + 1)
                take_ada(h, 1)
                act.wait_ge(h_var, h + 1)
                a.activation(std[:, 0:TT], std[:, 0:TT], ACT.Sqrt).then_inc(h_std, 1)

                if h + 1 < H:
                    for s in range(2, ST):
                        weights(h + 1, s)
                act.wait_ge(h_rs, h + 1)
                for i in range(TT):
                    a.activation(hn[:, h % 2, i], hn[:, h % 2, i], ACT.Identity, scale=rstd[:, i:i + 1],
                                 bias=nmr[:, i:i + 1])
                act.drain().then_inc(h_norm, 1)
            load_z(H * JH - 2)
            load_z(H * JH - 1)

            def boundary_loads(b):
                act.dma_start(pg[:], post_g[b // 2, b % 2:b % 2 + 1, :].to_broadcast([P, D])
                              ).then_inc(pgb_landed, 16)
                act.dma_start(pbb[:], post_b[b // 2, b % 2:b % 2 + 1, :].to_broadcast([P, D])
                              ).then_inc(pgb_landed, 16)

            def boundary(b):
                act.wait_ge(b_var, 2 * b + 1)
                a.activation(std[:, 0:TT], std[:, 0:TT], ACT.Sqrt).then_inc(b_std, 1)
                for i in range(TT):
                    act.wait_ge(b_norm_in, 2 * b + 1)
                    a.activation(y_acc[:, i], y_acc[:, i], ACT.Identity, scale=rstd[:, i:i + 1],
                                 bias=nmr[:, i:i + 1]).then_inc(b_norm, 1)
                if b == 3:
                    return
                act.wait_ge(b_var, 2 * b + 2)
                a.activation(std[:, 0:TT], std[:, 0:TT], ACT.Sqrt).then_inc(b_std, 1)
                for i in range(TT):
                    act.wait_ge(b_norm_in, 2 * b + 2)
                    a.activation(y_acc[:, i], x_nat[:, i], ACT.Identity, scale=rstd[:, i:i + 1],
                                 bias=nmr[:, i:i + 1])
                act.drain().then_inc(b_xhat, 1)
                sh, sc = MODS[b]
                act.wait_ge(b_cols, 1)
                for k in range(KD):
                    r = k % 2
                    act.wait_ge(b_full[r], 4 * b + k // 2 + 1)
                    if b * 4 + k // 2:
                        act.wait_ge(b_split[r], 4 * b + k // 2)
                    a.activation(btile[:, r], psum[:, r, :], ACT.Identity, scale=adac[:, sc + k:sc + k + 1],
                                 bias=adac[:, sh + k:sh + k + 1]).then_inc(b_tile[r], 1)

            act.wait_ge(y_full[0], 7)
            act.dma_start(x_res[:], x.rearrange("a (i p) d -> p (a i) d", p=P)).then_inc(res_landed, 16)
            boundary_loads(0)
            boundary(0)

            def mlp(layer):
                act.wait_ge(b_x, (2 * layer + 1) * TT)
                boundary_loads(2 * layer + 1)
                with act.Fori(0, GROUPS) as gr:
                    for u in range(4):
                        for c2 in range(2):
                            n = gr * 4 + layer * 16 + u
                            act.wait_ge(a_full[c2], n + 1)
                            act.wait_ge(a_sq[c2], n)
                            a.activation(relu[:, c2], psum[:, c2, :], ACT.Relu).then_inc(a_relu[c2], 1)
                            act.wait_ge(a_split[c2], n)
                            act.wait_ge(a_relu[c2], n + 1)
                            a.activation(sq[:, c2], relu[:, c2], ACT.Square).then_inc(a_sq[c2], 1)
            mlp(0)
            boundary(1)
            for n in range(24):
                act.wait_ge(f_full[n % 2], n // 2 + 1)
                if n >= 2:
                    act.wait_ge(f_split[n % 2], n // 2)
                a.copy(ftile[n % 2][:], psum[:, n % 2, :]).then_inc(f_tile[n % 2], 1)
            boundary_loads(2)
            boundary(2)
            mlp(1)
            boundary(3)

        @block.vector
        def _(dve):
            v = nc.vector

            def split(dst_hi, dst_lo, src):
                v.tensor_copy(dst_hi, src)
                dve.drain()
                return v.tensor_tensor(dst_lo, src, dst_hi.bitcast(F32), ALU.subtract)

            def finish_stats(n):
                dve.drain()
                for i in range(n):
                    v.bn_aggr(mv[:, i], stat[:, i].rearrange("p a b -> p (a b)"))
                dve.drain()
                return v.tensor_scalar(std[:, 0:n], mv[:, 0:n, 1], EPS, None, ALU.add)

            def rstd_nmr(n):
                v.reciprocal(rstd[:, 0:n], std[:, 0:n])
                dve.drain()
                return v.scalar_tensor_tensor(out=nmr[:, 0:n], in0=mv[:, 0:n, 0], scalar=-1.0,
                                              in1=rstd[:, 0:n], op0=ALU.mult, op1=ALU.mult)

            dve.wait_ge(in_landed[1], 16)
            for i in range(TT):
                for half in range(2):
                    v.bn_stats(stat[:, i, half], x_in[:, i, tblk(half, 512)])
            dve.wait_ge(in_landed[2], 16)
            for i in range(2):
                for half in range(2):
                    v.bn_stats(stat[:, TT + i, half], c_in[:, i, tblk(half, 512)])
            finish_stats(6).then_inc(var_done, 1)
            dve.wait_ge(std_done, 1)
            rstd_nmr(6)
            dve.drain()
            for i in range(TT):
                v.tensor_scalar(x_in[:, i], x_in[:, i], rstd[:, i:i + 1], nmr[:, i:i + 1], ALU.mult, ALU.add)
            for i in range(2):
                v.tensor_scalar(c_in[:, i], c_in[:, i], rstd[:, TT + i:TT + i + 1],
                                nmr[:, TT + i:TT + i + 1], ALU.mult, ALU.add)
            dve.drain().then_inc(xhat_done, 1)
            dve.wait_ge(col_T, 1)
            v.tensor_copy(cols[:], psum[:, 7, 0:288]).then_inc(cols_done, 1)
            dve.wait_ge(cols_done, 1)
            dve.wait_ge(mod_T, 1)
            for row in range(2):
                v.tensor_tensor(mod0[:, :, row], psum[:, 6, row:32:2], cols[:, 192:208], ALU.add)
            dve.drain()
            v.tensor_scalar(mod0[:, KD:2 * KD], mod0[:, KD:2 * KD], 1.0, None, ALU.add).then_inc(mod_done, 1)
            for k in range(KD):
                r = k % 3
                dve.wait_ge(x0_tile[r], k // 3 + 1)
                split(ht_hi[:, k], ht_lo[:, k], tile[:, r]).then_inc(x0_split[r], 1)
                dve.drain().then_inc(ht_ready, 1)

            def staged(what, h):
                n = USE[what]
                dve.wait_ge(evac[n % SLOTS], h * USES + n // SLOTS + 1)
                return n % SLOTS

            def conv(j, h):
                def tap(kl):
                    return cols[:, bass.ds(h * JH + kl * 16 + j, 1)]

                dve.drain()
                dve.wait_ge(sx_done, h * JH + (j - 1 if j >= 2 else 0))
                acc_ = xc[:, j % 2]
                src = xm[:, j]
                v.tensor_scalar(acc_, src, tap(4), cols[:, bass.ds(h * JH + 144 + j, 1)], ALU.mult, ALU.add)
                dve.drain()
                a_c, s_c = acc_[:, 0:NC], src[:, 0:NC]
                a_l = acc_[:, NC:NT].rearrange("p (r c) -> p r c", c=GRID)
                s_l = src[:, NC:NT].rearrange("p (r c) -> p r c", c=GRID)

                def add(dst, source, kl):
                    return v.scalar_tensor_tensor(out=dst, in0=source, scalar=tap(kl), in1=dst,
                                                  op0=ALU.mult, op1=ALU.add)

                add(a_c[:, 1:NC], s_c[:, 0:NC - 1], 3)
                for k in range(3):
                    for l in range(3):
                        if (k, l) == (1, 1):
                            continue
                        dr, dc = k - 1, l - 1
                        r0, r1 = max(0, -dr), ROWS - max(0, dr)
                        c0, c1 = max(0, -dc), GRID - max(0, dc)
                        add(a_l[:, r0:r1, c0:c1], s_l[:, r0 + dr:r1 + dr, c0 + dc:c1 + dc], 3 * k + l)
                        dve.drain()
                        if (k, l) == (0, 1):
                            add(a_c[:, 0:NC - 1], s_c[:, 1:NC], 5)
                dve.drain().then_inc(conv_done, 1)

            def split_v(j, h):
                r = staged(("vN", j), h)
                dve.wait_ge(v_spilled, (h * JH + j) * 32)
                split(v_st_hi[:].rearrange("p s e -> p (s e)"), v_st_lo[:].rearrange("p s e -> p (s e)"),
                      tile[:, r]).then_inc(taken[r], 1)
                dve.drain().then_inc(v_split, 1)

            def split_x(j, h):
                dve.wait_ge(xc_done, h * JH + j + 1)
                n = USE[("vT", 3)]
                dve.wait_ge(full[n % SLOTS], h * USES + n // SLOTS + 1)
                split(xx_hi[:, j], xx_lo[:, j], xc[:, j % 2]).then_inc(x_split, 1)

            with dve.Fori(0, H // 2) as it:
                for hh in range(2):
                    h = it * 2 + hh
                    for j in range(JH):
                        staged(("xm", j), h)
                        split(xx_hi[:, j], xx_lo[:, j], xm[:, j]).then_inc(x_split, 1)
                    conv(0, h)
                    split_v(0, h)
                    conv(1, h)
                    split_v(1, h)
                    split_x(0, h)
                    conv(2, h)
                    split_v(2, h)
                    split_x(1, h)
                    conv(3, h)
                    split_v(3, h)
                    split_x(2, h)
                    split_x(3, h)
                    for j in range(JH):
                        r = staged(("q", j), h)
                        split(q_hi[:, j], q_lo[:, j], tile[:, r, NC:NT]).then_inc(taken[r], 1)
                        dve.drain().then_inc(qk_split, 1)
                    for j in range(JH):
                        r = staged(("k", j), h)
                        split(k_hi[:, j], k_lo[:, j], tile[:, r]).then_inc(taken[r], 1)
                        dve.drain().then_inc(qk_split, 1)

            dve.wait_ge(gate_rows, 64)
            v.scalar_tensor_tensor(out=g_a[:], in0=g_f[:], scalar=-1.0, in1=g_f[:], op0=ALU.mult,
                                   op1=ALU.max).then_inc(abs_f, 1)
            v.memset(g_z[:], 0.0)
            dve.wait_ge(soft, 2)
            v.scalar_tensor_tensor(out=g_f[:], in0=g_f[:], scalar=0.0, in1=g_t[:], op0=ALU.min,
                                   op1=ALU.subtract)
            dve.drain()

            def scan(dst, src, other, op1):
                v.tensor_tensor_scan(dst[:, 0], src[:, 0], other(0, slice(0, NT)), 0.0, op1, op1)
                back_c, back_l = slice(NC - 1, None, -1), slice(NT - 1, NC - 1, -1)
                v.tensor_tensor_scan(dst[:, 1, back_c], src[:, 1, back_c], other(1, back_c), 0.0,
                                     op1, op1)
                dve.drain()
                v.tensor_tensor_scan(dst[:, 1, back_l], src[:, 1, back_l], other(1, back_l), dst[:, 1, 0:1],
                                     op1, op1)
                dve.drain()

            scan(g_F, g_f, lambda d, s: g_z[:, s], ALU.add)
            v.tensor_tensor(g_g[:], g_i[:], g_F[:], ALU.subtract)
            dve.drain().then_inc(g_done, 1)
            scan(g_M, g_g, lambda d, s: g_g[:, d, s], ALU.max)
            v.tensor_tensor(g_F[:], g_F[:], g_M[:], ALU.add).then_inc(scans, 1)
            dve.wait_ge(gT_full, 1)
            v.tensor_copy(gcol[:].rearrange("p d s h -> p (d s h)"), psum[:, 0, 0:2 * ST * H]
                          ).then_inc(m_done, 1)

            def diagonal(h, jj):
                n = ST * h + 2 + jj
                dve.wait_ge(mb_done, 2 * h + 2)
                if n >= 3:
                    dve.wait_ge(p_ready, n - 2)
                for d in range(2):
                    v.scalar_tensor_tensor(out=wt[n % 3][:, jj + d], in0=mb[:, d, tblk(jj)],
                                           scalar=gcol[:, d, 2 + jj, h:h + 1], in1=mask[:, d],
                                           op0=ALU.subtract, op1=ALU.max)
                dve.drain().then_inc(diag_in, 1)

            def products(h, s):
                n = ST * h + s
                w = wt[n % 3][:].rearrange("p b t -> p (b t)")
                dve.wait_ge(w_exp, n + 1)
                if s == 0:
                    dve.wait_ge(s_landed, 16 * (h + 1))
                    if h:
                        dve.wait_ge(pv_full[BACK], TT * h)
                for d in range(2):
                    t0 = 0 if s < 2 or d == BACK else (s - 2) * P
                    t1 = NL if s < 2 or d == FORTH else (s - 1) * P
                    w0 = P * pblock(d, s, 0)
                    v.tensor_tensor(w[:, w0 + t0:w0 + t1], w[:, w0 + t0:w0 + t1], s_in[:, s, t0:t1], ALU.mult)
                dve.drain()
                v.tensor_copy(p_hi[:, START[s]:START[s] + BLOCKS[s]], wt[n % 3][:, 0:BLOCKS[s]]
                              ).then_inc(p_hi_done, 1)

            def add_y(i, half, first):
                src = psum[:, 4 + i, :]
                dst = y_acc[:, i, tblk(half, 512)]
                if first:
                    v.tensor_copy(dst, src).then_inc(y_free[i], 1)
                else:
                    v.tensor_tensor(dst, dst, src, ALU.add).then_inc(y_free[i], 1)

            def take_y(h, n):
                half, i = n // TT, n % TT
                dve.wait_ge(y_full[i], 2 * h + half + 1)
                add_y(i, half, h == 0)

            def read_out(h, e):
                n = h * JH + e
                bank = 2 if h < H - 1 else (2, 0, 1, 3)[e]
                r = n % 3
                dve.wait_ge(tr_full, n + 1)
                dve.wait_ge(z_landed[r], 32 * (n // 3 + 1))
                if e == 0 and 0 < h < H - 1:
                    dve.wait_ge(y_full[TT - 1], 2 * h)
                v.scalar_tensor_tensor(out=sxt[:, r], in0=psum[:, bank, :], scalar=cols[:, 160 + n:161 + n],
                                       in1=sxt[:, r], op0=ALU.mult, op1=ALU.add).then_inc(tr_free, 1)
                dve.drain()
                v.tensor_tensor(zt[:, r], zt[:, r], sxt[:, r], ALU.mult)
                dve.drain()
                hi, lo = u_of(h)
                split(hi[:, e], lo[:, e], zt[:, r]).then_inc(zu_done, 1)
                if e == JH - 1:
                    dve.drain().then_inc(u_done, 1)

            def head_denominators(h):
                dve.wait_ge(bc_full, bc_use("den", h))
                src = psum[:, 3, 0:4 * TT:2].rearrange("p (d i) -> p d i", d=2)
                v.scalar_tensor_tensor(out=dena[:], in0=src, scalar=-1.0, in1=exp_m[:, :, :, h],
                                       op0=ALU.mult, op1=ALU.max)
                dve.drain()
                v.tensor_tensor(dena[:], dena[:], src, ALU.max).then_inc(bc_free, 1)
                dve.drain()
                v.reciprocal(den[:], dena[:])
                dve.drain().then_inc(den_done, 1)

            dve.wait_ge(exp_m_done, 1)
            dve.wait_ge(sel_ready, 1)
            diagonal(0, 0)
            for s in range(ST):
                products(0, s)
                if 1 <= s < TT:
                    diagonal(0, s)
            for h in range(H):
                head_denominators(h)
                for i in range(TT):
                    if h:
                        read_out(h - 1, i)
                    dve.wait_ge(forth_done, TT * h + i + 1)
                    dve.wait_ge(pv_full[BACK], TT * h + i + 1)
                    hh = hn[:, h % 2, i]
                    v.scalar_tensor_tensor(out=hh, in0=psum[:, BACK, :], scalar=den[:, BACK, i:i + 1], in1=hh,
                                           op0=ALU.mult, op1=ALU.add).then_inc(back_done, 1)
                    dve.drain()
                    v.bn_stats(stat[:, i, 0], hh)
                dve.drain()
                for i in range(TT):
                    v.bn_aggr(mv[:, i], stat[:, i, 0])
                dve.drain()
                v.tensor_scalar(std[:, 0:TT], mv[:, 0:TT, 1], EPS, None, ALU.add).then_inc(h_var, 1)
                if h + 1 < H:
                    diagonal(h + 1, 0)
                dve.wait_ge(h_std, h + 1)
                rstd_nmr(TT)
                dve.drain().then_inc(h_rs, 1)
                for n in range(2 * TT):
                    if h + 1 < H and n < ST:
                        products(h + 1, n)
                        if 1 <= n < TT:
                            diagonal(h + 1, n)
                    if h and h < H - 1:
                        take_y(h - 1, n)
            for n in range(TT):
                take_y(H - 2, n)
            for e in range(JH):
                read_out(H - 1, e)
                take_y(H - 2, TT + e)
            for n in range(2 * TT):
                take_y(H - 1, n)

            def boundary(b):
                old = x_res if b == 0 else x_nat
                if b == 0:
                    dve.wait_ge(bc_free, bc_use("ada", H - 1, 1))
                    used = slice(vec(0, G1), None)
                    v.tensor_tensor(adac[:, used], adac[:, used], cols[:, 192 + vec(0, G1):288], ALU.add)
                    dve.drain()
                    for _, sc in MODS:
                        v.tensor_scalar(adac[:, sc:sc + KD], adac[:, sc:sc + KD], 1.0, None, ALU.add)
                    dve.drain().then_inc(b_cols, 1)
                for k in range(KD):
                    c0 = GATE[b] + k
                    v.tensor_scalar(gate_diag[:, k], ident[:], adac[:, c0:c0 + 1], None, ALU.mult)
                dve.drain().then_inc(gate_in, 1)
                dve.wait_ge(gate_full, b + 1)
                for i in range(TT):
                    v.tensor_tensor(y_acc[:, i], y_acc[:, i], psum[:, 0:2, :].rearrange("p a n -> p (a n)"),
                                    ALU.mult)
                if b == 0:
                    dve.wait_ge(res_landed, 16)
                dve.drain()
                for i in range(TT):
                    v.scalar_tensor_tensor(out=y_acc[:, i], in0=old[:, i], scalar=ALPHA, in1=y_acc[:, i],
                                           op0=ALU.mult, op1=ALU.add)
                dve.drain()
                for i in range(TT):
                    for half in range(2):
                        v.bn_stats(stat[:, i, half], y_acc[:, i, tblk(half, 512)])
                finish_stats(TT).then_inc(b_var, 1)
                dve.wait_ge(b_std, 1 if b == 0 else 2 * b + 1)
                rstd_nmr(TT)
                dve.drain().then_inc(b_norm_in, 1)
                dve.wait_ge(pgb_landed, 32 * (b + 1))
                for i in range(TT):
                    dve.wait_ge(b_norm, b * TT + i + 1)
                    v.tensor_tensor(y_acc[:, i], y_acc[:, i], pg[:], ALU.mult)
                    dve.drain()
                    v.tensor_tensor(x_nat[:, i], y_acc[:, i], pbb[:], ALU.add).then_inc(b_x, 1)
                if b == 3:
                    return
                dve.drain()
                for i in range(TT):
                    for half in range(2):
                        v.bn_stats(stat[:, i, half], x_nat[:, i, tblk(half, 512)])
                finish_stats(TT).then_inc(b_var, 1)
                dve.wait_ge(b_std, 2 * b + 2)
                rstd_nmr(TT)
                dve.drain().then_inc(b_norm_in, 1)
                for k in range(KD):
                    r = k % 2
                    dve.wait_ge(b_tile[r], 4 * b + k // 2 + 1)
                    split(hh_hi[:, k], hh_lo[:, k], btile[:, r]).then_inc(b_split[r], 1)
                dve.wait_ge(b_turned, b + 1)
                v.memset(y_acc[:], 0.0)
                dve.drain()

            def mlp(layer, y0):
                with dve.Fori(0, GROUPS) as gr:
                    for u in range(4):
                        for c2 in range(2):
                            dve.wait_ge(a_sq[c2], gr * 4 + layer * 16 + u + 1)
                            split(ff_hi[:, 2 * u + c2], ff_lo[:, 2 * u + c2], sq[:, c2]
                                  ).then_inc(a_split[c2], 1)
                    for u in range(4):
                        for i in range(TT):
                            dve.wait_ge(y_full[i], gr * 4 + y0 + u + 1)
                            add_y(i, u // 2, False)

            boundary(0)
            mlp(0, 8)
            boundary(1)
            for n in range(16):
                dve.wait_ge(f_tile[n % 2], n // 2 + 1)
                split(a_hi[:, n % 4, n // 4], a_lo[:, n % 4, n // 4], ftile[n % 2][:]).then_inc(f_split[n % 2], 1)
            for n in range(16, 24):
                dve.wait_ge(f_tile[n % 2], n // 2 + 1)
                split(hh_hi[:, n - 16], hh_lo[:, n - 16], ftile[n % 2][:]).then_inc(f_split[n % 2], 1)
            for u in range(4):
                for i in range(TT):
                    dve.wait_ge(y_full[i], 24 + u + 1)
                    add_y(i, u // 2, False)
            boundary(2)
            mlp(1, 28)
            boundary(3)


def dft_tables():
    ch = np.outer(np.arange(FG), np.arange(FG)) % FG * (2 * np.pi / FG)
    chan = np.concatenate([np.cos(ch), np.sin(ch)], axis=1)
    sq = np.outer(np.arange(NL), np.arange(NL)) % NL * (2 * np.pi / NL)
    scale = 1.0 / np.sqrt(NL * FG)
    units = np.zeros((3, P, UNIT))
    units[0, :, 0:1024] = chan.reshape(2, P, 512).transpose(1, 0, 2).reshape(P, 1024)
    for n, t in ((1, np.cos(sq) * scale), (2, -np.sin(sq) * scale)):
        units[n] = t.reshape(4, P, 512).transpose(1, 0, 2).reshape(P, UNIT)
    return units.astype(np.float32)


_INS = ["x", "c", "ctx", "c_ctx", "ada_w", "ada_b", "post_g", "post_b", "m_w_in", "m_w_conv", "m_b_conv",
        "m_w_q", "m_w_k", "m_w_v", "m_w_gate", "m_b_gate", "m_gn_w", "m_skip", "m_w_out", "f_w_out",
        "mlp_w1", "mlp_w2"]


def kernel(**inputs):
    import concourse.bacc as bacc
    from concourse.bass_utils import run_bass_kernel_spmd

    nc = bacc.Bacc("TRN2", target_bir_lowering=False, num_devices=1)
    arrays = {f"in_{name}": np.ascontiguousarray(inputs[name]) for name in _INS}
    arrays["dft"] = dft_tables()
    args = [nc.dram_tensor(name, a.shape, mybir.dt.from_np(a.dtype), kind="ExternalInput").ap()
            for name, a in arrays.items()]
    out = nc.dram_tensor("out", (1, NL, D), F32, kind="ExternalOutput").ap()
    hybrid_block(nc, *args, out)
    r = run_bass_kernel_spmd(nc, [arrays], core_ids=[0])
    return r.results[0]["out"]
```

```python
from contextlib import ExitStack

import numpy as np

import concourse.bass as bass
from concourse import mybir

F32 = mybir.dt.float32
F32R = mybir.dt.float32r
ALU = mybir.AluOpType
ACT = mybir.ActivationFunctionType

P = 128
D = 1024
NL, NC = 512, 256
NT = NL + NC
KD = D // P
DI = 2048
H, DH = 4, 512
JH = DH // P
ST = NT // P
TT = NL // P
DFF = 4096
GRID = 64
ROWS = NL // GRID
NG = 16
GROUPS = 4
FT = DFF // P // GROUPS
FG = 256
ALPHA = float(4 ** 0.25)
EPS = 1e-5
K_SCALE = float(DH ** -0.5)
UNIT = 2048
KB = 1024

SH1, SC1, G1, SH2, SC2, G2 = range(6)


def vec(layer, v):
    return (layer * 6 + v) * KD


ADA0 = [SH2, SC2, G1, G2]
PAIRS = 8
EARLY = [0, 1]
PAIRS_OF = [[2, 3], [4], [5], [6, 7]]
MODS = [(vec(0, SH2), vec(0, SC2)), (vec(1, SH1), vec(1, SC1)), (vec(1, SH2), vec(1, SC2))]
GATE = [vec(0, G1), vec(0, G2), vec(1, G1), vec(1, G2)]

HEAD = ([("xm", j) for j in range(4)] + [("ada", 0), ("vT", 0), ("vT", 1), ("vN", 0), ("vT", 2), ("vN", 1),
        ("vT", 3), ("vN", 2), ("z", 0), ("vN", 3), ("z", 1), ("z", 2), ("z", 3), ("ada", 1)]
        + [("q", j) for j in range(4)] + [("k", j) for j in range(4)]
        + [("S", 0), ("ada", 2)] + [("S", j) for j in range(1, 6)])
STREAM = [0, None, 1, None, 2, None, 3, 4, None, 5, None, 6, None]
ADA_UNITS = STREAM.count(None)
SLOTS = 3
USES = len(HEAD) // SLOTS
USE = {what: n for n, what in enumerate(HEAD)}
READERS = {"xm": (), "ada": (), "vT": ("turn",), "vN": ("dve",), "z": ("dma",), "S": ("dma",),
           "q": ("pe", "dve"), "k": ("pe", "dve")}


def reads_before(reader, n):
    return sum(reader in READERS[HEAD[m][0]] for m in range(n % SLOTS, n + 1, SLOTS))


def reads_per_head(reader, slot):
    return reads_before(reader, len(HEAD) - SLOTS + slot)


STREAM_P2 = [("w_out", 0, 0)] + [("ada", p, u) for p in EARLY for u in range(2)]
STREAM_P2 += [("w_out", 0, 1)]
for _h in range(H):
    STREAM_P2 += [("ada", p, u) for p in PAIRS_OF[_h] for u in range(2)]
    if _h:
        STREAM_P2 += [("w_out", _h, 0), ("w_out", _h, 1)]
RAW_P1, RAW_P2 = len(STREAM) * H, len(STREAM_P2)
RAW0_P2 = RAW_P1
RAW0_MLP0 = RAW0_P2 + RAW_P2
RAW0_F = RAW0_MLP0 + 8 * GROUPS
RAW0_MLP1 = RAW0_F + 3 + 4
SPLIT0_P2 = 7 * H
SPLIT0_MLP0 = SPLIT0_P2 + 2 * H
SPLIT0_F = SPLIT0_MLP0 + 8 * GROUPS
SPLIT0_MLP1 = SPLIT0_F + 7
POOL_TILES = 2
Y_MLP0, Y_F, Y_MLP1 = 2 * H, 2 * H + 2 * GROUPS, 2 * H + 2 * GROUPS + 2
ADA0_P2 = ADA_UNITS * H


BLOCKS = [8, 8, 5, 5, 5, 5]
START = [sum(BLOCKS[:s]) for s in range(ST)]
BACK, FORTH = 0, 1
NOT_SEEN = 200.0


def pblock(d, s, i):
    return i + d * (4 if s < 2 else 1)


def key_tiles(d, i):
    return [0, 1] + (list(range(2 + i, ST)) if d == BACK else list(range(2, 3 + i)))


LAST_TURN = (2, 0, 1, 2)


def b_order(b):
    out = []
    for step in range(TT + 4):
        out += [("first", step - 1)] * (0 <= step - 1 < TT)
        out += [("second", step - 4)] * (0 <= step - 4 < TT and b < 3)
    return out


def root_order(b):
    out = []
    for step in range(TT + 4):
        out += [("first", step)] * (step < TT)
        out += [("second", step - 3)] * (0 <= step - 3 < TT and b < 3)
    return out


BANK3 = [("ada", p) for p in EARLY] + [("M", 0, BACK), ("M", 0, FORTH)]
for _h in range(H):
    BANK3 += [("den", _h, BACK), ("den", _h, FORTH)]
    if _h + 1 < H:
        BANK3 += [("M", _h + 1, BACK), ("M", _h + 1, FORTH)]
    BANK3 += [("ada", p) for p in PAIRS_OF[_h]]


def bc_use(*what):
    return BANK3.index(what) + 1


def hybrid_block(nc, x, c, ctx, c_ctx, ada_w, ada_b, post_g, post_b, m_w_in, m_w_conv, m_b_conv, m_w_q,
                 m_w_k, m_w_v, m_w_gate, m_b_gate, m_gn_w, m_skip, m_w_out, f_w_out, mlp_w1, mlp_w2,
                 dft, out):
    es = ExitStack()
    with es:
        base = 16512
        region = base + 54 * KB

        def at(name, shape, off_kb, dt=F32):
            return nc.alloc_sbuf_tensor_at(name, shape, dt, offset=int(region + off_kb * KB))

        def fixed(name, shape, off, dt=F32):
            return nc.alloc_sbuf_tensor_at(name, shape, dt, offset=base + off)

        def sem(name):
            return es.enter_context(nc.semaphore(name))

        def sems(name, n):
            return [sem(f"{name}{i}") for i in range(n)]

        raw = fixed("raw", [P, 2, UNIT], 0)
        w_hi = fixed("w_hi", [P, 2, UNIT], 16 * KB, F32R)
        w_lo = fixed("w_lo", [P, 2, UNIT], 32 * KB, F32R)
        o = [48 * KB]

        def const(name, shape):
            n = 4 * int(np.prod(shape[1:]))
            o[0] += (n + 31) // 32 * 32
            assert o[0] <= 54 * KB
            return fixed(name, shape, o[0] - (n + 31) // 32 * 32)

        ident = const("ident", [P, P])
        ones = const("ones", [P, P])

        exp_m = const("exp_m", [P, 2, TT, H])
        den = const("den", [P, 2, TT])
        dena = const("dena", [P, 2, TT])
        asum = const("asum", [P, 2, 256])

        cols = const("cols", [P, 288])
        cvec = const("cvec", [P, 2, KD])
        svec = const("svec", [P, 2, KD])
        mod0 = const("mod0", [P, 2 * KD, 2])
        adac = const("adac", [P, 12 * KD])
        stat = const("stat", [P, 6, 2, 6])
        mv = const("mv", [P, 6, 2])
        eps = const("eps", [P, 1])
        pair_row = const("pair_row", [P, 2])
        std = const("std", [P, 6])
        rstd = const("rstd", [P, 6])
        nmr = const("nmr", [P, 6])
        gcol = const("gcol", [P, 2, ST, H])

        x_in = at("x_in", [P, TT, D], 48)
        c_in = at("c_in", [P, 2, D], 64)
        ada_in = at("ada_in", [P, 4, KD, 512], 72)
        modrow = at("modrow", [2, 2 * D], 24)
        colrow = at("colrow", [P, 3, P], 32)
        ht_hi = at("ht_hi", [P, KD, NT], 0, F32R)
        ht_lo = at("ht_lo", [P, KD, NT], 24, F32R)
        xx_hi = at("xx_hi", [P, JH, NT], 48, F32R)
        xx_lo = at("xx_lo", [P, JH, NT], 60, F32R)
        xm = at("xm", [P, JH, NT], 72)
        q_hi = at("q_hi", [P, JH, NL], 84, F32R)
        q_lo = at("q_lo", [P, JH, NL], 92, F32R)
        k_hi = at("k_hi", [P, JH, NT], 100, F32R)
        k_lo = at("k_lo", [P, JH, NT], 112, F32R)
        tile = at("tile", [P, SLOTS, NT], 124)
        v_st_hi = at("v_st_hi", [P, ST, P], 133, F32R)
        v_st_lo = at("v_st_lo", [P, ST, P], 136, F32R)
        xc = at("xc", [P, 2, NT], 139)
        sx_st = at("sx_st", [P, 2, NL], 145)
        wg = at("wg", [P, 2, 3, JH, NG], 149)
        bg = at("bg", [1, NG], 151)
        pre = at("pre", [NG, NT], 48)
        g_i = at("g_i", [H, 2, NT], 52)
        g_f = at("g_f", [H, 2, NT], 58)
        g_t = at("g_t", [H, 2, NT], 64)
        g_F = at("g_F", [H, 2, NT], 70)
        g_g = at("g_g", [H, 2, NT], 76)
        g_M = at("g_M", [H, 2, NT], 82)
        g_z = at("g_z", [H, NT], 88)
        g_a = at("g_a", [H, 2, NT], 92)
        m_rows = at("m_rows", [P, NL], 144)
        mb = at("mb", [P, 2, NL], 146)
        sel = at("sel", [P, H, P], 150)
        ones_r = at("ones_r", [P, P], 153, F32R)
        mask = at("mask", [P, 2, P], 152)
        y_acc = at("y_acc", [P, TT, D], 0)
        u_hi = at("u_hi", [P, JH, NL], 16, F32R)
        u_lo = at("u_lo", [P, JH, NL], 24, F32R)
        gate_diag = at("gate_diag", [P, KD, P], 32)
        v_hi = at("v_hi", [P, ST, DH], 44, F32R)
        v_lo = at("v_lo", [P, ST, DH], 56, F32R)
        s_in = at("s_in", [P, ST, NL], 68)
        p_hi = at("p_hi", [P, sum(BLOCKS), P], 80, F32R)
        p_lo = at("p_lo", [P, sum(BLOCKS), P], 98, F32R)
        wt = [at(f"wt{n}", [P, 8, P], 32 + 4 * n) for n in range(3)]
        hn = at("hn", [P, 2, TT, DH], 116)
        u3_hi = at("u3_hi", [P, JH, NL], 108, F32R)
        u3_lo = at("u3_lo", [P, JH, NL], 98, F32R)
        zt = at("zt", [P, 3, NL], 132)
        sxt = at("sxt", [P, 3, NL], 138)
        x_nat = at("x_nat", [P, TT, D], 16)
        x_res = at("x_res", [P, TT, D], 80)
        hh_hi = at("hh_hi", [P, KD, NL], 44, F32R)
        hh_lo = at("hh_lo", [P, KD, NL], 60, F32R)
        ff_hi = at("ff_hi", [P, FT, NL], 76, F32R)
        ff_lo = at("ff_lo", [P, FT, NL], 92, F32R)
        gate = at("gate", [P, D], 36)
        rtmp = at("rtmp", [P, 2, NL], 40)
        relu = at("relu", [P, 2, NL], 108)
        sq = at("sq", [P, 2, NL], 112)
        btile = at("btile", [P, 2, NL], 116)
        pg = at("pg", [P, D], 120)
        pbb = at("pbb", [P, D], 124)

        a_hi = at("a_hi", [P, TT, 4, FG], 76, F32R)
        a_lo = at("a_lo", [P, TT, 4, FG], 108, F32R)
        mid_hi = at("mid_hi", [P, TT, P], 92, F32R)
        mid_lo = at("mid_lo", [P, TT, P], 94, F32R)
        folded = at("folded", [P, 2, UNIT], 128)
        ftile = [at("ftile0", [P, NL], 148), at("ftile1", [P, NL], 150)]

        psum = es.enter_context(nc.psum_tensor("psum", [P, 8, 512], F32))

        v_hi_d = nc.dram_tensor("v_hi_d", [H, P, ST, DH], F32, kind="Internal").ap()
        v_lo_d = nc.dram_tensor("v_lo_d", [H, P, ST, DH], F32, kind="Internal").ap()
        s_d = nc.dram_tensor("s_d", [H, ST, P, NL], F32, kind="Internal").ap()
        z_d = nc.dram_tensor("z_d", [DI // P, P, NL], F32, kind="Internal").ap()
        sx_d = nc.dram_tensor("sx_d", [DI // P, P, NL], F32, kind="Internal").ap()

        raw_landed = sems("raw_landed", 2)
        prepared = sem("prepared")
        w_ready = sem("w_ready")
        w_begun = sem("w_begun")
        pool_step = sem("pool_step")
        ada_ready = sem("ada_ready")
        ada_used = sem("ada_used")
        sel_ready = sem("sel_ready")
        consts = sem("consts")
        in_landed = sems("in_landed", 4)
        ada0_landed = sems("ada0_landed", 4)
        silu_c = sem("silu_c")
        mod_sum = sem("mod_sum")
        modrow_done = sem("modrow_done")
        mod_T = sem("mod_T")
        col_T = sem("col_T")
        cols_done = sem("cols_done")
        mod_done = sem("mod_done")
        var_done = sem("var_done")
        std_done = sem("std_done")
        xhat_done = sem("xhat_done")
        x0_full = sems("x0_full", 3)
        x0_tile = sems("x0_tile", 3)
        x0_split = sems("x0_split", 3)
        x0_high = sem("x0_high")
        ht_ready = sems("ht_ready", 2)
        full = sems("full", SLOTS)
        evac = sems("evac", SLOTS)
        aux = sems("aux", SLOTS)
        taken = sems("taken", SLOTS)
        spilled = sems("spilled", SLOTS)
        x_split = sem("x_split")
        qk_split = sem("qk_split")
        conv_done = sem("conv_done")
        xc_done = sem("xc_done")
        xc_high = sem("xc_high")
        sx_done = sem("sx_done")
        sx_spilled = sems("sx_spilled", 2)
        v_split = sem("v_split")
        v_spilled = sem("v_spilled")
        wg_landed = sems("wg_landed", 2)
        wg_used = sem("wg_used")
        bg_landed = sem("bg_landed")
        gates_full = sem("gates_full")
        scans = sem("scans")
        m_landed = sem("m_landed")
        pre_done = sem("pre_done")
        gate_rows = sem("gate_rows")
        abs_f = sem("abs_f")
        soft = sem("soft")
        g_done = sem("g_done")
        gT_full = sem("gT_full")
        m_done = sem("m_done")
        s_landed = sem("s_landed")
        v_landed = sem("v_landed")
        z_landed = sems("z_landed", 3)
        bc_full = sem("bc_full")
        bc_free = sem("bc_free")
        mT_full = sem("mT_full")
        exp_m_done = sem("exp_m_done")
        mb_done = sem("mb_done")
        diag_in = sem("diag_in")
        w_exp = sem("w_exp")
        p_hi_done = sem("p_hi_done")
        p_ready = sem("p_ready")
        den_done = sem("den_done")
        forth_done = sem("forth_done")
        h_rs = sem("h_rs")
        pv_full = sems("pv_full", 2)
        back_done = sem("back_done")
        h_var = sem("h_var")
        h_std = sem("h_std")
        h_norm = sem("h_norm")
        tr_full = sem("tr_full")
        tr_free = sem("tr_free")
        u_done = sem("u_done")
        zu_done = sem("zu_done")
        y_full = sems("y_full", TT)
        y_free = sems("y_free", TT)
        res_landed = sem("res_landed")
        pgb_landed = sem("pgb_landed")
        b_var = sem("b_var")
        b_std = sem("b_std")
        b_stat = sem("b_stat")
        b_norm = sem("b_norm")
        b_g = sem("b_g")
        b_x = sem("b_x")
        b_xhat = sem("b_xhat")
        b_full = sem("b_full")
        b_tile = sem("b_tile")
        b_split = sem("b_split")
        b_cols = sem("b_cols")
        gate_in = sem("gate_in")
        gate_full = sem("gate_full")
        gate_done = sem("gate_done")
        y_zero = sem("y_zero")
        a_full = sems("a_full", 2)
        a_relu = sems("a_relu", 2)
        a_sq = sems("a_sq", 2)
        a_split = sems("a_split", 2)

        heads_summed = sem("heads_summed")
        half_gated = sem("half_gated")
        mid_in = sem("mid_in")
        mid_full = sem("mid_full")
        fold_done = sem("fold_done")
        f_full = sems("f_full", 2)
        f_tile = sems("f_tile", 2)
        f_split = sems("f_split", 2)
        stored = sem("stored")

        def mul3(pe, dst, lh, ll, rh, rl, first, last, begun=None):
            mm = pe.matmul(dst, lh, rh, start=first, stop=False)
            if begun is not None:
                mm.then_inc(begun, 1)
            pe.matmul(dst, lh, rl, start=False, stop=False)
            return pe.matmul(dst, ll, rh, start=False, stop=last)

        def tblk(i, n=P):
            return slice(i * n, (i + 1) * n)

        def u_of(h):
            return (u_hi, u_lo) if h < H - 1 else (u3_hi, u3_lo)

        block = es.enter_context(nc.Block())

        @block.sync
        def _(sp):
            sp.dma_start(cvec[:, 0], c.rearrange("a (p k) -> p (a k)", k=KD)).then_inc(in_landed[0], 16)
            sp.dma_start(cvec[:, 1], c_ctx.rearrange("(p k) -> p k", k=KD)).then_inc(in_landed[0], 16)
            for n in range(4):
                if n == 3:
                    sp.dma_start(x_in[:], x.rearrange("a (i p) d -> p (a i) d", p=P)).then_inc(in_landed[1], 16)
                sp.dma_start(ada_in[:, n], ada_w[0].rearrange("(p k) n -> p k n", k=KD)[:, :, tblk(n, 512)]
                             ).then_inc(ada0_landed[n], 16)
            sp.dma_start(c_in[:], ctx.rearrange("a (i p) d -> p (a i) d", p=P)).then_inc(in_landed[2], 16)
            sp.dma_start(colrow[:, 0], m_w_conv.rearrange("a k l (j p) -> (a k l j) p", p=P)[0:128]
                         ).then_inc(in_landed[3], 16)
            sp.dma_start(colrow[0:16, 1], m_w_conv.rearrange("a k l (j p) -> (a k l j) p", p=P)[128:144]
                         ).then_inc(in_landed[3], 16)
            for n, v in enumerate((m_b_conv, m_gn_w, m_skip)):
                sp.dma_start(colrow[16 + 16 * n:32 + 16 * n, 1], v.rearrange("a (j p) -> (a j) p", p=P)
                             ).then_inc(in_landed[3], 16)
            sp.dma_start(colrow[0:96, 2], ada_b.rearrange("a (j p) -> (a j) p", p=P)
                         ).then_inc(in_landed[3], 16)
            sp.dma_start(bg[:, :], m_b_gate).then_inc(bg_landed, 16)

            def raw_unit(n, slot, src, free=True):
                if free:
                    sp.wait_ge(prepared, n - 1)
                sp.dma_start(raw[:, slot], src).then_inc(raw_landed[slot], 16)

            def ada_unit(layer, col):
                return ada_w[layer].rearrange("(p k) n -> p k n", k=KD)[:, :, bass.ds(col, 256)]

            w_in_v = m_w_in[0].rearrange("(k p) n -> p k n", p=P)

            def head_units(h, hh, n, lead=False):
                def cols_of(start):
                    return w_in_v[:, :, bass.ds(start, 256)]

                def square(w):
                    return w[0][bass.ds(h, 1)].rearrange("a (k p) n -> p (a k) n", p=P)

                sp.wait_ge(wg_used, h + 1)
                for m in range(3):
                    sp.dma_start(wg[:, hh, m], m_w_gate[0, m].rearrange("(j p) n -> p j n", p=P)
                                 [:, bass.ds(h * JH, JH)]).then_inc(wg_landed[hh], 16)
                src = [cols_of(h * DH), cols_of(h * DH + 256), square(m_w_v), cols_of(h * DH + DI),
                       cols_of(h * DH + DI + 256), square(m_w_q), square(m_w_k)]
                for u, what in enumerate(STREAM):
                    a_ = STREAM[:u].count(None)
                    raw_unit(n + u, (len(STREAM) * hh + u) % 2,
                             ada_unit(1, h * (ADA_UNITS * 256) + 256 * a_) if what is None else src[what])

            with sp.Fori(0, H // 2) as it:
                for hh in range(2):
                    head_units(it * 2 + hh, hh, it * (2 * len(STREAM)) + len(STREAM) * hh + 2)

            w_out_v = m_w_out[0].rearrange("(k p) n -> p k n", p=P)
            for u, (what, h, i) in enumerate(STREAM_P2):
                n = RAW0_P2 + u
                raw_unit(n + 2, n % 2, ada_unit(0, ADA0[h // 2] * D + (h % 2 * 2 + i) * 256)
                         if what == "ada" else w_out_v[:, tblk(h, JH), tblk(i, 512)])

            def mlp_units(layer, n0):
                w1 = mlp_w1[layer].rearrange("(k p) n -> p k n", p=P)
                w2 = mlp_w2[layer].rearrange("(k p) n -> p k n", p=P)
                with sp.Fori(0, GROUPS) as g:
                    n = g * 8 + n0 + 2
                    for u in range(4):
                        raw_unit(n + u, (n0 + u) % 2, w1[:, :, bass.ds(g * 1024 + u * 256, 256)])
                    n = n + 4
                    for u in range(4):
                        raw_unit(n + u, (n0 + u) % 2,
                                 w2[:, bass.ds(g * FT + (u % 2) * 4, 4), tblk(u // 2, 512)])

            mlp_units(0, RAW0_MLP0)

            n = RAW0_F
            for u in range(3):
                raw_unit(n + 2, n % 2, dft[u])
                n += 1
            f_v = f_w_out[0].rearrange("(k p) n -> p k n", p=P)
            for u in range(4):
                raw_unit(n + 2, n % 2, f_v[:, tblk(u % 2, 4), tblk(u // 2, 512)])
                n += 1
            mlp_units(1, RAW0_MLP1)

            out_v = out.rearrange("a (i p) d -> p (a i) d", p=P)
            for i in range(TT):
                sp.wait_ge(b_x, 3 * TT + i + 1)
                sp.dma_start(out_v[:, i], x_nat[:, i]).then_inc(stored, 16)
            sp.wait_ge(stored, 16 * TT)

        @block.gpsimd
        def _(pool):
            g = nc.gpsimd
            g.memset(ident[:], 0.0)
            g.memset(ones[:], 1.0)
            g.memset(eps[:], EPS)

            pool.drain()
            g.affine_select(out=ident[:], in_=ident[:], compare_op=ALU.not_equal, fill=1.0, base=0,
                            pattern=[[-1, P]], channel_multiplier=1)

            pool.drain().then_inc(consts, 1)
            pool.wait_ge(consts, 1)
            pool.sem_inc(prepared, 2)
            pool.sem_inc(wg_used, 2)
            pool.sem_inc(ada_used, 2)
            pool.wait_ge(silu_c, 1)

            def split_unit(n, slot, m, wslot, begun=True, fold=None):
                src = raw[:, slot]
                if fold is None:
                    pool.wait_ge(raw_landed[slot], n)
                else:
                    pool.wait_ge(fold_done, fold + 1)
                    src = folded[:, fold % 2]
                if begun:
                    pool.wait_ge(w_begun, m)
                pool.sem_inc(pool_step, 1)
                g.tensor_scalar(w_hi[:, wslot], src, 1.0, 0.0, ALU.mult, ALU.add)
                pool.drain()
                g.tensor_tensor(w_lo[:, wslot], src, w_hi[:, wslot].bitcast(F32), ALU.subtract)
                pool.drain().then_inc(w_ready, 1)
                pool.sem_inc(prepared, 1)

            def ada_unit(landed, slot, par, used):
                pool.wait_ge(raw_landed[slot], landed)
                pool.wait_ge(ada_used, used)
                pool.sem_inc(pool_step, 1)
                part = raw[:, slot].rearrange("p (k n) -> p k n", k=KD)
                g.tensor_tensor(part, part, svec[:, 0].unsqueeze(2).to_broadcast([P, KD, 256]), ALU.mult)
                pool.drain()
                g.tensor_tensor(part[:, 0:4], part[:, 0:4], part[:, 4:8], ALU.add)
                pool.drain()
                g.tensor_tensor(part[:, 0:2], part[:, 0:2], part[:, 2:4], ALU.add)
                pool.drain()
                g.tensor_tensor(asum[:, par], part[:, 0], part[:, 1], ALU.add)
                pool.drain().then_inc(ada_ready, 1)
                pool.sem_inc(prepared, 1)

            def stream_unit(u, it=None):
                what = STREAM[u % len(STREAM)]
                first, m0, a0 = (0, 0, 0) if it is None else (it * (len(STREAM) * 16), it * 14,
                                                              it * (2 * ADA_UNITS))
                landed = first + 16 * (u // 2 + 1)
                a_ = u // len(STREAM) * ADA_UNITS + STREAM[:u % len(STREAM)].count(None)
                if what is None:
                    ada_unit(landed, u % 2, a_ % 2, a0 + a_ + 1)
                else:
                    m = u // len(STREAM) * 7 + what
                    split_unit(landed, u % 2, m0 + m, m % 2)

            stream_unit(0)
            for k in range(1, KD, 2):
                pool.wait_ge(x0_high, k + 1)
                g.tensor_tensor(ht_lo[:, k], tile[:, k % 3], ht_hi[:, k].bitcast(F32), ALU.subtract
                                ).then_inc(x0_split[k % 3], 1)
                pool.drain().then_inc(ht_ready[1], 1)

            with pool.Fori(0, H // 2) as it:
                for u in range(1, 2 * len(STREAM) + 1):
                    stream_unit(u, it)

            def pair(p):
                for u in range(2):
                    n = RAW0_P2 + STREAM_P2.index(("ada", p, u))
                    ada_unit(16 * (n // 2 + 1), n % 2, u, ADA0_P2 + 2 * p + u + 1)

            def w_out_unit(h, half):
                n = RAW0_P2 + STREAM_P2.index(("w_out", h, half))
                m = SPLIT0_P2 + 2 * h + half
                if h:
                    pool.wait_ge(y_full[TT - 1], 2 * (h - 1) + half + 1)
                split_unit(16 * (n // 2 + 1), n % 2, m, m % 2, False)

            for p in EARLY:
                pair(p)
            pool.wait_ge(gates_full, 1)
            g.memset(sel[:], 0.0)
            g.memset(mask[:], 0.0)
            g.tensor_scalar(ones_r[:], ones[:], 1.0, 0.0, ALU.mult, ALU.add)
            pool.drain()
            g.affine_select(out=mask[:, BACK], in_=mask[:, BACK], compare_op=ALU.is_ge, fill=NOT_SEEN,
                            base=0, pattern=[[-1, P]], channel_multiplier=1)
            g.affine_select(out=mask[:, FORTH], in_=mask[:, FORTH], compare_op=ALU.is_ge, fill=NOT_SEEN,
                            base=0, pattern=[[1, P]], channel_multiplier=-1)
            for q in range(2):
                pool.drain()
                g.affine_select(out=sel[32 * q:32 * q + 32], in_=sel[32 * q:32 * q + 32],
                                compare_op=ALU.not_equal, fill=1.0, base=0,
                                pattern=[[-1, H], [0, P]], channel_multiplier=1)
            pool.drain().then_inc(sel_ready, 1)



            def products_lo(h):
                for s in range(ST):
                    n = ST * h + s
                    part = slice(START[s], START[s] + BLOCKS[s])
                    pool.wait_ge(p_hi_done, n + 1)
                    g.tensor_tensor(p_lo[:, part], wt[n % 3][:, 0:BLOCKS[s]], p_hi[:, part].bitcast(F32),
                                    ALU.subtract)
                    pool.drain().then_inc(p_ready, 1)

            w_out_unit(0, 1)
            products_lo(0)
            for h in range(H):
                for p in PAIRS_OF[h]:
                    pair(p)
                if h + 1 < H:
                    products_lo(h + 1)
                if h:
                    w_out_unit(h, 0)
                    w_out_unit(h, 1)

            def boundary(b):
                pool.wait_ge(pgb_landed, 32 * (b + 1))
                for i in range(TT):
                    if i < POOL_TILES:
                        pool.wait_ge(b_norm, TT * b + i + 1)
                        g.tensor_tensor(y_acc[:, i], y_acc[:, i], pg[:], ALU.mult)
                        pool.drain()
                    else:
                        pool.wait_ge(b_g, (TT - POOL_TILES) * b + i - POOL_TILES + 1)
                    g.tensor_tensor(x_nat[:, i], y_acc[:, i], pbb[:], ALU.add)
                    pool.drain().then_inc(b_x, 1)
                if b in (0, 2):
                    pool.wait_ge(b_full, KD * (b + 1))
                    g.memset(y_acc[:], 0.0)
                    pool.drain().then_inc(y_zero, 1)

            def split_next(u, gr=None):
                n, m = RAW0_MLP0 + u, SPLIT0_MLP0 + u
                if gr is None:
                    f_unit = n - (RAW0_F + 3)
                    split_unit(16 * (n // 2 + 1), n % 2, m, m % 2, fold=f_unit if 0 <= f_unit < 4 else None)
                else:
                    split_unit(gr * 64 + 16 * (n // 2 + 1), n % 2, gr * 8 + m, m % 2)

            pool.wait_ge(gate_done, 1)
            pool.wait_ge(heads_summed, 1)
            for i in range(TT):
                g.tensor_tensor(y_acc[:, i, tblk(1, 512)], y_acc[:, i, tblk(1, 512)], gate[:, tblk(1, 512)],
                                ALU.mult)
            pool.drain().then_inc(half_gated, 1)
            split_next(0)
            boundary(0)
            with pool.Fori(0, GROUPS) as gr:
                for u in range(1, 9):
                    split_next(u, gr)
            boundary(1)
            u0 = 8 * GROUPS + 7
            for u in range(8 * GROUPS + 1, u0 + 1):
                split_next(u)
            boundary(2)
            with pool.Fori(0, GROUPS - 1) as gr:
                for u in range(1, 9):
                    split_next(u0 + u, gr)
            for u in range(1, 8):
                split_next(u0 + 8 * (GROUPS - 1) + u)
            boundary(3)

        @block.tensor
        def _(pe):
            pe.wait_ge(silu_c, 1)
            for n in range(4):
                pe.wait_ge(ada0_landed[n], 16)
                for k in range(KD):
                    mm = pe.matmul(psum[0:2, n, :], svec[:, :, k], ada_in[:, n, k], start=(k == 0),
                                   stop=(k == KD - 1))
                mm.then_inc(mod_sum, 1)
            pe.wait_ge(consts, 1)
            pe.wait_ge(in_landed[3], 96)
            pe.transpose(psum[:, 7, 0:128], colrow[:, 0], ident[:])
            pe.transpose(psum[:, 7, 128:192], colrow[0:64, 1], ident[0:64, 0:64])
            pe.transpose(psum[:, 7, 192:288], colrow[0:96, 2], ident[0:96, 0:96]).then_inc(col_T, 1)
            pe.wait_ge(modrow_done, 4)
            for j in range(2 * KD):
                mm = pe.transpose(psum[:, 6, 2 * j:2 * j + 2], modrow[0:2, tblk(j)], ident[0:2, 0:2])
            mm.then_inc(mod_T, 1)
            pe.wait_ge(xhat_done, 1)
            for k in range(KD):
                r = k % 3
                if k >= 3:
                    pe.wait_ge(x0_tile[r], k // 3)
                for i in range(TT):
                    pe.transpose(psum[:, 2 * r, tblk(i)], x_in[:, i, tblk(k)], ident[:])
                for i in range(2):
                    mm = pe.transpose(psum[:, 2 * r + 1, tblk(i)], c_in[:, i, tblk(k)], ident[:])
                mm.then_inc(x0_full[r], 1)

            pe.wait_ge(bg_landed, 16)
            pe.wait_ge(cols_done, 1)
            pe.wait_ge(mod_done, 1)
            pe.wait_ge(x0_tile[1], 3)
            pe.matmul(psum[0:NG, 6, 0:128], bg[0:1, :], ones[0:1, :], start=True, stop=False,
                      skip_group_check=True)
            for i in range(1, 4):
                pe.matmul(psum[0:NG, 6, tblk(i)], bg[0:1, :], ones[0:1, :], start=False, stop=False,
                          skip_group_check=True)
            pe.matmul(psum[0:NG, 7, 0:128], bg[0:1, :], ones[0:1, :], start=True, stop=False,
                      skip_group_check=True)
            pe.matmul(psum[0:NG, 7, 128:256], bg[0:1, :], ones[0:1, :], start=False, stop=False,
                      skip_group_check=True)
            def slot_of(what, h):
                n = USE[what]
                pe.wait_ge(evac[n % SLOTS], h * USES + n // SLOTS)
                return n % SLOTS

            def expand(what, h, slot, col, rh, rl, kt, ctx_too, begun=None):
                r = slot_of(what, h)
                wh = w_hi[:, slot].rearrange("p (k n) -> p k n", k=kt)
                wl = w_lo[:, slot].rearrange("p (k n) -> p k n", k=kt)
                for k in range(kt):
                    if what == ("xm", 0):
                        pe.wait_ge(ht_ready[k % 2], k // 2 + 1)
                    elif what == ("vT", 0):
                        pe.wait_ge(x_split, h * 8 + k + 1)
                    elif what == ("q", 0):
                        pe.wait_ge(x_split, h * 8 + JH + k + 1)
                    mm = mul3(pe, psum[:, 2 * r, :], wh[:, k, tblk(col)], wl[:, k, tblk(col)],
                              rh[:, k, NC:NT], rl[:, k, NC:NT], k == 0, k == kt - 1,
                              begun if k == 0 else None)
                if ctx_too:
                    for k in range(kt):
                        mm = mul3(pe, psum[:, 2 * r + 1, 0:NC], wh[:, k, tblk(col)], wl[:, k, tblk(col)],
                                  rh[:, k, 0:NC], rl[:, k, 0:NC], k == 0, k == kt - 1)
                mm.then_inc(full[r], 1)
                return mm

            def unit_ready(m):
                pe.wait_ge(w_ready, m + 1)

            def gate(kind, j, h, hh):
                what = ("vT" if kind == 2 else "qk"[kind], j)
                n = USE[what]
                r = n % SLOTS
                pe.wait_ge(evac[r], h * USES + n // SLOTS + 1)
                pe.matmul(psum[0:NG, 6, :], wg[:, hh, kind, j], tile[:, r, NC:NT], start=False, stop=False,
                          skip_group_check=True)
                mm = pe.matmul(psum[0:NG, 7, 0:NC], wg[:, hh, kind, j], tile[:, r, 0:NC], start=False,
                               stop=False, skip_group_check=True)
                if kind < 2:
                    mm.then_inc(aux[r], 1)

            def turn_v(j, h):
                r = slot_of(("vN", j), h)
                src = USE[("vT", j)] % SLOTS
                for s in range(ST):
                    bank, at_ = (2 * r, s - 2) if s >= 2 else (2 * r + 1, s)
                    mm = pe.transpose(psum[:, bank, tblk(at_)], tile[:, src, tblk(s)], ident[:])
                mm.then_inc(full[r], 1)

            def ada_columns(i, h):
                r = slot_of(("ada", i), h)
                for u in range(2):
                    pe.wait_ge(ada_ready, h * ADA_UNITS + 2 * i + u + 1)
                    for b_ in range(2):
                        mm = pe.matmul(psum[:, 2 * r, 2 * u + b_:2 * u + b_ + 1], asum[:, u, tblk(b_)],
                                       ones[:, 0:1], start=True, stop=True)
                    mm.then_inc(ada_used, 1)
                pe.drain().then_inc(full[r], 1)

            with pe.Fori(0, H // 2) as it:
                for hh in range(2):
                    h = it * 2 + hh
                    m0 = it * 14 + 7 * hh
                    sl = [(7 * hh + u) % 2 for u in range(7)]
                    for u in range(2):
                        unit_ready(m0 + u)
                        for c2 in range(2):
                            expand(("xm", 2 * u + c2), h, sl[u], c2, ht_hi, ht_lo, KD, True,
                                   w_begun if c2 == 0 else None)
                    ada_columns(0, h)
                    unit_ready(m0 + 2)
                    pe.wait_ge(wg_landed[hh], it * 48 + 48)
                    for j in range(JH):
                        expand(("vT", j), h, sl[2], j, xx_hi, xx_lo, JH, True, w_begun if j == 0 else None)
                        if j >= 1:
                            gate(2, j - 1, h, hh)
                            turn_v(j - 1, h)
                    for u in range(2):
                        unit_ready(m0 + 3 + u)
                        for c2 in range(2):
                            expand(("z", 2 * u + c2), h, sl[3 + u], c2, ht_hi, ht_lo, KD, False,
                                   w_begun if c2 == 0 else None)
                            if u == 0 and c2 == 0:
                                gate(2, 3, h, hh)
                                turn_v(3, h)
                    ada_columns(1, h)
                    unit_ready(m0 + 5)
                    for j in range(JH):
                        expand(("q", j), h, sl[5], j, xx_hi, xx_lo, JH, True, w_begun if j == 0 else None)
                        if j >= 1:
                            gate(0, j - 1, h, hh)
                    unit_ready(m0 + 6)
                    for j in range(JH):
                        expand(("k", j), h, sl[6], j, xx_hi, xx_lo, JH, True, w_begun if j == 0 else None)
                        gate(1, j - 1, h, hh) if j >= 1 else gate(0, 3, h, hh)
                    for s in range(ST):
                        r = slot_of(("S", s), h)
                        for k in range(JH):
                            if s == 0:
                                pe.wait_ge(qk_split, h * 8 + JH + k + 1)
                            mm = mul3(pe, psum[:, 2 * r, :], k_hi[:, k, tblk(s)], k_lo[:, k, tblk(s)],
                                      q_hi[:, k], q_lo[:, k], k == 0, k == JH - 1,
                                      wg_used if s == 1 and k == 0 else None)
                        mm.then_inc(full[r], 1)
                        if s == 0:
                            gate(1, 3, h, hh)
                            ada_columns(2, h)
            pe.drain().then_inc(gates_full, 1)

            def bc_bank(use):
                if use > 1:
                    pe.wait_ge(bc_free, use - 1)

            def ada_pair(p):
                bc_bank(bc_use("ada", p))
                for u in range(2):
                    pe.wait_ge(ada_ready, ADA0_P2 + 2 * p + u + 1)
                    for b_ in range(2):
                        mm = pe.matmul(psum[:, 3, 2 * u + b_:2 * u + b_ + 1], asum[:, u, tblk(b_)],
                                       ones[:, 0:1], start=True, stop=True)
                    mm.then_inc(ada_used, 1)
                pe.drain().then_inc(bc_full, 1)

            ada_pair(0)
            ada_pair(1)
            pe.wait_ge(g_done, 1)
            for d in range(2):
                for s in range(ST):
                    mm = pe.transpose(psum[:, 0, (d * ST + s) * H:(d * ST + s + 1) * H],
                                      g_g[0:H, 1 - d, tblk(s)], ident[0:H, 0:H])
            mm.then_inc(gT_full, 1)
            pe.wait_ge(scans, 1)
            for d in range(2):
                for i in range(TT):
                    c0 = (d * TT + i) * H
                    mm = pe.transpose(psum[:, 1, c0:c0 + H], g_F[0:H, 1 - d, NC + i * P:NC + i * P + P],
                                      ident[0:H, 0:H])
            mm.then_inc(mT_full, 1)
            pe.wait_ge(m_landed, 32)
            pe.wait_ge(sel_ready, 1)

            def spread_m(h, d):
                bc_bank(bc_use("M", h, d))
                pe.matmul(psum[:, 3, :], sel[32 * d:32 * d + H, h], m_rows[32 * d:32 * d + H, :], start=True,
                          stop=True).then_inc(bc_full, 1)

            def denominators(h, d):
                bc_bank(bc_use("den", h, d))
                for s in range(ST):
                    i0, i1 = (0, TT) if s < 2 else ((0, s - 1) if d == BACK else (s - 2, TT))
                    b0 = START[s] + pblock(d, s, i0)
                    for p_ in (p_hi, p_lo):
                        mm = pe.matmul(psum[:, 3, i0 * P:i1 * P], ones_r[:],
                                       p_[:, b0:b0 + i1 - i0].rearrange("p b t -> p (b t)"),
                                       start=(s == 0 and p_ is p_hi), stop=(s == ST - 1 and p_ is p_lo),
                                       skip_group_check=True)
                mm.then_inc(bc_full, 1)



            def contract(lh, ll, k0, slot, uses, first=True, last=True):
                wh = w_hi[:, slot].rearrange("p (k n) -> p k n", k=4)
                wl = w_lo[:, slot].rearrange("p (k n) -> p k n", k=4)
                for i in range(TT):
                    if first and uses is not None:
                        pe.wait_ge(y_free[i], uses)
                    for k in range(4):
                        mm = mul3(pe, psum[:, 4 + i, :], lh[:, k0 + k, tblk(i)], ll[:, k0 + k, tblk(i)],
                                  wh[:, k], wl[:, k], first and k == 0, last and k == 3,
                                  w_begun if i == 0 and k == 0 else None)
                    if last:
                        mm.then_inc(y_full[i], 1)

            def turn_h(h, e):
                pe.wait_ge(h_norm, h + 1)
                bank = 2
                if h == H - 1:
                    bank = LAST_TURN[e]
                    pe.wait_ge(back_done, TT * H)
                    pe.wait_ge(forth_done, TT * H)
                if bank == 2 and h == H - 1:
                    pe.wait_ge(tr_free, h * JH + (1 if e else 0))
                elif bank == 2 and h:
                    pe.wait_ge(tr_free, h * JH + e)
                elif bank == 2 and e:
                    pe.wait_ge(tr_free, e)
                for i in range(TT):
                    mm = pe.transpose(psum[:, bank, tblk(i)], hn[:, h % 2, i, tblk(e)], ident[:])
                mm.then_inc(tr_full, 1)

            def attend(h, i):
                for d in (FORTH, BACK):
                    if h or i:
                        pe.wait_ge(back_done if d == BACK else forth_done, TT * h + i)
                    keys = key_tiles(d, i)
                    for s in keys:
                        at_ = START[s] + pblock(d, s, i)
                        mm = mul3(pe, psum[:, d, :], p_hi[:, at_], p_lo[:, at_], v_hi[:, s], v_lo[:, s],
                                  s == keys[0], s == keys[-1])
                    mm.then_inc(pv_full[d], 1)

            def project(h, half):
                pe.wait_ge(u_done, h + 1)
                unit_ready(SPLIT0_P2 + 2 * h + half)
                contract(*u_of(h), 0, (SPLIT0_P2 + 2 * h + half) % 2, 2 * h + half or None)

            def gate_row(b):
                pe.wait_ge(gate_in, b + 1)
                bank = 0 if b == 0 else 2
                if b == 0:
                    pe.wait_ge(tr_free, JH * H)
                for half in range(2):
                    mm = pe.matmul(psum[:, bank + half, :], ones[:],
                                   gate_diag[:, tblk(half, 4)].rearrange("p k n -> p (k n)"),
                                   start=True, stop=True)
                mm.then_inc(gate_full, 1)

            spread_m(0, 0)
            spread_m(0, 1)
            for h in range(H):
                pe.wait_ge(p_ready, ST * (h + 1))
                denominators(h, BACK)
                if h:
                    turn_h(h - 1, 0)
                denominators(h, FORTH)
                pe.wait_ge(v_landed, 32 * (h + 1))
                for i in range(TT):
                    if h and i:
                        turn_h(h - 1, i)
                    attend(h, i)
                    if h + 1 < H and i < 2:
                        spread_m(h + 1, i)
                    if h == 0 and i == 1:
                        ada_pair(PAIRS_OF[0][0])
                ada_pair(PAIRS_OF[h][1 if h == 0 else 0])
                if h:
                    project(h - 1, 0)
                    if h == H - 1:
                        for e in range(JH):
                            turn_h(h, e)
                    project(h - 1, 1)
            gate_row(0)
            ada_pair(PAIRS - 1)
            project(H - 1, 0)
            project(H - 1, 1)

            def boundary(b):
                for i in range(TT):
                    pe.wait_ge(b_xhat, TT * b + i + 1)
                    for k in range(KD):
                        mm = pe.transpose(psum[:, k, tblk(i)], y_acc[:, i, tblk(k)], ident[:])
                        if i == TT - 1:
                            mm.then_inc(b_full, 1)
                pe.wait_ge(b_tile, KD * b + 4)
                gate_row(b + 1)

            def mlp(layer, m0, y0):
                with pe.Fori(0, GROUPS) as gr:
                    for u in range(4):
                        slot = (m0 + u) % 2
                        wh = w_hi[:, slot].rearrange("p (k n) -> p k n", k=KD)
                        wl = w_lo[:, slot].rearrange("p (k n) -> p k n", k=KD)
                        unit_ready(gr * 8 + m0 + u)
                        for c2 in range(2):
                            pe.wait_ge(a_relu[c2], gr * 4 + layer * 16 + u)
                            for k in range(KD):
                                if u == 0 and c2 == 0:
                                    pe.wait_ge(b_split, KD * 2 * layer + k + 1)
                                mm = mul3(pe, psum[:, c2, :], wh[:, k, tblk(c2)], wl[:, k, tblk(c2)],
                                          hh_hi[:, k], hh_lo[:, k], k == 0, k == KD - 1,
                                          w_begun if c2 == 0 and k == 0 else None)
                            mm.then_inc(a_full[c2], 1)
                    for u in range(4):
                        unit_ready(gr * 8 + m0 + 4 + u)
                        if u < 2:
                            pe.wait_ge(a_split[0], gr * 4 + layer * 16 + 2 * (u + 1))
                            pe.wait_ge(a_split[1], gr * 4 + layer * 16 + 2 * (u + 1))
                        contract(ff_hi, ff_lo, (u % 2) * 4, (m0 + u) % 2, gr * 2 + y0 + u // 2, u % 2 == 0,
                                 u % 2 == 1)

            boundary(0)
            mlp(0, SPLIT0_MLP0, Y_MLP0)
            boundary(1)

            m = SPLIT0_F
            unit_ready(m)
            s0 = m % 2
            n = 0
            for gr in range(4):
                pe.wait_ge(b_split, KD + 2 * gr + 2)
                for i in range(TT):
                    if n >= 2:
                        pe.wait_ge(f_tile[n % 2], n // 2)
                    for k in range(2):
                        mm = mul3(pe, psum[:, n % 2, 0:FG], hh_hi[:, 2 * gr + k, tblk(i)],
                                  hh_lo[:, 2 * gr + k, tblk(i)], w_hi[:, s0, tblk(k, FG)],
                                  w_lo[:, s0, tblk(k, FG)], k == 0, k == 1,
                                  w_begun if n == 0 and k == 0 else None)
                    mm.then_inc(f_full[n % 2], 1)
                    n += 1
            unit_ready(m + 1)
            pe.wait_ge(f_split[0], 8)
            pe.wait_ge(f_split[1], 8)
            pe.wait_ge(gate_done, 3)
            pe.wait_ge(mid_in, 1)
            sl = (m + 1) % 2
            for i in range(TT):
                mm = mul3(pe, psum[:, 3, :], mid_hi[:, i], mid_lo[:, i],
                          w_hi[:, sl, tblk(i, 512)], w_lo[:, sl, tblk(i, 512)], i == 0, i == TT - 1,
                          w_begun if i == 0 else None)
            mm.then_inc(mid_full, 1)
            for gr in range(4):
                for part in range(2):
                    n = 16 + 2 * gr + part
                    sl = (m + 1 + part) % 2
                    if n == 17:
                        unit_ready(m + 2)
                    pe.wait_ge(f_tile[n % 2], n // 2)
                    for i in range(TT):
                        mm = mul3(pe, psum[:, n % 2, :], a_hi[:, i, gr, tblk(part)], a_lo[:, i, gr, tblk(part)],
                                  w_hi[:, sl, tblk(i, 512)], w_lo[:, sl, tblk(i, 512)], i == 0, i == TT - 1,
                                  w_begun if n == 23 and i == 0 else None)
                    mm.then_inc(f_full[n % 2], 1)
            pe.wait_ge(f_split[0], 12)
            pe.wait_ge(f_split[1], 12)
            for u in range(4):
                unit_ready(m + 3 + u)
                contract(hh_hi, hh_lo, (u % 2) * 4, (m + 3 + u) % 2, Y_F + u // 2, u % 2 == 0, u % 2 == 1)
            boundary(2)
            mlp(1, SPLIT0_MLP1, Y_MLP1)

        @block.scalar
        def _(act):
            a = nc.scalar

            act.wait_ge(in_landed[0], 32)
            a.activation(svec[:], cvec[:], ACT.Silu).then_inc(silu_c, 1)
            for n in range(4):
                if n == 3:
                    for m, part in enumerate((slice(0, TT), slice(TT, ST))):
                        act.wait_ge(var_done, m + 1)
                        a.activation(std[:, part], std[:, part], ACT.Sqrt).then_inc(std_done, 1)
                act.wait_ge(mod_sum, n + 1)
                a.copy(modrow[0:2, tblk(n, 512)], psum[0:2, n, :]).then_inc(modrow_done, 1)
            act.wait_ge(mod_done, 1)
            for k in range(KD):
                r = k % 3
                act.wait_ge(x0_full[r], k // 3 + 1)
                if k >= 3:
                    act.wait_ge(x0_split[r], k // 3)
                a.activation(tile[:, r, NC:NT], psum[:, 2 * r, :], ACT.Identity,
                             scale=mod0[:, KD + k, 0:1], bias=mod0[:, k, 0:1])
                a.activation(tile[:, r, 0:NC], psum[:, 2 * r + 1, 0:NC], ACT.Identity,
                             scale=mod0[:, KD + k, 1:2], bias=mod0[:, k, 1:2]).then_inc(x0_tile[r], 1)

            for r in range(2):
                act.wait_ge(ht_ready[r], KD // 2)

            def stage_tile(what, h):
                n = USE[what]
                r = n % SLOTS
                act.wait_ge(full[r], h * USES + n // SLOTS + 1)
                if what[0] == "ada":
                    a.copy(adac[:, bass.ds(h * (2 * ADA_UNITS) + vec(1, 0) + 4 * what[1], 4)],
                           psum[:, 2 * r, 0:4]).then_inc(evac[r], 1)
                    return n, r
                if what[0] == "xm":
                    act.wait_ge(conv_done, h * JH)
                else:
                    prev = n - SLOTS
                    while prev >= 0 and HEAD[prev][0] in ("xm", "ada"):
                        prev -= SLOTS
                    for reader, s, w in (("pe", aux, 1), ("dve", taken, 1), ("dma", spilled, 16)):
                        if reader in READERS[HEAD[prev][0]]:
                            act.wait_ge(s[r], h * (w * reads_per_head(reader, r))
                                        + w * reads_before(reader, prev))
                    if HEAD[prev][0] == "vT":
                        t = USE[("vN", HEAD[prev][1])]
                        act.wait_ge(full[t % SLOTS], h * USES + t // SLOTS + 1)
                dst = xm[:, what[1]] if what[0] == "xm" else tile[:, r]
                lat_only = what[0] in ("z", "S")
                if what[0] == "z":
                    op = a.activation(dst[:, NC:NT], psum[:, 2 * r, :], ACT.Silu)
                elif lat_only:
                    op = a.copy(dst[:, NC:NT], psum[:, 2 * r, :])
                else:
                    scale = K_SCALE if what[0] == "k" else 1.0
                    high = {"xm": xx_hi, "q": q_hi, "k": k_hi}.get(what[0])
                    if high is not None:
                        off = NC if what[0] == "q" else 0
                        a.activation(high[:, what[1], NC - off:NT - off], psum[:, 2 * r, :], ACT.Copy,
                                     scale=scale)
                        if what[0] != "q":
                            a.activation(high[:, what[1], 0:NC], psum[:, 2 * r + 1, 0:NC], ACT.Copy,
                                         scale=scale)
                    a.activation(dst[:, NC:NT], psum[:, 2 * r, :], ACT.Copy, scale=scale)
                    op = a.activation(dst[:, 0:NC], psum[:, 2 * r + 1, 0:NC], ACT.Copy, scale=scale)
                op.then_inc(evac[r], 1)
                return n, r

            def spill(n, r, h, dst):
                act.wait_ge(evac[r], h * USES + n // SLOTS + 1)
                act.dma_start(dst, tile[:, r, NC:NT]).then_inc(spilled[r], 16)

            def spill_v(j, h):
                act.wait_ge(v_split, h * JH + j + 1)
                for st_, d_ in ((v_st_hi, v_hi_d), (v_st_lo, v_lo_d)):
                    act.dma_start(d_[bass.ds(h, 1)].rearrange("a p s e -> p (a s) e")[:, :, tblk(j)],
                                  st_[:].bitcast(F32)).then_inc(v_spilled, 16)

            def gate_x(j, h):
                act.wait_ge(conv_done, h * JH + j + 1)
                a.activation(xc[:, j % 2], xc[:, j % 2], ACT.Silu).then_inc(xc_done, 1)
                act.wait_ge(xc_done, h * JH + j + 1)
                act.wait_ge(sx_spilled[j % 2], h * 32 + 16 * (j // 2))
                a.activation(sx_st[:, j % 2], xc[:, j % 2, NC:NT], ACT.Copy,
                             scale=cols[:, bass.ds(h * JH + 176 + j, 1)]).then_inc(sx_done, 1)
                act.wait_ge(sx_done, h * JH + j + 1)
                act.dma_start(sx_d[bass.ds(h * JH + j, 1)].rearrange("a p t -> p (a t)"), sx_st[:, j % 2]
                              ).then_inc(sx_spilled[j % 2], 16)
                n = USE[("vT", 3)]
                act.wait_ge(full[n % SLOTS], h * USES + n // SLOTS + 1)
                a.copy(xx_hi[:, j], xc[:, j % 2]).then_inc(xc_high, 1)

            def z_out(j, h):
                n, r = stage_tile(("z", j), h)
                spill(n, r, h, z_d[bass.ds(h * JH + j, 1)].rearrange("a p t -> p (a t)"))

            with act.Fori(0, H // 2) as it:
                for hh in range(2):
                    h = it * 2 + hh
                    for what in HEAD[0:10]:
                        stage_tile(what, h)
                    spill_v(0, h)
                    stage_tile(("vT", 3), h)
                    gate_x(0, h)
                    spill_v(1, h)
                    stage_tile(("vN", 2), h)
                    gate_x(1, h)
                    z_out(0, h)
                    stage_tile(("vN", 3), h)
                    spill_v(2, h)
                    gate_x(2, h)
                    z_out(1, h)
                    z_out(2, h)
                    gate_x(3, h)
                    spill_v(3, h)
                    z_out(3, h)
                    stage_tile(("ada", 1), h)
                    for j in range(JH):
                        stage_tile(("q", j), h)
                    for j in range(JH):
                        stage_tile(("k", j), h)
                    for s in range(ST):
                        n, r = stage_tile(("S", s), h)
                        spill(n, r, h, s_d[bass.ds(h, 1), s].rearrange("a p t -> p (a t)"))
                        if s == 0:
                            stage_tile(("ada", 2), h)

            act.wait_ge(gates_full, 1)
            a.copy(pre[:, NC:NT], psum[0:NG, 6, :])
            a.copy(pre[:, 0:NC], psum[0:NG, 7, 0:NC]).then_inc(pre_done, 1)
            act.wait_ge(pre_done, 1)
            for d in range(2):
                act.dma_start(g_i[:, d], pre[8 * d:8 * d + 4, :]).then_inc(gate_rows, 16)
                act.dma_start(g_f[:, d], pre[8 * d + 4:8 * d + 8, :]).then_inc(gate_rows, 16)

            def take_ada(p):
                act.wait_ge(bc_full, bc_use("ada", p))
                c0 = vec(0, ADA0[p // 2]) + p % 2 * 4
                a.copy(adac[:, c0:c0 + 4], psum[:, 3, 0:4]).then_inc(bc_free, 1)

            take_ada(0)
            act.wait_ge(abs_f, 1)
            a.activation(g_t[:], g_a[:], ACT.Exp, scale=-1.0).then_inc(soft, 1)
            act.wait_ge(soft, 1)
            a.activation(g_t[:], g_t[:], ACT.Ln, bias=1.0).then_inc(soft, 1)

            def load_s(h):
                if h:
                    act.wait_ge(p_hi_done, ST * h)
                act.dma_start(s_in[:], s_d[h].rearrange("s p t -> p s t")).then_inc(s_landed, 16)

            def load_v(h):
                if h:
                    act.wait_ge(pv_full[BACK], TT * h)
                act.dma_start(v_hi[:].bitcast(F32), v_hi_d[h]).then_inc(v_landed, 16)
                act.dma_start(v_lo[:].bitcast(F32), v_lo_d[h]).then_inc(v_landed, 16)

            def load_z(n):
                if n >= 3:
                    act.wait_ge(zu_done, n - 2)
                act.dma_start(zt[:, n % 3], z_d[n]).then_inc(z_landed[n % 3], 16)
                act.dma_start(sxt[:, n % 3], sx_d[n]).then_inc(z_landed[n % 3], 16)

            for r in range(SLOTS):
                act.wait_ge(spilled[r], 16 * H * reads_per_head("dma", r))
            for r in range(2):
                act.wait_ge(sx_spilled[r], 32 * H)
            act.wait_ge(v_spilled, 32 * JH * H)
            act.wait_ge(scans, 1)
            for d, scan_d in ((BACK, 1), (FORTH, 0)):
                act.dma_start(m_rows[32 * d:32 * d + H, :], g_M[:, scan_d, NC:NT]).then_inc(m_landed, 16)
            take_ada(1)
            act.wait_ge(mT_full, 1)
            a.activation(exp_m[:].rearrange("p d i h -> p (d i h)"), psum[:, 1, 0:2 * TT * H], ACT.Exp,
                         scale=-1.0).then_inc(exp_m_done, 1)
            act.wait_ge(m_done, 1)
            act.wait_ge(m_landed, 32)
            load_s(0)
            load_v(0)
            load_z(0)
            load_z(1)

            def take_m(h, d):
                act.wait_ge(bc_full, bc_use("M", h, d))
                a.copy(mb[:, d], psum[:, 3, :]).then_inc(bc_free, 1)
                act.drain().then_inc(mb_done, 1)

            def weights(h, s):
                n = ST * h + s
                if n >= 3:
                    act.wait_ge(p_ready, n - 2)
                w = wt[n % 3][:].rearrange("p b t -> p (b t)")
                jj = s - 2
                if s >= 2:
                    act.wait_ge(diag_in, 4 * h + jj + 1)
                    a.activation(w[:, jj * P:(jj + 2) * P], w[:, jj * P:(jj + 2) * P], ACT.Exp, scale=-1.0)
                for d, t0, t1 in (((BACK, 0, NL), (FORTH, 0, NL)) if s < 2
                                  else ((BACK, 0, jj * P), (FORTH, (jj + 1) * P, NL))):
                    if t0 < t1:
                        w0 = P * pblock(d, s, 0)
                        a.activation(w[:, w0 + t0:w0 + t1], mb[:, d, t0:t1], ACT.Exp, scale=-1.0,
                                     bias=gcol[:, d, s, h:h + 1])
                act.drain().then_inc(w_exp, 1)

            take_m(0, 0)
            take_m(0, 1)
            for s in range(ST):
                weights(0, s)
            for h in range(H):
                act.wait_ge(den_done, h + 1)
                if h + 1 < H:
                    load_s(h + 1)
                for i in range(TT):
                    act.wait_ge(pv_full[FORTH], TT * h + i + 1)
                    a.activation(hn[:, h % 2, i], psum[:, FORTH, :], ACT.Copy, scale=den[:, FORTH, i:i + 1]
                                 ).then_inc(forth_done, 1)
                    if h:
                        load_z(4 * (h - 1) + i + 2)
                    if h + 1 < H:
                        if i < 2:
                            take_m(h + 1, i)
                        elif i == 2:
                            weights(h + 1, 0)
                            weights(h + 1, 1)
                    if h == 0 and i == 1:
                        take_ada(PAIRS_OF[0][0])
                if h + 1 < H:
                    load_v(h + 1)
                take_ada(PAIRS_OF[h][1 if h == 0 else 0])
                act.wait_ge(h_var, h + 1)
                a.activation(std[:, 0:TT], std[:, 0:TT], ACT.Sqrt).then_inc(h_std, 1)

                if h + 1 < H:
                    for s in range(2, ST):
                        weights(h + 1, s)
                act.wait_ge(h_rs, h + 1)
                for i in range(TT):
                    a.activation(hn[:, h % 2, i], hn[:, h % 2, i], ACT.Identity, scale=rstd[:, i:i + 1],
                                 bias=nmr[:, i:i + 1])
                act.drain().then_inc(h_norm, 1)
            act.wait_ge(pv_full[BACK], TT * H)
            act.dma_start(x_res[:], x.rearrange("a (i p) d -> p (a i) d", p=P)).then_inc(res_landed, 16)
            load_z(H * JH - 2)
            load_z(H * JH - 1)

            def boundary_loads(b):
                act.dma_start(pg[:], post_g[b // 2, b % 2:b % 2 + 1, :].to_broadcast([P, D])
                              ).then_inc(pgb_landed, 16)
                act.dma_start(pbb[:], post_b[b // 2, b % 2:b % 2 + 1, :].to_broadcast([P, D])
                              ).then_inc(pgb_landed, 16)

            def take_gate(b):
                bank = 0 if b == 0 else 2
                act.wait_ge(gate_full, b + 1)
                a.copy(gate[:], psum[:, bank:bank + 2, :].rearrange("p a n -> p (a n)")).then_inc(gate_done, 1)

            def boundary(b):
                def root(n, i):
                    act.wait_ge(b_var, n + 1)
                    a.activation(std[:, i:i + 1], mv[:, i, 1:2], ACT.Sqrt, bias=eps[:, 0:1]).then_inc(b_std, 1)

                n = 2 * TT * b
                for step in range(TT + (4 if b < 3 else 1)):
                    if step < TT:
                        root(n, step)
                        n += 1
                    i = step - 1
                    if 0 <= i < TT:
                        act.wait_ge(b_stat, b_order(b).index(("first", i)) + 2 * TT * b + 1)
                        a.activation(y_acc[:, i], y_acc[:, i], ACT.Identity, scale=rstd[:, i:i + 1],
                                     bias=nmr[:, i:i + 1]).then_inc(b_norm, 1)
                    if b == 3:
                        continue
                    i = step - 3
                    if 0 <= i < TT:
                        root(n, i)
                        n += 1
                    i = step - 4
                    if 0 <= i < TT:
                        act.wait_ge(b_stat, b_order(b).index(("second", i)) + 2 * TT * b + 1)
                        a.activation(y_acc[:, i], x_nat[:, i], ACT.Identity, scale=rstd[:, i:i + 1],
                                     bias=nmr[:, i:i + 1]).then_inc(b_xhat, 1)
                if b == 3:
                    return
                sh, sc = MODS[b]
                act.wait_ge(b_cols, 1)
                for k in range(KD):
                    act.wait_ge(b_full, KD * b + k + 1)
                    if KD * b + k >= 2:
                        act.wait_ge(b_split, KD * b + k - 1)
                    a.activation(btile[:, k % 2], psum[:, k, :], ACT.Identity, scale=adac[:, sc + k:sc + k + 1],
                                 bias=adac[:, sh + k:sh + k + 1]).then_inc(b_tile, 1)
                take_gate(b + 1)

            act.wait_ge(tr_full, JH * H)
            boundary_loads(0)
            take_gate(0)
            take_ada(PAIRS - 1)
            boundary(0)

            def mlp(layer):
                act.wait_ge(b_x, (2 * layer + 1) * TT)
                boundary_loads(2 * layer + 1)
                with act.Fori(0, GROUPS) as gr:
                    for u in range(4):
                        for c2 in range(2):
                            n = gr * 4 + layer * 16 + u
                            act.wait_ge(a_full[c2], n + 1)
                            act.wait_ge(a_sq[c2], n)
                            a.activation(relu[:, c2], psum[:, c2, :], ACT.Relu).then_inc(a_relu[c2], 1)
                            act.wait_ge(a_split[c2], n)
                            act.wait_ge(a_relu[c2], n + 1)
                            a.activation(sq[:, c2], relu[:, c2], ACT.Square).then_inc(a_sq[c2], 1)
            mlp(0)
            boundary(1)
            for n in range(24):
                act.wait_ge(f_full[n % 2], n // 2 + 1)
                if n >= 2:
                    act.wait_ge(f_split[n % 2], n // 2)
                if n < 16:
                    a.copy(ftile[n % 2][:, 0:FG], psum[:, n % 2, 0:FG]).then_inc(f_tile[n % 2], 1)
                elif n % 2 == 0:
                    a.copy(ftile[0][:], psum[:, 0, :]).then_inc(f_tile[0], 1)
                else:
                    row = 32 * ((n - 16) // 2)
                    act.wait_ge(mid_full, 1)
                    a.copy(ftile[1][:], psum[:, 1, :])
                    act.drain()
                    a.copy(ftile[1][0:1, :], psum[row:row + 1, 3, :]).then_inc(f_tile[1], 1)
            boundary_loads(2)
            boundary(2)
            mlp(1)
            boundary(3)

        @block.vector
        def _(dve):
            v = nc.vector

            def split(dst_hi, dst_lo, src):
                v.tensor_copy(dst_hi, src)
                dve.drain()
                return v.tensor_tensor(dst_lo, src, dst_hi.bitcast(F32), ALU.subtract)

            def finish_stats(i0, i1):
                dve.drain()
                for i in range(i0, i1):
                    v.bn_aggr(mv[:, i], stat[:, i].rearrange("p a b -> p (a b)"))
                dve.drain()
                return v.tensor_scalar(std[:, i0:i1], mv[:, i0:i1, 1], EPS, None, ALU.add)

            def rstd_nmr(i0, i1):
                v.reciprocal(rstd[:, i0:i1], std[:, i0:i1])
                dve.drain()
                return v.scalar_tensor_tensor(out=nmr[:, i0:i1], in0=mv[:, i0:i1, 0], scalar=-1.0,
                                              in1=rstd[:, i0:i1], op0=ALU.mult, op1=ALU.mult)

            for m, (src, i0, i1) in enumerate(((x_in, 0, TT), (c_in, TT, ST))):
                dve.wait_ge(in_landed[1 + m], 16)
                for i in range(i0, i1):
                    for half in range(2):
                        v.bn_stats(stat[:, i, half], src[:, i - i0, tblk(half, 512)])
                finish_stats(i0, i1).then_inc(var_done, 1)
                dve.wait_ge(std_done, m + 1)
                rstd_nmr(i0, i1)
                dve.drain()
                for i in range(i0, i1):
                    v.tensor_scalar(src[:, i - i0], src[:, i - i0], rstd[:, i:i + 1], nmr[:, i:i + 1],
                                    ALU.mult, ALU.add)
            dve.drain().then_inc(xhat_done, 1)
            dve.wait_ge(col_T, 1)
            v.tensor_copy(cols[:], psum[:, 7, 0:288]).then_inc(cols_done, 1)
            dve.wait_ge(cols_done, 1)
            dve.wait_ge(mod_T, 1)
            for row in range(2):
                v.tensor_tensor(mod0[:, :, row], psum[:, 6, row:32:2], cols[:, 192:208], ALU.add)
            dve.drain()
            v.tensor_scalar(mod0[:, KD:2 * KD], mod0[:, KD:2 * KD], 1.0, None, ALU.add).then_inc(mod_done, 1)
            for k in range(KD):
                r = k % 3
                dve.wait_ge(x0_tile[r], k // 3 + 1)
                v.tensor_copy(ht_hi[:, k], tile[:, r]).then_inc(x0_high, 1)
                if k % 2 == 0:
                    dve.drain()
                    v.tensor_tensor(ht_lo[:, k], tile[:, r], ht_hi[:, k].bitcast(F32), ALU.subtract
                                    ).then_inc(x0_split[r], 1)
                    dve.drain().then_inc(ht_ready[0], 1)

            def staged(what, h):
                n = USE[what]
                dve.wait_ge(evac[n % SLOTS], h * USES + n // SLOTS + 1)
                return n % SLOTS

            def conv(j, h):
                def tap(kl):
                    return cols[:, bass.ds(h * JH + kl * 16 + j, 1)]

                dve.drain()
                dve.wait_ge(sx_done, h * JH + (j - 1 if j >= 2 else 0))
                acc_ = xc[:, j % 2]
                src = xm[:, j]
                v.tensor_scalar(acc_, src, tap(4), cols[:, bass.ds(h * JH + 144 + j, 1)], ALU.mult, ALU.add)
                dve.drain()
                a_c, s_c = acc_[:, 0:NC], src[:, 0:NC]
                a_l = acc_[:, NC:NT].rearrange("p (r c) -> p r c", c=GRID)
                s_l = src[:, NC:NT].rearrange("p (r c) -> p r c", c=GRID)

                def add(dst, source, kl):
                    return v.scalar_tensor_tensor(out=dst, in0=source, scalar=tap(kl), in1=dst,
                                                  op0=ALU.mult, op1=ALU.add)

                add(a_c[:, 1:NC], s_c[:, 0:NC - 1], 3)
                for k in range(3):
                    for l in range(3):
                        if (k, l) == (1, 1):
                            continue
                        dr, dc = k - 1, l - 1
                        r0, r1 = max(0, -dr), ROWS - max(0, dr)
                        c0, c1 = max(0, -dc), GRID - max(0, dc)
                        add(a_l[:, r0:r1, c0:c1], s_l[:, r0 + dr:r1 + dr, c0 + dc:c1 + dc], 3 * k + l)
                        dve.drain()
                        if (k, l) == (0, 1):
                            add(a_c[:, 0:NC - 1], s_c[:, 1:NC], 5)
                dve.drain().then_inc(conv_done, 1)

            def low(dst, src, high):
                return v.tensor_tensor(dst, src, high.bitcast(F32), ALU.subtract)

            def split_v(j, h):
                r = staged(("vN", j), h)
                dve.wait_ge(v_spilled, (h * JH + j) * 32)
                split(v_st_hi[:].rearrange("p s e -> p (s e)"), v_st_lo[:].rearrange("p s e -> p (s e)"),
                      tile[:, r]).then_inc(taken[r], 1)
                dve.drain().then_inc(v_split, 1)

            def split_xm(j, h):
                staged(("xm", j), h)
                low(xx_lo[:, j], xm[:, j], xx_hi[:, j]).then_inc(x_split, 1)

            def split_x(j, h):
                dve.wait_ge(xc_high, h * JH + j + 1)
                low(xx_lo[:, j], xc[:, j % 2], xx_hi[:, j]).then_inc(x_split, 1)

            with dve.Fori(0, H // 2) as it:
                for hh in range(2):
                    h = it * 2 + hh
                    split_xm(0, h)
                    split_xm(1, h)
                    conv(0, h)
                    split_xm(2, h)
                    split_xm(3, h)
                    conv(1, h)
                    split_v(0, h)
                    split_v(1, h)
                    split_x(0, h)
                    conv(2, h)
                    split_v(2, h)
                    split_x(1, h)
                    conv(3, h)
                    split_x(2, h)
                    split_x(3, h)
                    split_v(3, h)
                    for j in range(JH):
                        r = staged(("q", j), h)
                        low(q_lo[:, j], tile[:, r, NC:NT], q_hi[:, j]).then_inc(taken[r], 1)
                        dve.drain().then_inc(qk_split, 1)
                    for j in range(JH):
                        r = staged(("k", j), h)
                        low(k_lo[:, j], tile[:, r], k_hi[:, j]).then_inc(taken[r], 1)
                        dve.drain().then_inc(qk_split, 1)

            dve.wait_ge(gate_rows, 64)
            v.scalar_tensor_tensor(out=g_a[:], in0=g_f[:], scalar=-1.0, in1=g_f[:], op0=ALU.mult,
                                   op1=ALU.max).then_inc(abs_f, 1)
            v.memset(g_z[:], 0.0)
            dve.wait_ge(soft, 2)
            v.scalar_tensor_tensor(out=g_f[:], in0=g_f[:], scalar=0.0, in1=g_t[:], op0=ALU.min,
                                   op1=ALU.subtract)
            dve.drain()

            def scan(dst, src, other, op1):
                v.tensor_tensor_scan(dst[:, 0], src[:, 0], other(0, slice(0, NT)), 0.0, op1, op1)
                back_c, back_l = slice(NC - 1, None, -1), slice(NT - 1, NC - 1, -1)
                v.tensor_tensor_scan(dst[:, 1, back_c], src[:, 1, back_c], other(1, back_c), 0.0,
                                     op1, op1)
                dve.drain()
                v.tensor_tensor_scan(dst[:, 1, back_l], src[:, 1, back_l], other(1, back_l), dst[:, 1, 0:1],
                                     op1, op1)
                dve.drain()

            scan(g_F, g_f, lambda d, s: g_z[:, s], ALU.add)
            v.tensor_tensor(g_g[:], g_i[:], g_F[:], ALU.subtract)
            dve.drain().then_inc(g_done, 1)
            scan(g_M, g_g, lambda d, s: g_g[:, d, s], ALU.max)
            v.tensor_tensor(g_F[:], g_F[:], g_M[:], ALU.add).then_inc(scans, 1)
            dve.wait_ge(gT_full, 1)
            v.tensor_copy(gcol[:].rearrange("p d s h -> p (d s h)"), psum[:, 0, 0:2 * ST * H]
                          ).then_inc(m_done, 1)

            def diagonal(h, jj):
                n = ST * h + 2 + jj
                dve.wait_ge(mb_done, 2 * h + 2)
                if n >= 3:
                    dve.wait_ge(p_ready, n - 2)
                for d in range(2):
                    v.scalar_tensor_tensor(out=wt[n % 3][:, jj + d], in0=mb[:, d, tblk(jj)],
                                           scalar=gcol[:, d, 2 + jj, h:h + 1], in1=mask[:, d],
                                           op0=ALU.subtract, op1=ALU.max)
                dve.drain().then_inc(diag_in, 1)

            def products(h, s):
                n = ST * h + s
                w = wt[n % 3][:].rearrange("p b t -> p (b t)")
                dve.wait_ge(w_exp, n + 1)
                if s == 0:
                    dve.wait_ge(s_landed, 16 * (h + 1))
                for d in range(2):
                    t0 = 0 if s < 2 or d == BACK else (s - 2) * P
                    t1 = NL if s < 2 or d == FORTH else (s - 1) * P
                    w0 = P * pblock(d, s, 0)
                    v.tensor_tensor(w[:, w0 + t0:w0 + t1], w[:, w0 + t0:w0 + t1], s_in[:, s, t0:t1], ALU.mult)

            def products_hi(h, s):
                n = ST * h + s
                dve.drain()
                if h and s == 0:
                    dve.wait_ge(pv_full[BACK], TT * h)
                v.tensor_copy(p_hi[:, START[s]:START[s] + BLOCKS[s]], wt[n % 3][:, 0:BLOCKS[s]]
                              ).then_inc(p_hi_done, 1)

            def add_y(i, half, first):
                src = psum[:, 4 + i, :]
                dst = y_acc[:, i, tblk(half, 512)]
                if first:
                    v.tensor_copy(dst, src).then_inc(y_free[i], 1)
                else:
                    v.tensor_tensor(dst, dst, src, ALU.add).then_inc(y_free[i], 1)

            def take_y(h, n):
                half, i = n // TT, n % TT
                dve.wait_ge(y_full[i], 2 * h + half + 1)
                add_y(i, half, h == 0)

            def read_out(h, e):
                n = h * JH + e
                bank = 2 if h < H - 1 else LAST_TURN[e]
                r = n % 3
                dve.wait_ge(tr_full, n + 1)
                dve.wait_ge(z_landed[r], 32 * (n // 3 + 1))
                if e == 0 and 0 < h < H - 1:
                    dve.wait_ge(y_full[TT - 1], 2 * h)
                v.scalar_tensor_tensor(out=sxt[:, r], in0=psum[:, bank, :], scalar=cols[:, 160 + n:161 + n],
                                       in1=sxt[:, r], op0=ALU.mult, op1=ALU.add).then_inc(tr_free, 1)
                dve.drain()
                v.tensor_tensor(zt[:, r], zt[:, r], sxt[:, r], ALU.mult)
                dve.drain()
                hi, lo = u_of(h)
                split(hi[:, e], lo[:, e], zt[:, r]).then_inc(zu_done, 1)
                if e == JH - 1:
                    dve.drain().then_inc(u_done, 1)

            def head_denominators(h):
                for d in range(2):
                    dve.wait_ge(bc_full, bc_use("den", h, d))
                    for i in range(TT):
                        v.tensor_tensor_reduce(out=psum[:, 3, tblk(i)], in0=psum[:, 3, tblk(i)],
                                               in1=ident[:], scale=1.0, scalar=0.0, op0=ALU.mult, op1=ALU.add,
                                               accum_out=dena[:, d, i:i + 1])
                        dve.drain()
                    dve.drain().then_inc(bc_free, 1)
                v.scalar_tensor_tensor(out=den[:], in0=dena[:], scalar=-1.0, in1=exp_m[:, :, :, h],
                                       op0=ALU.mult, op1=ALU.max)
                dve.drain()
                v.tensor_tensor(den[:], den[:], dena[:], ALU.max)
                dve.drain()
                v.reciprocal(den[:], den[:])
                dve.drain().then_inc(den_done, 1)

            dve.wait_ge(exp_m_done, 1)
            dve.wait_ge(sel_ready, 1)
            diagonal(0, 0)
            for s in range(ST):
                products(0, s)
                products_hi(0, s)
                if 1 <= s < TT:
                    diagonal(0, s)
            for h in range(H):
                head_denominators(h)
                for i in range(TT):
                    if h:
                        read_out(h - 1, i)
                    if i == TT - 1 and h + 1 < H:
                        products(h + 1, 0)
                        products(h + 1, 1)
                    dve.wait_ge(forth_done, TT * h + i + 1)
                    dve.wait_ge(pv_full[BACK], TT * h + i + 1)
                    hh = hn[:, h % 2, i]
                    v.scalar_tensor_tensor(out=hh, in0=psum[:, BACK, :], scalar=den[:, BACK, i:i + 1], in1=hh,
                                           op0=ALU.mult, op1=ALU.add).then_inc(back_done, 1)
                    dve.drain()
                    v.bn_stats(stat[:, i, 0], hh)
                dve.drain()
                for i in range(TT):
                    v.bn_aggr(mv[:, i], stat[:, i, 0])
                dve.drain()
                v.tensor_scalar(std[:, 0:TT], mv[:, 0:TT, 1], EPS, None, ALU.add).then_inc(h_var, 1)
                if h + 1 < H:
                    diagonal(h + 1, 0)
                dve.wait_ge(h_std, h + 1)
                rstd_nmr(0, TT)
                dve.drain().then_inc(h_rs, 1)
                for n in range(2 * TT):
                    if h + 1 < H and n < ST:
                        if n >= 2:
                            products(h + 1, n)
                        products_hi(h + 1, n)
                        if 1 <= n < TT:
                            diagonal(h + 1, n)
                    if h and h < H - 1:
                        take_y(h - 1, n)

            def add_bias(c0, c1):
                v.tensor_tensor(adac[:, c0:c1], adac[:, c0:c1], cols[:, 192 + c0:192 + c1], ALU.add)

            def gate_diagonals(b):
                if b:
                    dve.wait_ge(gate_full, b)
                for k in range(KD):
                    c0 = GATE[b] + k
                    v.tensor_scalar(gate_diag[:, k], ident[:], adac[:, c0:c0 + 1], None, ALU.mult)
                dve.drain().then_inc(gate_in, 1)



            def before_last(b, half):
                cs = tblk(half, 512)
                dve.wait_ge(gate_done, b + 1)
                dve.drain()
                if (b, half) == (0, 1):
                    dve.wait_ge(half_gated, 1)
                else:
                    for i in range(TT):
                        v.tensor_tensor(y_acc[:, i, cs], y_acc[:, i, cs], gate[:, cs], ALU.mult)
                old = x_res if b == 0 else x_nat
                if b == 0:
                    dve.wait_ge(res_landed, 16)
                dve.drain()
                for i in range(TT):
                    v.scalar_tensor_tensor(out=y_acc[:, i, cs], in0=old[:, i, cs], scalar=ALPHA,
                                           in1=y_acc[:, i, cs], op0=ALU.mult, op1=ALU.add)
                dve.drain()

            def next_gate(b):
                if b == 0:
                    dve.wait_ge(bc_free, bc_use("ada", PAIRS - 1))
                    add_bias(vec(0, G2), vec(1, SH1))
                    dve.drain()
                if b < 3:
                    gate_diagonals(b + 1)

            def last_share(b, uses, half, i):
                dve.wait_ge(y_full[i], uses + half + 1)
                t = rtmp[:, i % 2]
                dst = y_acc[:, i, tblk(half, 512)]
                if b == 2 and i == half == 0:
                    dve.wait_ge(gate_done, b + 1)
                v.tensor_tensor(t, psum[:, 4 + i, :], gate[:, tblk(half, 512)], ALU.mult).then_inc(y_free[i], 1)
                dve.drain()
                if b == 2:
                    v.scalar_tensor_tensor(out=dst, in0=x_nat[:, i, tblk(half, 512)], scalar=ALPHA, in1=t,
                                           op0=ALU.mult, op1=ALU.add)
                else:
                    v.tensor_tensor(dst, dst, t, ALU.add)
                dve.drain()
                v.bn_stats(stat[:, i, half], dst)

            def variance(i):
                dve.drain()
                v.bn_aggr(mv[:, i], stat[:, i].rearrange("p a b -> p (a b)")).then_inc(b_var, 1)

            def normalisation(n, i):
                dve.wait_ge(b_std, n + 1)
                v.reciprocal(rstd[:, i:i + 1], std[:, i:i + 1])
                dve.drain()
                v.scalar_tensor_tensor(out=nmr[:, i:i + 1], in0=mv[:, i, 0:1], scalar=-1.0,
                                       in1=rstd[:, i:i + 1], op0=ALU.mult, op1=ALU.mult)
                dve.drain().then_inc(b_stat, 1)

            def boundary(b, uses):
                if b == 0:
                    dve.drain().then_inc(heads_summed, 1)
                    before_last(0, 0)
                for i in range(TT):
                    last_share(b, uses, 0, i)
                if b == 0:
                    before_last(0, 1)
                if b in (1, 3):
                    next_gate(b)
                roots = root_order(b)
                for step in range(TT + (4 if b < 3 else 2)):
                    if step < TT:
                        last_share(b, uses, 1, step)
                        variance(step)
                    i = step - 1
                    if 0 <= i < TT:
                        normalisation(2 * TT * b + roots.index(("first", i)), i)
                    i = step - 2
                    if 0 <= i < TT:
                        dve.wait_ge(b_norm, TT * b + i + 1)
                        if i == 0:
                            dve.wait_ge(pgb_landed, 32 * (b + 1))
                        if i >= POOL_TILES:
                            v.tensor_tensor(y_acc[:, i], y_acc[:, i], pg[:], ALU.mult).then_inc(b_g, 1)
                    if b == 3:
                        continue
                    i = step - 3
                    if 0 <= i < TT:
                        dve.wait_ge(b_x, TT * b + i + 1)
                        for half in range(2):
                            v.bn_stats(stat[:, i, half], x_nat[:, i, tblk(half, 512)])
                        variance(i)
                    i = step - 4
                    if 0 <= i < TT:
                        normalisation(2 * TT * b + roots.index(("second", i)), i)
                if b == 0:
                    next_gate(0)
                if b == 3:
                    return
                for k in range(KD):
                    dve.wait_ge(b_tile, KD * b + k + 1)
                    split(hh_hi[:, k], hh_lo[:, k], btile[:, k % 2]).then_inc(b_split, 1)
                if b != 1:
                    dve.wait_ge(y_zero, 1 + b // 2)

            def mlp(layer, y0):
                def split_group(gr):
                    for u in range(4):
                        for c2 in range(2):
                            dve.wait_ge(a_sq[c2], gr * 4 + layer * 16 + u + 1)
                            split(ff_hi[:, 2 * u + c2], ff_lo[:, 2 * u + c2], sq[:, c2]
                                  ).then_inc(a_split[c2], 1)

                with dve.Fori(0, GROUPS - 1) as gr:
                    split_group(gr)
                    for half in range(2):
                        for i in range(TT):
                            dve.wait_ge(y_full[i], gr * 2 + y0 + half + 1)
                            add_y(i, half, False)
                split_group(GROUPS - 1)
                for half in range(2):
                    before_last(2 * layer + 1, half)

            for n in range(TT):
                take_y(H - 2, n)
            dve.wait_ge(bc_free, bc_use("ada", PAIRS - 2))
            add_bias(vec(0, G1), vec(0, G2))
            add_bias(vec(1, SH1), 12 * KD)
            dve.drain()
            for _, sc in MODS:
                v.tensor_scalar(adac[:, sc:sc + KD], adac[:, sc:sc + KD], 1.0, None, ALU.add)
            dve.drain().then_inc(b_cols, 1)
            dve.wait_ge(p_ready, ST * H)
            gate_diagonals(0)
            for e in range(JH):
                read_out(H - 1, e)
                take_y(H - 2, TT + e)
            boundary(0, 2 * H - 2)
            mlp(0, Y_MLP0)
            boundary(1, Y_MLP0 + 2 * GROUPS - 2)
            for n in range(16):
                dve.wait_ge(f_tile[n % 2], n // 2 + 1)
                split(a_hi[:, n % 4, n // 4], a_lo[:, n % 4, n // 4], ftile[n % 2][:, 0:FG]
                      ).then_inc(f_split[n % 2], 1)

            dve.drain()
            for part, mid in ((a_hi, mid_hi), (a_lo, mid_lo)):
                v.tensor_copy(mid[:].rearrange("p i (g c) -> p (i g) c", c=32),
                              part[:].rearrange("p i g f -> p (i g) f")[:, :, P:P + 32])
            dve.drain().then_inc(mid_in, 1)

            def fold(u):
                n = RAW0_F + 3 + u
                dve.wait_ge(raw_landed[n % 2], 16 * (n // 2 + 1))
                if u >= 2:
                    dve.wait_ge(w_ready, SPLIT0_F + 3 + u - 1)
                src = raw[:, n % 2].rearrange("p (g a n) -> p g a n", g=2, a=2)
                dst = folded[:, u % 2].rearrange("p (g a n) -> p g a n", g=2, a=2)
                v.scalar_tensor_tensor(out=dst[:, :, 0], in0=src[:, :, 1], scalar=pair_row[:, 0:1],
                                       in1=src[:, :, 0], op0=ALU.mult, op1=ALU.add)
                v.scalar_tensor_tensor(out=dst[:, :, 1], in0=src[:, :, 0], scalar=pair_row[:, 1:2],
                                       in1=src[:, :, 1], op0=ALU.mult, op1=ALU.add)
                dve.drain().then_inc(fold_done, 1)

            v.tensor_scalar(pair_row[:, 0:1], ident[:, 0:1], -1.0, 1.0, ALU.mult, ALU.add)
            v.tensor_scalar(pair_row[:, 1:2], ident[:, 0:1], 1.0, None, ALU.subtract)
            dve.drain()
            fold(0)
            for n in range(16, 24):
                dve.wait_ge(f_tile[n % 2], n // 2 + 1)
                split(hh_hi[:, n - 16], hh_lo[:, n - 16], ftile[n % 2][:]).then_inc(f_split[n % 2], 1)
                if n == 19:
                    fold(1)
            fold(2)
            fold(3)
            gate_diagonals(3)
            boundary(2, Y_F)
            mlp(1, Y_MLP1)
            boundary(3, Y_MLP1 + 2 * GROUPS - 2)


def dft_tables():
    ch = np.outer(np.arange(FG), np.arange(FG)) % FG * (2 * np.pi / FG)
    chan = np.concatenate([np.cos(ch)[:, 0:P + 1], np.sin(ch)[:, 1:P]], axis=1)
    sq = np.outer(np.arange(NL), np.arange(NL)) % NL * (2 * np.pi / NL)
    scale = 1.0 / np.sqrt(NL * FG)
    units = np.zeros((3, P, UNIT))
    units[0, :, 0:2 * FG] = chan.reshape(2, P, FG).transpose(1, 0, 2).reshape(P, 2 * FG)
    for n, t in ((1, np.cos(sq) * scale), (2, np.sin(sq) * scale)):
        units[n] = t.reshape(4, P, 512).transpose(1, 0, 2).reshape(P, UNIT)
    return units.astype(np.float32)


_INS = ["x", "c", "ctx", "c_ctx", "ada_w", "ada_b", "post_g", "post_b", "m_w_in", "m_w_conv", "m_b_conv",
        "m_w_q", "m_w_k", "m_w_v", "m_w_gate", "m_b_gate", "m_gn_w", "m_skip", "m_w_out", "f_w_out",
        "mlp_w1", "mlp_w2"]


def kernel(**inputs):
    import concourse.bacc as bacc
    from concourse.bass_utils import run_bass_kernel_spmd

    nc = bacc.Bacc("TRN2", target_bir_lowering=False, num_devices=1)
    arrays = {f"in_{name}": np.ascontiguousarray(inputs[name]) for name in _INS}
    order = [g * FG + k for g in range(D // FG) for k in [*range(P + 1), *range(FG - 1, P, -1)]]
    arrays["in_f_w_out"] = np.ascontiguousarray(inputs["f_w_out"][:, order])
    arrays["dft"] = dft_tables()
    args = [nc.dram_tensor(name, a.shape, mybir.dt.from_np(a.dtype), kind="ExternalInput").ap()
            for name, a in arrays.items()]
    out = nc.dram_tensor("out", (1, NL, D), F32, kind="ExternalOutput").ap()
    hybrid_block(nc, *args, out)
    r = run_bass_kernel_spmd(nc, [arrays], core_ids=[0])
    return r.results[0]["out"]
```
